# Optimizing a Trainium2 kernel written in Bass

```python
import jax, jax.numpy as jnp
from jax import lax
import numpy as np

D_MODEL = 1024
BATCH = 1
SEQ = 1024
DEPTH = 2
DEC_BATCH = 1
DEC_SEQ = 64
PAST_LEN = 2048

CHUNK = 64
N_EVEN = (DEPTH + 1) // 2
N_ODD = DEPTH // 2
PLE_DIM = 256
D_A = D_MODEL // 2
CONV_W = 3
H_F = 8
HD_F = 64
D_F = H_F * HD_F
D_MIX = D_A + D_F
IN_COLS = 3 * D_A + 3 * D_F + H_F
IN_SPLITS = (D_A, 2 * D_A, 3 * D_A, 3 * D_A + D_F, 3 * D_A + 2 * D_F, 3 * D_A + 3 * D_F)
QBLK = 128
HD_R = 64
H_R = D_MODEL // HD_R
LORA_W = 64
LORA_A = 64
LORA_G = 128
D_FF = -(-8 * D_MODEL // (3 * 256)) * 256
NORM_EPS = 1e-6
GN_EPS = 64e-5
L2_EPS = 1e-12
NEG_INF = -1e30
RWKV_NAMES = ('r_mu', 'r_w_r', 'r_w_k', 'r_w_v', 'r_w_o', 'r_w0', 'r_w1', 'r_w2', 'r_a0', 'r_a1', 'r_a2',
              'r_g1', 'r_g2', 'r_k_k', 'r_k_a', 'r_r_k', 'r_ln_w', 'r_ln_b')

kernel_name = 'hybrid_conv_fox_rwkv7_stream_step'

def rms_norm(x, g):
    x32 = x.astype(jnp.float32)
    y = x32 * lax.rsqrt(jnp.mean(x32 * x32, axis=-1, keepdims=True) + NORM_EPS)
    return (y * g.astype(jnp.float32)).astype(x.dtype)

def swiglu(x, w_gate, w_up, w_down):
    return (jax.nn.silu(x @ w_gate) * (x @ w_up)) @ w_down

def short_conv(u, prev, w):
    T = u.shape[1]
    ext = jnp.concatenate([prev.astype(u.dtype), u], axis=1)
    out = sum(ext[:, j:j + T] * w[j] for j in range(CONV_W))
    return out, ext[:, -(CONV_W - 1):]

def fox_prompt(q, k, v, logf):
    B, S = q.shape[:2]
    nb = S // QBLK
    scale = HD_F ** -0.5
    cum = jnp.cumsum(logf, axis=1).transpose(0, 2, 1)
    qb = q.reshape(B, nb, QBLK, H_F, HD_F).transpose(1, 0, 2, 3, 4)
    cq = cum.reshape(B, H_F, nb, QBLK).transpose(2, 0, 1, 3)
    qpos = jnp.arange(S, dtype=jnp.int32).reshape(nb, QBLK)
    kpos = jnp.arange(S, dtype=jnp.int32)

    def block(args):
        qi, ci, pi = args
        s = jnp.einsum('bqhd,bkhd->bhqk', qi, k).astype(jnp.float32) * scale
        s = s + ci[..., None] - cum[:, :, None, :]
        s = jnp.where(pi[:, None] >= kpos[None, :], s, NEG_INF)
        p = jax.nn.softmax(s, axis=-1).astype(v.dtype)
        return jnp.einsum('bhqk,bkhd->bqhd', p, v)

    o = lax.map(block, (qb, cq, qpos))
    return o.transpose(1, 0, 2, 3, 4).reshape(B, S, D_F)

def fox_sample(q, k, v, logf, ck, cv, clogf):
    B, T = q.shape[:2]
    P = ck.shape[1]
    scale = HD_F ** -0.5
    kall = jnp.concatenate([ck.astype(k.dtype), k], axis=1)
    vall = jnp.concatenate([cv.astype(v.dtype), v], axis=1)
    cum = jnp.cumsum(jnp.concatenate([clogf.astype(jnp.float32), logf], axis=1), axis=1).transpose(0, 2, 1)
    s = jnp.einsum('bqhd,bkhd->bhqk', q, kall).astype(jnp.float32) * scale
    s = s + cum[:, :, P:, None] - cum[:, :, None, :]
    qpos = P + jnp.arange(T, dtype=jnp.int32)
    kpos = jnp.arange(P + T, dtype=jnp.int32)
    s = jnp.where(qpos[:, None] >= kpos[None, :], s, NEG_INF)
    p = jax.nn.softmax(s, axis=-1).astype(vall.dtype)
    return jnp.einsum('bhqk,bkhd->bqhd', p, vall).reshape(B, T, D_F)

def conv_fox_mixer(x, conv_prev, fox_cache, w_in, b_f, conv_w, w_out):
    B, T = x.shape[:2]
    z = x @ w_in
    ax, a_b, a_c, q, k, v, fl = jnp.split(z, IN_SPLITS, axis=-1)
    u = a_c * ax
    cu, conv_state = short_conv(u, conv_prev, conv_w)
    y_a = a_b * cu
    logf = jax.nn.log_sigmoid(fl.astype(jnp.float32) + b_f.astype(jnp.float32))
    q = q.reshape(B, T, H_F, HD_F)
    k = k.reshape(B, T, H_F, HD_F)
    v = v.reshape(B, T, H_F, HD_F)
    if fox_cache is None:
        o = fox_prompt(q, k, v, logf)
    else:
        o = fox_sample(q, k, v, logf, *fox_cache)
    y = jnp.concatenate([y_a, o.astype(x.dtype)], axis=-1) @ w_out
    return y, k, v, logf, conv_state

def rwkv7_mixer(x, shift_prev, wkv_prev, mu, w_r, w_k, w_v, w_o, w0, w1, w2, a0, a1, a2,
                g1, g2, k_k, k_a, r_k, ln_w, ln_b):
    f32 = jnp.float32
    B, T, _ = x.shape
    x_prev = jnp.concatenate([shift_prev[:, None, :].astype(x.dtype), x[:, :-1]], axis=1)
    xx = x_prev - x
    xr, xw, xk, xv, xa, xg = (x + xx * mu[n] for n in range(6))
    r = xr @ w_r
    k = xk @ w_k
    v = xv @ w_v
    logw = -jax.nn.softplus(-(w0 + jnp.tanh(xw @ w1) @ w2).astype(f32)) - 0.5
    decay = jnp.exp(-jnp.exp(logw))
    a = jax.nn.sigmoid((a0 + (xa @ a1) @ a2).astype(f32))
    g = jax.nn.sigmoid(xg @ g1) @ g2
    heads = lambda t: t.astype(f32).reshape(B, T, H_R, HD_R)
    kk = heads(k * k_k)
    kk = kk / jnp.maximum(jnp.sqrt(jnp.sum(kk * kk, axis=-1, keepdims=True)), L2_EPS)
    k_mod = k.astype(f32) * (1.0 + (a - 1.0) * k_a.astype(f32))
    r_h, k_h, v_h, w_h, a_h = heads(r), heads(k_mod), heads(v), heads(decay), heads(a)
    b_h = kk * a_h

    def step(S, inp):
        r_t, w_t, k_t, v_t, kk_t, b_t = inp
        sa = jnp.einsum('bhvk,bhk->bhv', S, -kk_t)
        S = S * w_t[:, :, None, :] + sa[..., None] * b_t[:, :, None, :] + v_t[..., None] * k_t[:, :, None, :]
        return S, jnp.einsum('bhvk,bhk->bhv', S, r_t)

    xs = tuple(t.transpose(1, 0, 2, 3) for t in (r_h, w_h, k_h, v_h, kk, b_h))
    S_fin, o = lax.scan(step, wkv_prev.astype(f32), xs)
    o = o.transpose(1, 0, 2, 3)
    mean = jnp.mean(o, axis=-1, keepdims=True)
    var = jnp.mean(jnp.square(o - mean), axis=-1, keepdims=True)
    o = ((o - mean) * lax.rsqrt(var + GN_EPS)).reshape(B, T, D_MODEL)
    o = o * ln_w.astype(f32) + ln_b.astype(f32)
    o = o + (jnp.sum(r_h * k_h * r_k.astype(f32), axis=-1, keepdims=True) * v_h).reshape(B, T, D_MODEL)
    y = (o.astype(x.dtype) * g) @ w_o
    return y, x[:, -1], S_fin

def trunk(x, p, fox_cache, conv_prev, shift_prev, wkv_prev, W):
    h = x
    ks, vs, lfs, convs, shifts, wkvs = [], [], [], [], [], []
    for i in range(DEPTH):
        j = i // 2
        hn = rms_norm(h, W['mix_norm_pre'][i])
        if i % 2 == 0:
            cache_j = None if fox_cache is None else tuple(c[j] for c in fox_cache)
            y, k, v, lf, cst = conv_fox_mixer(hn, conv_prev[j], cache_j, W['e_w_in'][j], W['e_b_f'][j],
                                              W['e_conv_w'][j], W['e_w_out'][j])
            ks.append(k)
            vs.append(v)
            lfs.append(lf)
            convs.append(cst)
        else:
            y, sh, st = rwkv7_mixer(hn, shift_prev[j], wkv_prev[j], *[W[n][j] for n in RWKV_NAMES])
            shifts.append(sh)
            wkvs.append(st)
        h = h + rms_norm(y, W['mix_norm_post'][i])
        f = swiglu(rms_norm(h, W['ffn_norm_pre'][i]), W['f_w_gate'][i], W['f_w_up'][i], W['f_w_down'][i])
        h = h + rms_norm(f, W['ffn_norm_post'][i])
        gate = jax.nn.sigmoid(rms_norm(h, W['ple_norm'][i]) @ W['ple_gate'][i])
        h = h + gate * (p[i].astype(h.dtype) @ W['ple_proj'][i])
    return (h, jnp.stack(ks), jnp.stack(vs), jnp.stack(lfs), jnp.stack(convs), jnp.stack(shifts), jnp.stack(wkvs))

def setup_inputs(seed: int = 0) -> dict:
    key = jax.random.key(seed)
    ks = iter(jax.random.split(key, 64))
    nrm = lambda shape, s=1.0: jax.random.normal(next(ks), shape, jnp.float32) * s
    gain = lambda shape: 1.0 + nrm(shape, 0.05)
    D = D_MODEL
    return {
        'x_prompt': nrm((BATCH, SEQ, D)),
        'x_sample': nrm((DEC_BATCH, DEC_SEQ, D)),
        'p_prompt': nrm((DEPTH, BATCH, SEQ, PLE_DIM)),
        'p_sample': nrm((DEPTH, DEC_BATCH, DEC_SEQ, PLE_DIM)),
        'cache_k': nrm((N_EVEN, DEC_BATCH, PAST_LEN, H_F, HD_F)),
        'cache_v': nrm((N_EVEN, DEC_BATCH, PAST_LEN, H_F, HD_F)),
        'cache_logf': jax.nn.log_sigmoid(4.0 + nrm((N_EVEN, DEC_BATCH, PAST_LEN, H_F))),
        'state_conv': nrm((N_EVEN, DEC_BATCH, CONV_W - 1, D_A)),
        'state_shift': nrm((N_ODD, DEC_BATCH, D)),
        'state_wkv': nrm((N_ODD, DEC_BATCH, H_R, HD_R, HD_R), 0.5),
        'mix_norm_pre': gain((DEPTH, D)),
        'mix_norm_post': gain((DEPTH, D)),
        'ffn_norm_pre': gain((DEPTH, D)),
        'ffn_norm_post': gain((DEPTH, D)),
        'e_w_in': nrm((N_EVEN, D, IN_COLS), D ** -0.5),
        'e_b_f': 4.0 + nrm((N_EVEN, H_F), 0.1),
        'e_conv_w': nrm((N_EVEN, CONV_W, D_A), CONV_W ** -0.5),
        'e_w_out': nrm((N_EVEN, D_MIX, D), D_MIX ** -0.5),
        'r_mu': jax.random.uniform(next(ks), (N_ODD, 6, D), jnp.float32),
        'r_w_r': nrm((N_ODD, D, D), D ** -0.5),
        'r_w_k': nrm((N_ODD, D, D), D ** -0.5),
        'r_w_v': nrm((N_ODD, D, D), D ** -0.5),
        'r_w_o': nrm((N_ODD, D, D), D ** -0.5),
        'r_w0': 0.5 + nrm((N_ODD, D), 0.5),
        'r_w1': nrm((N_ODD, D, LORA_W), D ** -0.5),
        'r_w2': nrm((N_ODD, LORA_W, D), 0.1 * LORA_W ** -0.5),
        'r_a0': nrm((N_ODD, D), 0.1),
        'r_a1': nrm((N_ODD, D, LORA_A), D ** -0.5),
        'r_a2': nrm((N_ODD, LORA_A, D), 0.1 * LORA_A ** -0.5),
        'r_g1': nrm((N_ODD, D, LORA_G), D ** -0.5),
        'r_g2': nrm((N_ODD, LORA_G, D), LORA_G ** -0.5),
        'r_k_k': 0.85 + nrm((N_ODD, D), 0.05),
        'r_k_a': 1.0 + nrm((N_ODD, D), 0.05),
        'r_r_k': nrm((N_ODD, H_R, HD_R), 0.1),
        'r_ln_w': gain((N_ODD, D)),
        'r_ln_b': nrm((N_ODD, D), 0.02),
        'f_w_gate': nrm((DEPTH, D, D_FF), D ** -0.5),
        'f_w_up': nrm((DEPTH, D, D_FF), D ** -0.5),
        'f_w_down': nrm((DEPTH, D_FF, D), D_FF ** -0.5),
        'ple_norm': gain((DEPTH, D)),
        'ple_gate': nrm((DEPTH, D, D), D ** -0.5),
        'ple_proj': nrm((DEPTH, PLE_DIM, D), PLE_DIM ** -0.5),
    }

def reference(x_prompt, x_sample, p_prompt, p_sample, cache_k, cache_v, cache_logf, state_conv, state_shift,
              state_wkv, mix_norm_pre, mix_norm_post, ffn_norm_pre, ffn_norm_post, e_w_in, e_b_f, e_conv_w,
              e_w_out, r_mu, r_w_r, r_w_k, r_w_v, r_w_o, r_w0, r_w1, r_w2, r_a0, r_a1, r_a2, r_g1, r_g2,
              r_k_k, r_k_a, r_r_k, r_ln_w, r_ln_b, f_w_gate, f_w_up, f_w_down, ple_norm, ple_gate, ple_proj):
    W = dict(mix_norm_pre=mix_norm_pre, mix_norm_post=mix_norm_post, ffn_norm_pre=ffn_norm_pre,
             ffn_norm_post=ffn_norm_post, e_w_in=e_w_in, e_b_f=e_b_f, e_conv_w=e_conv_w, e_w_out=e_w_out,
             r_mu=r_mu, r_w_r=r_w_r, r_w_k=r_w_k, r_w_v=r_w_v, r_w_o=r_w_o, r_w0=r_w0, r_w1=r_w1, r_w2=r_w2,
             r_a0=r_a0, r_a1=r_a1, r_a2=r_a2, r_g1=r_g1, r_g2=r_g2, r_k_k=r_k_k, r_k_a=r_k_a, r_r_k=r_r_k,
             r_ln_w=r_ln_w, r_ln_b=r_ln_b, f_w_gate=f_w_gate, f_w_up=f_w_up, f_w_down=f_w_down,
             ple_norm=ple_norm, ple_gate=ple_gate, ple_proj=ple_proj)
    bp = x_prompt.shape[0]
    zero_conv = jnp.zeros((N_EVEN, bp, CONV_W - 1, D_A), x_prompt.dtype)
    zero_shift = jnp.zeros((N_ODD, bp, D_MODEL), x_prompt.dtype)
    zero_wkv = jnp.zeros((N_ODD, bp, H_R, HD_R, HD_R), jnp.float32)
    y_p, k_p, v_p, lf_p, c_p, sh_p, s_p = trunk(x_prompt, p_prompt, None, zero_conv, zero_shift, zero_wkv, W)
    y_s, k_s, v_s, lf_s, c_s, sh_s, s_s = trunk(x_sample, p_sample, (cache_k, cache_v, cache_logf),
                                                state_conv, state_shift, state_wkv, W)
    return (y_p, y_s, k_p, v_p, lf_p, c_p, sh_p, s_p, k_s, v_s, lf_s, c_s, sh_s, s_s)


_drawn_inputs = setup_inputs


def setup_inputs(seed=0):
    import zlib

    import numpy as np

    out = dict(_drawn_inputs(seed))
    spreads = {}
    factors = {'cache_logf': 5.358,
     'r_w1': 6.487,
     'r_w2': 6.43,
     'r_k_k': 5.295,
     'r_ln_b': 5.738,
     'ple_norm': 5.922}
    for name, (base, spread) in spreads.items():
        noise = np.random.default_rng([zlib.crc32(name.encode()), seed]).standard_normal(out[name].shape)
        drawn = base * np.exp(spread * noise) if base else spread * noise
        out[name] = __import__('jax').numpy.asarray(drawn.astype(out[name].dtype))
    for name, factor in factors.items():
        out[name] = (out[name] * factor).astype(out[name].dtype)
    return out
```

```python
from contextlib import ExitStack, contextmanager

import numpy as np

import concourse.bass as bass
from concourse import mybir

F32 = mybir.dt.float32
BF16 = mybir.dt.bfloat16
U8 = mybir.dt.uint8
ALU = mybir.AluOpType
ACT = mybir.ActivationFunctionType
AX_X = mybir.AxisListType.X

P = 128
D = 1024
KT = D // P
SEQ, DEC, PAST = 1024, 64, 2048
PAD = 2
P0 = PAD
S0 = PAD + SEQ + PAD
T = S0 + DEC
NCH = 3
CH = T // NCH
assert NCH * CH == T and CH <= 512
DA = 512
NA = DA // P
HF = 8
DFF = 2816
NF = DFF // P
HALF = NF // 2
PLE = 256
NP_ = PLE // P
HR = 16
NPAIR = HR // 2
C = 64
NCHUNK = SEQ // C
NALL = PAST + DEC
NORM_EPS, GN_EPS, L2_EPS = 1e-6, 64e-5, 1e-12
NEG = -1e30
DECAY = float(np.exp(-0.5))
SLOTS = 4
SLOT = HALF * P

VEC = ["pre0", "pre1", "post0", "post1", "fpre0", "fpre1", "fpost0", "fpost1", "ple0", "ple1",
       "mu0", "mu1", "mu2", "mu3", "mu4", "mu5", "w0", "a0", "kk", "ka", "rk", "lnw", "lnb", "shift"]
V = {n: i for i, n in enumerate(VEC)}
NV = len(VEC)
CST = {"ident": (0, P), "ones": (P, P), "pair": (2 * P, P), "causal": (3 * P, P), "causal2": (4 * P, C),
       "gram_even": (4 * P + C, P), "gram_odd": (5 * P + C, P), "level0": (6 * P + C, P)}
NCST = 7 * P + C
LEVELS = (2, 4, 8, 16, 32)


class Tally:

    def __init__(self, engine):
        self.engine, self.n, self.per, self.i = engine, {}, {}, None

    def val(self, name, off=0):
        base = self.n.get(name, 0) + off
        if self.per.get(name):
            return self.i * self.per[name] + base
        return base

    def some(self, name, off=0):
        return bool(self.per.get(name)) or self.n.get(name, 0) + off > 0

    def up(self, name, k=1):
        self.n[name] = self.n.get(name, 0) + k
        return self.val(name)

    @contextmanager
    def loop(self, times, **per):
        before = dict(self.n)
        with self.engine.Fori(0, times) as i:
            self.i, self.per = i, per
            yield i
        for name in self.n.keys() | per.keys():
            moved = self.n.get(name, 0) - before.get(name, 0)
            assert moved == per.get(name, 0), (self.engine, name, moved, per.get(name, 0))
            self.n[name] = self.n.get(name, 0) + moved * (times - 1)
        self.i, self.per = None, {}

    def unit(self):
        s = self.n.get("mm_done", 0) % 2
        return s, self.up("mm_done"), self.up(f"read{s}")

    def skip(self, units):
        for _ in range(units):
            self.unit()


def build_trunk(nc, I, O, stop=99):
    ctx = ExitStack()
    with ctx:
        def sb(name, shape, dt=F32):
            return ctx.enter_context(nc.sbuf_tensor(name, shape, dt))

        def sem(name):
            return ctx.enter_context(nc.semaphore(name))

        def scratch(name, shape):
            return nc.dram_tensor(name, shape, F32, kind="Internal").ap()

        H = sb("H", [P, KT, T])
        A = sb("A", [P, KT, T])
        B = sb("B", [P, NF, T])
        W = sb("W", [P, SLOTS, SLOT])
        TM = sb("TM", [P, 4, T])
        cst = sb("cst", [P, NCST])
        vec = sb("vec", [P, NV, KT])
        convw = sb("convw", [P, 3, NA])
        convs = sb("convs", [P, NA, 2])
        bf = sb("bf", [HF, 1])
        mub = sb("mub", [P, 6, KT])
        kab = sb("kab", [P, KT])
        eps = sb("eps", [P, 2])
        last = sb("last", [P, 2, KT])
        identb = sb("identb", [P, P], BF16)
        causb = sb("causb", [P, P + C], BF16)
        lvl = sb("lvl", [P, len(LEVELS), P], U8)
        mx = sb("mx", [P, 8])
        ps = ctx.enter_context(nc.psum_tensor("ps", [P, 8, 512], F32))

        Af = A[:, :, :].rearrange("p a n -> p (a n)")
        Bf = B[:, :, :].rearrange("p a n -> p (a n)")
        Tf = TM[:, :, :].rearrange("p a n -> p (a n)")
        eLC = Bf[:, 21 * T:21 * T + NPAIR * (NCHUNK + 1)].rearrange("p (a n) -> p a n", a=NPAIR)

        def k(name):
            o, n = CST[name]
            return cst[:, o:o + n]

        def v1(name, kt):
            return vec[:, V[name], kt:kt + 1]

        def c3(ap):
            return ap.rearrange("p (c n) -> p c n", c=NCH)

        def pset(s):
            return ps[:, NCH * s:NCH * s + NCH, 0:CH]

        d_cum = scratch("d_cum", [HF, SEQ])
        d_cums = scratch("d_cums", [HF, NALL])
        d_x = {n: scratch(f"d_{n}", [NPAIR, P, T]) for n in
               ("w", "a", "g", "r", "k", "v", "bh", "kh", "ah", "rh", "bonus")}

        names = ["setup", "held", "x_in", "mm_done", "read0", "read1", "w_used", "sq_ready", "sq_used", "rs_ready",
                 "normed", "h_ready", "pe_step", "act_step", "dve_step", "pool_step", "out_done",
                 "wv_in", "v_ready", "tm_free", "ax_ready", "gate_ready", "p_in",
                 "cum_ready", "cum_out", "cum_in", "stage_in", "staged", "s_done", "s_read", "p_ready", "e_ready",
                 "pt_done", "pt_read", "o_done", "o_read", "ot_done", "ot_read", "kv_in", "attn_pair",
                 "xn_ready", "xn_tmp", "xs0", "xs1", "xs2", "xs3", "zi", "key_sq", "rk_ready", "m_first", "gn_in", "dev_sq",
                 "b_out", "shift_in", "conv_out",
                 "g_done", "g_ready", "t_done", "t_ready", "n_ready", "m_ready", "y_done", "y_ready",
                 "z_done", "c_done", "c_ready", "c_u", "c_st", "c_in", "chunk_done", "st_ready", "state_in", "pa_done", "pb_done",
                 "o_all", "l_in", "l_out", "dve_p", "act_p", "pool_p", "gn_ready"]
        S = {n: sem(n) for n in names}
        for j in range(SLOTS):
            S[f"w{j}"] = sem(f"w{j}")
        block = ctx.enter_context(nc.Block())


        @block.sync
        def _(sp):
            t = Tally(sp)

            def chunk(src, n, rows=P):
                w = t.n.get("chunk", 0)
                slot = w % SLOTS
                t.up("chunk")
                if t.some("chunk", -3):
                    sp.wait_ge(S["w_used"], t.val("chunk", -3))
                sp.dma_start(W[0:rows, slot, 0:n], src).then_inc(S[f"w{slot}"], 16)

            for dst, src in ((cst[:, :], I["cst"]), (vec[:, :, :], I["vecs"]), (convw[:, :, :], I["convw"]),
                             (convs[:, :, :], I["convs"]), (bf[:, :], I["bf"]), (TM[:, 3, 0:len(LEVELS) * P], I["lvl"])):
                sp.dma_start(dst, src).then_inc(S["setup"], 16)
            for j in range(KT):
                sp.dma_start(H[:, j, :], I["x"][:, j, :]).then_inc(S["x_in"], 16)
            sp.dma_start(Bf[:, 8 * T:8 * T + KT * 512], I["wv"]).then_inc(S["wv_in"], 16)

            for j in range(2 * NA):
                chunk(I["wqk"][j], KT * P)
            chunk(I["wf"], KT * HF)
            for j in range(3 * NA):
                chunk(I["wconv"][j], KT * P)
            with t.loop(2, chunk=4) as i:
                for j in range(4):
                    chunk(I["wout"][bass.ds(i * 4 + j, 1)].rearrange("a p n -> (a p) n"), KT * P)

            def channel_mixer(l):
                with t.loop(NF // 2, chunk=4) as i:
                    for j in range(4):
                        chunk(I["wgu"][l, bass.ds(i * 4 + j, 1)].rearrange("a p n -> (a p) n"), KT * P)
                with t.loop(KT // 2, chunk=4) as i:
                    for j in range(4):
                        chunk(I["wdown"][l, bass.ds(i * 4 + j, 1)].rearrange("a p n -> (a p) n"), SLOT)
                t.up("p_in", 16)
                sp.wait_ge(S["normed"], 8 * (5 * l + 5))
                sp.dma_start(B[:, 0:NP_, :], I["p"][l]).then_inc(S["p_in"], 16)
                with t.loop(KT // 2, chunk=4) as i:
                    for j in range(2):
                        chunk(I["wpg"][l, bass.ds(i * 2 + j, 1)].rearrange("a p n -> (a p) n"), KT * P)
                        chunk(I["wpp"][l, bass.ds(i * 2 + j, 1)].rearrange("a p n -> (a p) n"), NP_ * P)

            channel_mixer(0)
            if stop < 2:
                return
            chunk(I["lw1"], KT * C)
            chunk(I["lw2"], D, C)
            chunk(I["la1"], KT * C)
            chunk(I["la2"], D, C)
            chunk(I["lg1"], KT * P)
            chunk(I["lg2"], D)
            with t.loop(3 * KT // 4, chunk=4) as i:
                for j in range(4):
                    chunk(I["wrkv"][bass.ds(i * 4 + j, 1)].rearrange("a p n -> (a p) n"), KT * P)
            with t.loop(2, chunk=4) as i:
                for j in range(4):
                    chunk(I["wo"][bass.ds(i * 4 + j, 1)].rearrange("a p n -> (a p) n"), KT * P)
            channel_mixer(1)

        @block.tensor
        def _(pe):
            t = Tally(pe)

            def first_use(ins):
                ins.then_inc(S["w_used"], 1)

            def unit(chunks, xs, cols=P, rows=P, ws=None):
                s, mm, rd = t.unit()
                pe.wait_ge(S[f"read{s}"], t.val(f"read{s}", -1))
                n, total = 0, sum(chunks)
                for count in chunks:
                    w = t.n.get("chunk", 0)
                    slot = w % SLOTS
                    t.up("chunk")
                    t.up("w_used")
                    pe.wait_ge(S[f"w{slot}"], t.up(f"w{slot}", 16))
                    for j in range(count):
                        for c in range(NCH):
                            ins = nc.tensor.matmul(
                                ps[0:cols, NCH * s + c, 0:CH], W[0:rows, slot, j * cols:(j + 1) * cols],
                                xs[n][0:rows, c * CH:(c + 1) * CH], start=(n == 0), stop=(n == total - 1))
                            if j == 0 and c == 0:
                                first_use(ins)
                        n += 1
                ins.then_inc(S["mm_done"], 1)

            def sums(lhs, x):
                s, mm, rd = t.unit()
                if t.some(f"read{s}", -1):
                    pe.wait_ge(S[f"read{s}"], t.val(f"read{s}", -1))
                for c in range(NCH):
                    ins = nc.tensor.matmul(ps[:, NCH * s + c, 0:CH], lhs, x[:, c * CH:(c + 1) * CH],
                                           start=True, stop=True)
                ins.then_inc(S["mm_done"], 1)

            def norm():
                pe.wait_ge(S["sq_used"], t.up("sq_used", KT))
                sums(k("ones"), TM[:, 2, :])

            def wait_normed():
                pe.wait_ge(S["normed"], t.up("normed", KT))

            xs = [A[:, j, :] for j in range(KT)]

            def dense8(count):
                with t.loop(count // 4, chunk=4, w_used=4, mm_done=4, read0=2, read1=2, w0=16, w1=16, w2=16, w3=16):
                    for j in range(4):
                        unit([KT], xs)

            pe.wait_ge(S["setup"], 96)
            norm()
            wait_normed()
            pe.wait_ge(S["wv_in"], 16)
            wv = Bf[:, 8 * T:8 * T + KT * 512].rearrange("p (k n) -> p k n", k=KT)
            for tt in range(9):
                s, mm, rd = t.unit()
                if t.some(f"read{s}", -1):
                    pe.wait_ge(S[f"read{s}"], t.val(f"read{s}", -1))
                c0, n = (P0 + P * tt, P) if tt < 8 else (S0, DEC)
                for j in range(KT):
                    ins = nc.tensor.matmul(ps[0:n, NCH * s, :], A[:, j, c0:c0 + n], wv[:, j, :],
                                           start=(j == 0), stop=(j == KT - 1))
                ins.then_inc(S["mm_done"], 1)
            dense8(8)
            unit([KT], xs, cols=HF)
            for j in range(3 * NA):
                unit([KT], xs)

            def s_set(u):
                return ps[:, 2 * (u % 2):2 * (u % 2) + 2, :]

            PTp = [ps[:, 4 + b, :] for b in range(2)]
            Qs = Af[:, 0:T]
            Ks = Af[:, T:2 * T]
            Vs = Af[:, 2 * T:2 * T + 1024].rearrange("p (b n) -> p b n", b=8)
            PTs = Tf[:, 0:2048].rearrange("p (u n) -> p u n", u=2)

            def scores(u):
                qb, h = u // 2, u % 2
                r = slice(C * h, C * h + C)
                nk = P * (qb + 1)
                if u >= 2:
                    pe.wait_ge(S["s_read"], t.val("s_done", -1))
                st = s_set(u)
                for n0 in range(0, nk, 512):
                    n1 = min(nk, n0 + 512)
                    nc.tensor.matmul(st[:, n0 // 512, 0:n1 - n0], Qs[r, P0 + P * qb:P0 + P * qb + P],
                                     Ks[r, P0 + n0:P0 + n1], start=True, stop=True)
                o = (nk - P) % 512
                nc.tensor.matmul(st[:, (nk - P) // 512, o:o + P], identb[:, :], causb[:, 0:P],
                                 start=False, stop=True, skip_group_check=True).then_inc(S["s_done"], 1)
                t.up("s_done")

            def values(u):
                qb, h = u // 2, u % 2
                pe.wait_ge(S["e_ready"], t.up("e_ready"))
                E = Af[:, 2 * T + 1024 + 2048 + 1024 * (u % 2):][:, 0:1024]
                for b in range(qb + 1):
                    ins = nc.tensor.transpose(PTp[b // 4][:, P * (b % 4):P * (b % 4) + P], E[:, P * b:P * b + P],
                                              k("ident"))
                ins.then_inc(S["pt_done"], 1)
                pe.wait_ge(S["pt_read"], t.up("pt_done"))
                if u >= 2:
                    pe.wait_ge(S["o_read"], t.val("o_done", -1))
                if h == 0 and qb:
                    pe.wait_ge(S["ot_read"], t.val("ot_done"))
                for b in range(qb + 1):
                    ins = nc.tensor.matmul(ps[:, 6 + h, 0:C], PTs[:, 0, P * b:P * b + P],
                                           Vs[:, b, C * h:C * h + C], start=(b == 0), stop=(b == qb))
                ins.then_inc(S["o_done"], 1)
                t.up("o_done")

            def turn(n, qb):
                pe.wait_ge(S["o_read"], t.val("o_done"))
                OT = Tf[:, 2048:2048 + P]
                ins = nc.tensor.transpose(ps[0:n, 6, 0:P], OT[:, 0:n], k("ident"))
                ins.then_inc(S["ot_done"], 1)
                t.up("ot_done")

            pe.wait_ge(S["read0"], t.val("read0"))
            pe.wait_ge(S["read1"], t.val("read1"))
            with t.loop(4, s_done=16, e_ready=16, pt_done=16, o_done=16, ot_done=8, staged=1):
                pe.wait_ge(S["staged"], t.up("staged"))
                scores(0)
                for u in range(16):
                    if u < 15:
                        scores(u + 1)
                    values(u)
                    if u % 2:
                        turn(P, u // 2)

            t.up("kv_in", 128)
            Kc = Af[:, 0:PAST]
            Vc = Af[:, PAST:2 * PAST].rearrange("p (b n) -> p b n", b=16)
            Es = Af[:, 2 * PAST:2 * PAST + NALL]
            sm = Tf[:, 2304:]
            Qn, Kn, Vn, OTs = sm[:, 0:P], sm[:, P:P + C], sm[:, P + C:2 * P + C], sm[:, 2 * P + C:3 * P]
            PTl = Tf[:, 0:17 * P]
            with t.loop(4, s_done=3, e_ready=1, pt_done=3, o_done=1, ot_done=1, staged=1, kv_in=64):
                pe.wait_ge(S["staged"], t.up("staged"))
                pe.wait_ge(S["kv_in"], t.up("kv_in", 64))
                for piece in range(3):
                    pe.wait_ge(S["s_read"], t.val("s_done", -1))
                    st = ps[:, 2 * (piece % 2):2 * (piece % 2) + 2, :]
                    if piece < 2:
                        for n in range(2):
                            ins = nc.tensor.matmul(st[:, n, :], Qn, Kc[:, 1024 * piece + 512 * n:1024 * piece + 512 * n + 512],
                                                   start=True, stop=True)
                    else:
                        nc.tensor.matmul(st[:, 0, 0:C], Qn, Kn, start=True, stop=False)
                        ins = nc.tensor.matmul(st[:, 0, 0:C], identb[:, :], causb[:, P:P + C], start=False, stop=True)
                    ins.then_inc(S["s_done"], 1)
                    t.up("s_done")
                pe.wait_ge(S["e_ready"], t.up("e_ready"))
                for part in range(3):
                    pe.wait_ge(S["pt_read"], t.val("pt_done"))
                    pe.sem_inc(S["held"], 1)
                    for b in range(8 * part, min(17, 8 * part + 8)):
                        n = P if b < 16 else C
                        ins = nc.tensor.transpose(PTp[b % 8 // 4][0:n, P * (b % 4):P * (b % 4) + P],
                                                  Es[:, P * b:P * b + n], k("ident"))
                    ins.then_inc(S["pt_done"], 1)
                    t.up("pt_done")
                pe.wait_ge(S["pt_read"], t.val("pt_done"))
                pe.wait_ge(S["o_read"], t.val("o_done"))
                for h in range(2):
                    r = slice(C * h, C * h + C)
                    for b in range(17):
                        n = P if b < 16 else C
                        vb = Vc[:, b, C * h:C * h + C] if b < 16 else Vn[0:C, C * h:C * h + C]
                        ins = nc.tensor.matmul(ps[r, 6, 0:C], PTl[0:n, P * b + C * h:P * b + C * h + C], vb,
                                               start=(b == 0), stop=(b == 16), skip_group_check=True)
                ins.then_inc(S["o_done"], 1)
                t.up("o_done")
                pe.wait_ge(S["o_read"], t.val("o_done"))
                pe.wait_ge(S["ot_read"], t.val("ot_done"))
                pe.sem_inc(S["held"], 1)
                nc.tensor.transpose(ps[0:C, 7, 0:P], OTs, k("ident")).then_inc(S["ot_done"], 1)
                t.up("ot_done")
            pe.wait_ge(S["ot_read"], t.val("ot_done"))

            xs = [B[:, 8 + j, :] for j in range(KT)]
            dense8(KT)

            def channel_mixer():
                nonlocal xs
                norm()
                t.up("normed", KT)
                norm()
                wait_normed()
                xs = [A[:, j, :] for j in range(KT)]
                dense8(2 * NF)
                pe.wait_ge(S["read0"], t.val("read0"))
                pe.wait_ge(S["read1"], t.val("read1"))
                mid = [B[:, j, :] for j in range(NF)]
                with t.loop(KT // 2, chunk=4, w_used=4, mm_done=2, read0=1, read1=1, w0=16, w1=16, w2=16, w3=16):
                    for j in range(2):
                        unit([HALF, HALF], mid)
                norm()
                t.up("normed", KT)
                norm()
                wait_normed()
                pe.wait_ge(S["p_in"], t.up("p_in", 16))
                with t.loop(KT // 2, chunk=4, w_used=4, mm_done=4, read0=2, read1=2, w0=16, w1=16, w2=16, w3=16):
                    for j in range(2):
                        unit([KT], xs)
                        unit([NP_], [B[:, 0, :], B[:, 1, :]])

            channel_mixer()
            if stop < 2:
                return

            norm()
            t.up("normed", KT)
            X = [[B[:, 8 * b + j, :] for j in range(KT)] for b in range(2)]

            def lora(b, first, rows, out):
                pe.wait_ge(S["xn_ready"], t.up("xn_ready", KT))
                unit([KT], X[b], cols=rows)
                s = (t.n["mm_done"] - 1) % 2
                pe.wait_ge(S[f"read{s}"], t.val(f"read{s}"))
                w = t.n.get("chunk", 0)
                slot = w % SLOTS
                t.up("chunk")
                t.up("w_used")
                pe.wait_ge(S[f"w{slot}"], t.up(f"w{slot}", 16))
                for m in range(KT):
                    s, mm, rd = t.unit()
                    pe.wait_ge(S[f"read{s}"], t.val(f"read{s}", -1))
                    for c in range(NCH):
                        ins = nc.tensor.matmul(ps[:, NCH * s + c, 0:CH], W[0:rows, slot, m * P:(m + 1) * P],
                                               out[0:rows, c * CH:(c + 1) * CH], start=True, stop=True)
                        if m == 0 and c == 0:
                            first_use(ins)
                    ins.then_inc(S["mm_done"], 1)

            lora(0, 0, C, B[:, 16, :])
            lora(1, 0, C, B[:, 17, :])
            lora(0, 0, P, B[:, 16, :])
            for n in range(3):
                pe.wait_ge(S["xn_ready"], t.up("xn_ready", KT))
                xs = X[(n + 1) % 2]
                dense8(KT)

            with t.loop(NPAIR, mm_done=2, read0=1, read1=1, key_sq=1, rk_ready=1):
                pe.wait_ge(S["key_sq"], t.up("key_sq"))
                sums(k("pair"), TM[:, 1, :])
                pe.wait_ge(S["rk_ready"], t.up("rk_ready"))
                sums(k("pair"), TM[:, 2, :])

            for s in range(2):
                pe.wait_ge(S[f"read{s}"], t.val(f"read{s}"))
            ZF = Bf[:, 0:4608]
            ZB, ZA, ZV = (ZF[:, 1536 * j:1536 * j + 1536].rearrange("p (a n) -> p a n", a=NPAIR) for j in range(3))
            CB = Bf[:, 9 * T:]
            BK, UV, NT, AB, M, MT, Y = (CB[:, 1024 * j:1024 * j + 1024].rearrange("p (a n) -> p a n", a=NPAIR)
                                       for j in range(7))
            G = CB[:, 7168:7168 + 2048].rearrange("p (a n) -> p a n", a=2 * NPAIR)
            P1 = CB[:, 9216:9216 + 512].rearrange("p (a n) -> p a n", a=NPAIR)
            ST = CB[:, 9728:9728 + 1024].rearrange("p (a n) -> p a n", a=NPAIR)

            def chunk():
                pe.wait_ge(S["zi"], t.up("zi", 7 * 16))
                for g in range(2):
                    for a in range(4):
                        for h in range(2):
                            r = slice(C * h, C * h + C)
                            p = 4 * g + a
                            ins = nc.tensor.matmul(ps[:, 4 * g + h, P * a:P * a + P],
                                                   ZB[r, p, C * h:C * h + P], ZA[r, p, C * h:C * h + P],
                                                   start=True, stop=True)
                    ins.then_inc(S["g_done"], 1)
                    t.up("g_done")
                for g in range(2):
                    for a in range(4):
                        for h in range(2):
                            p = 4 * g + a
                            r = slice(C * h, C * h + C)
                            for j, z in enumerate((ZB, ZV)):
                                o = P * a + C * j
                                ins = nc.tensor.transpose(ps[:, 4 * g + 2 + h, o:o + C],
                                                          z[r, p, C * h:C * h + P], k("ident")[r, r])
                    ins.then_inc(S["t_done"], 1)
                    t.up("t_done")
                for g in range(2):
                    pe.wait_ge(S["m_first"], t.up("m_first"))
                    pe.wait_ge(S["t_ready"], t.up("t_ready", 2))
                    for a in range(4):
                        nc.tensor.transpose(ps[:, 4 * g + 2, P * a:P * a + P], NT[:, 4 * g + a, :], k("ident"))
                        ins = nc.tensor.transpose(ps[:, 4 * g + 3, P * a:P * a + P], M[:, 4 * g + a, :], k("ident"))
                    ins.then_inc(S["t_done"], 1)
                    t.up("t_done")
                for l in range(len(LEVELS)):
                    for g in range(2):
                        pe.wait_ge(S["t_ready"], t.up("t_ready", 2 if l == 0 else 1))
                        for a in range(4):
                            ins = nc.tensor.matmul(ps[:, 4 * g, P * a:P * a + P], AB[:, 4 * g + a, :],
                                                   M[:, 4 * g + a, :], start=True, stop=True)
                        ins.then_inc(S["y_done"], 1)
                        t.up("y_done")
                    for g in range(2):
                        pe.wait_ge(S["y_ready"], t.up("y_ready"))
                        for a in range(4):
                            ins = nc.tensor.matmul(ps[:, 4 * g + 1, P * a:P * a + P], MT[:, 4 * g + a, :],
                                                   Y[:, 4 * g + a, :], start=True, stop=True)
                        ins.then_inc(S["z_done"], 1)
                        t.up("z_done")
                    for g in range(2):
                        pe.wait_ge(S["m_ready"], t.up("m_ready"))
                        if l < len(LEVELS) - 1:
                            for a in range(4):
                                ins = nc.tensor.transpose(ps[:, 4 * g + 2, P * a:P * a + P], M[:, 4 * g + a, :],
                                                          k("ident"))
                            ins.then_inc(S["t_done"], 1)
                            t.up("t_done")
                for g in range(2):
                    for a in range(4):
                        p = 4 * g + a
                        for h in range(2):
                            r, q = slice(C * h, C * h + C), slice(C * h, C * h + C)
                            nc.tensor.matmul(ps[r, 4 * g + 3, C * a:C * a + C], G[:, 2 * p + h, q], UV[:, p, q],
                                             start=True, stop=False, skip_group_check=True)
                            ins = nc.tensor.matmul(ps[r, 4 * g + 3, C * a:C * a + C], ZA[:, p, P * h:P * h + C],
                                                   ST[:, p, q], start=False, stop=True, skip_group_check=True)
                    ins.then_inc(S["c_done"], 1)
                    t.up("c_done")
                for g in range(2):
                    pe.wait_ge(S["c_ready"], t.up("c_ready"))
                    for a in range(4):
                        p = 4 * g + a
                        ins = nc.tensor.matmul(ps[:, 4 * g + 3, 256 + C * a:256 + C * a + C], M[:, p, :], P1[:, p, :],
                                               start=True, stop=True)
                    ins.then_inc(S["c_done"], 1)
                    t.up("c_done")
                for g in range(2):
                    pe.wait_ge(S["c_ready"], t.up("c_ready"))
                    for a in range(4):
                        p = 4 * g + a
                        for h in range(2):
                            r = slice(C * h, C * h + C)
                            ins = nc.tensor.matmul(ps[r, 4 * g + 1, C * a:C * a + C], BK[:, p, C * h:C * h + C],
                                                   UV[:, p, C * h:C * h + C], start=True, stop=True,
                                                   skip_group_check=True)
                    ins.then_inc(S["c_done"], 1)
                    t.up("c_done")
                    for a in range(4):
                        p = 4 * g + a
                        for h in range(2):
                            r = slice(C * h, C * h + C)
                            nc.tensor.matmul(ps[r, 4 * g, C * a:C * a + C], UV[:, p, C * h:C * h + C],
                                             G[:, 2 * p + h, C - C * h:P - C * h], start=True, stop=False,
                                             skip_group_check=True)
                            ins = nc.tensor.matmul(ps[r, 4 * g, C * a:C * a + C], ST[:, p, C * h:C * h + C],
                                                   ZA[:, p, C:2 * C], start=False, stop=True,
                                                   skip_group_check=True)
                    ins.then_inc(S["c_done"], 1)
                    t.up("c_done")
                pe.wait_ge(S["c_in"], t.up("c_in", 4))

            per = dict(zi=7 * 16, g_done=2, t_done=4 + 2 * (len(LEVELS) - 1), m_first=2, m_ready=2 * len(LEVELS),
                       t_ready=4 + 4 + 2 * (len(LEVELS) - 1), y_done=2 * len(LEVELS), y_ready=2 * len(LEVELS),
                       z_done=2 * len(LEVELS), c_done=8, c_ready=4, c_in=4)
            pe.wait_ge(S["st_ready"], 1)
            with t.loop(NCHUNK, **per):
                chunk()
            pe.wait_ge(S["state_in"], 32)
            chunk()

            with t.loop(NPAIR, mm_done=2, read0=1, read1=1, dev_sq=1, gn_in=32) as i:
                pe.wait_ge(S["gn_in"], t.up("gn_in", 32))
                sums(k("pair"), A[:, bass.ds(i, 1), :].rearrange("p a n -> p (a n)"))
                pe.wait_ge(S["dev_sq"], t.up("dev_sq"))
                sums(k("pair"), TM[:, 1, :])
            pe.wait_ge(S["gn_ready"], NPAIR)
            xs = [B[:, 8 + j, :] for j in range(KT)]
            dense8(KT)
            channel_mixer()

        @block.scalar
        def _(act):
            t = Tally(act)

            def square(src, needs=None):
                j = t.n.get("sq_ready", 0) % 2
                if t.some("sq_ready", -1):
                    act.wait_ge(S["sq_used"], t.val("sq_ready", -1))
                nc.scalar.activation(TM[:, j, :], src, ACT.Square).then_inc(S["sq_ready"], 1)
                t.up("sq_ready")

            def root(scale=1.0 / D, e=0):
                s, mm, rd = t.unit()
                act.wait_ge(S["mm_done"], mm)
                nc.scalar.activation(c3(TM[:, 3, :]), pset(s), ACT.Sqrt, scale=scale,
                                     bias=eps[:, e:e + 1]).then_inc(S[f"read{s}"], 1)

            def copy_unit(dst, cols=P, func=ACT.Copy, **kw):
                s, mm, rd = t.unit()
                act.wait_ge(S["mm_done"], mm)
                nc.scalar.activation(c3(dst)[0:cols], pset(s)[0:cols], func, **kw).then_inc(S[f"read{s}"], 1)
                return s, rd

            act.wait_ge(S["setup"], 96 + 4)
            act.wait_ge(S["x_in"], 16 * KT)
            for j in range(KT):
                square(H[:, j, :])
            root()
            Vt = Bf[:, 16 * T:16 * T + 9 * 512].rearrange("p (b n) -> p b n", b=9)
            for tt in range(9):
                s, mm, rd = t.unit()
                act.wait_ge(S["mm_done"], mm)
                n = P if tt < 8 else DEC
                nc.scalar.activation(Vt[0:n, tt, :], ps[0:n, NCH * s, :], ACT.Copy).then_inc(S[f"read{s}"], 1)
            with t.loop(2, mm_done=4, read0=2, read1=2) as i:
                for j in range(4):
                    copy_unit(B[:, bass.ds(i * 4 + j, 1), :].rearrange("p a n -> p (a n)"))
            t.skip(1)
            for c in range(NA):
                if t.some("ax_ready"):
                    act.wait_ge(S["tm_free"], t.val("ax_ready"))
                s, mm, rd = t.unit()
                act.wait_ge(S["mm_done"], mm)
                nc.scalar.activation(c3(TM[:, 0, :]), pset(s), ACT.Copy).then_inc(S[f"read{s}"], 1)
                t.up("ax_ready")
                t.skip(2)

            z, e = B[0:HF, 21, :], Af[0:HF, 0:T]
            act.wait_ge(S["dve_p"], t.up("dve_p"))
            act.wait_ge(S["mm_done"], t.val("mm_done"))
            nc.scalar.activation(e, z, ACT.Abs).then_inc(S["act_step"], 1)
            act.wait_ge(S["act_step"], t.up("act_step"))
            nc.scalar.activation(e, e, ACT.Exp, scale=-1.0).then_inc(S["act_step"], 1)
            act.wait_ge(S["act_step"], t.up("act_step"))
            nc.scalar.activation(e, e, ACT.Ln, bias=1.0).then_inc(S["act_p"], 1)
            t.up("act_p")

            E0 = 2 * T + 1024 + 2048
            PTs = Tf[:, 0:2048].rearrange("p (u n) -> p u n", u=2)
            PTp = ps[:, 4:6, :].rearrange("p b n -> p (b n)")
            PTl = Tf[:, 0:17 * P]
            OT = Tf[:, 2048:2048 + P]
            Vpair = Bf[:, 16 * T:16 * T + 9 * 512].rearrange("p (b h n) -> p b h n", b=9, h=4)

            def exp(u, n, E):
                act.wait_ge(S["p_ready"], t.up("p_ready"))
                nc.scalar.activation(E, E, ACT.Exp, scale=0.125, bias=mx[:, 2 * u + 1:2 * u + 2],
                                     accum_out=mx[:, 4 + u:5 + u]).then_inc(S["e_ready"], 1)
                t.up("e_ready")

            def turned(u, n):
                act.wait_ge(S["pt_done"], t.up("pt_done"))
                if u:
                    act.wait_ge(S["o_done"], t.val("o_done"))
                nc.scalar.activation(PTs[:, 0, 0:n], PTp[:, 0:n], ACT.Copy).then_inc(S["pt_read"], 1)
                t.up("pt_read")

            with t.loop(4, p_ready=16, e_ready=16, pt_done=16, pt_read=16, o_done=16, ot_done=8, ot_read=8) as i:
                exp(0, P, Af[:, E0:E0 + P])
                for u in range(16):
                    if u < 15:
                        n1 = P * ((u + 1) // 2 + 1)
                        exp((u + 1) % 2, n1, Af[:, E0 + 1024 * ((u + 1) % 2):][:, 0:n1])
                    turned(u, P * (u // 2 + 1))
                    t.up("o_done")
                    if u % 2:
                        act.wait_ge(S["ot_done"], t.up("ot_done"))
                        qb = u // 2
                        nc.scalar.activation(B[:, bass.ds(i + 12, 1), P0 + P * qb:P0 + P * qb + P].rearrange("p a n -> p (a n)"),
                                             ps[:, 6, 0:P], ACT.Copy).then_inc(S["ot_read"], 1)
                        t.up("ot_read")
            Es = Af[:, 2 * PAST:2 * PAST + NALL]
            with t.loop(4, p_ready=1, e_ready=1, pt_done=3, pt_read=3, o_done=1, ot_done=1, ot_read=1) as i:
                exp(0, NALL, Es)
                for part in range(3):
                    act.wait_ge(S["pt_done"], t.up("pt_done"))
                    act.wait_ge(S["o_done"], t.val("o_done"))
                    if part < 2:
                        nc.scalar.activation(PTl[:, 1024 * part:1024 * part + 1024], PTp[:, :],
                                             ACT.Copy).then_inc(S["pt_read"], 1)
                    else:
                        nc.scalar.activation(PTl[0:C, 2048:2048 + P], PTp[0:C, 0:P],
                                             ACT.Copy).then_inc(S["pt_read"], 1)
                    t.up("pt_read")
                t.up("o_done")
                act.wait_ge(S["ot_done"], t.up("ot_done"))
                for h in range(2):
                    ins = nc.scalar.activation(
                        B[C * h:C * h + C, bass.ds(i + 12, 1), S0:T].rearrange("p a n -> p (a n)"),
                        ps[0:C, 7, C * h:C * h + C], ACT.Copy)
                ins.then_inc(S["ot_read"], 1)
                t.up("ot_read")

            def output_tiles(count):
                for j in range(count):
                    s, mm, rd = t.unit()
                    act.wait_ge(S["mm_done"], mm)
                    nc.scalar.activation(c3(A[:, j, :]), pset(s), ACT.Copy).then_inc(S[f"read{s}"], 1)
                    act.wait_ge(S[f"read{s}"], rd)
                    square(A[:, j, :])

            def post_and_pre():
                root()
                for j in range(KT):
                    act.wait_ge(S["h_ready"], t.up("h_ready"))
                    square(H[:, j, :])
                root()

            def channel_mixer():
                output_tiles(KT)
                post_and_pre()
                with t.loop(NF // 2, mm_done=4, read0=2, read1=2) as i:
                    for j in range(2):
                        s, mm, rd = t.unit()
                        act.wait_ge(S["mm_done"], mm)
                        act.wait_ge(S[f"read{1 - s}"], t.val(f"read{1 - s}", -1))
                        nc.scalar.activation(c3(TM[:, j, :]), pset(s), ACT.Silu).then_inc(S[f"read{s}"], 1)
                        t.skip(1)
                output_tiles(KT)
                post_and_pre()
                with t.loop(KT // 2, mm_done=4, read0=2, read1=2, h_ready=2) as i:
                    for j in range(2):
                        s, mm, rd = t.unit()
                        act.wait_ge(S["mm_done"], mm)
                        act.wait_ge(S["h_ready"], t.val("h_ready", -1))
                        nc.scalar.activation(c3(TM[:, j, :]), pset(s), ACT.Sigmoid).then_inc(S[f"read{s}"], 1)
                        t.up("h_ready")
                        t.skip(1)

            channel_mixer()
            if stop < 2:
                return

            act.wait_ge(S["h_ready"], t.val("h_ready"))
            for j in range(KT):
                square(H[:, j, :])
            root()
            act.wait_ge(S["dve_p"], t.up("dve_p"))

            def mix(n):
                for kt in range(KT):
                    j = t.n.get("xn_tmp", 0) % 2
                    if t.some("xn_tmp", -1):
                        act.wait_ge(S["xn_ready"], t.val("xn_tmp", -1))
                    nc.scalar.activation(TM[:, j, :], A[:, kt, :], ACT.Copy,
                                         scale=mub[:, n, kt:kt + 1]).then_inc(S["xn_tmp"], 1)
                    t.up("xn_tmp")

            def stage_first(func, bias):
                for n in range(KT):
                    j = n % 4
                    s, mm, rd = t.unit()
                    act.wait_ge(S["mm_done"], mm)
                    if n >= 4:
                        t.up(f"xs{j}", 16)
                        act.wait_ge(S[f"xs{j}"], t.val(f"xs{j}"))
                    nc.scalar.activation(c3(B[:, 18 + j, :]), pset(s), func,
                                         bias=v1(bias, n)).then_inc(S[f"read{s}"], 1)

            def stage(func=ACT.Copy, bias=None):
                with t.loop(2, mm_done=4, read0=2, read1=2, xs0=16, xs1=16, xs2=16, xs3=16) as i:
                    for j in range(4):
                        s, mm, rd = t.unit()
                        act.wait_ge(S["mm_done"], mm)
                        act.wait_ge(S[f"xs{j}"], t.val(f"xs{j}"))
                        t.up(f"xs{j}", 16)
                        kw = dict(bias=vec[:, V[bias], bass.ds(i * 4 + j, 1)]) if bias else {}
                        nc.scalar.activation(c3(B[:, 18 + j, :]), pset(s), func, **kw).then_inc(S[f"read{s}"], 1)

            def hidden(slot, rows, func):
                s, mm, rd = t.unit()
                act.wait_ge(S["mm_done"], mm)
                nc.scalar.activation(c3(B[:, slot, :])[0:rows], pset(s)[0:rows], func).then_inc(S[f"read{s}"], 1)

            mix(1)
            hidden(16, C, ACT.Tanh)
            mix(4)
            stage_first(ACT.Sigmoid, "w0")
            for j in range(4):
                t.up(f"xs{j}", 16)
            hidden(17, C, ACT.Copy)
            mix(5)
            stage(ACT.Sigmoid, bias="a0")
            hidden(16, P, ACT.Sigmoid)
            mix(0)
            stage()
            mix(2)
            stage()
            mix(3)
            stage()
            stage()

            L = {n: B[:, 1 + j, :] for j, n in enumerate(("r", "k", "v", "w", "a"))}
            Q = [B[:, 8 + j, :] for j in range(8)]
            with t.loop(NPAIR, l_in=80, act_p=4, dve_p=2, mm_done=2, read0=1, read1=1, pool_p=1, act_step=1, key_sq=1) as i:
                act.wait_ge(S["l_in"], t.up("l_in", 80))
                nc.scalar.activation(Q[0], L["k"], ACT.Copy, scale=vec[:, V["kk"], bass.ds(i, 1)]).then_inc(S["act_step"], 1)
                act.wait_ge(S["act_step"], t.up("act_step"))
                nc.scalar.activation(TM[:, 1, :], Q[0], ACT.Square).then_inc(S["key_sq"], 1)
                t.up("key_sq")
                nc.scalar.activation(Q[1], L["w"], ACT.Copy, scale=-DECAY).then_inc(S["act_p"], 1)
                t.up("act_p")
                s, mm, rd = t.unit()
                act.wait_ge(S["mm_done"], mm)
                nc.scalar.activation(c3(TM[:, 3, :]), pset(s), ACT.Sqrt).then_inc(S[f"read{s}"], 1)
                t.skip(1)
                act.wait_ge(S["dve_p"], t.up("dve_p"))
                nc.scalar.activation(Q[3], Q[2], ACT.Exp).then_inc(S["act_p"], 1)
                act.wait_ge(S["act_p"], t.up("act_p"))
                for c0, n, o in ((P0, NCHUNK, 0), (S0, 1, NCHUNK)):
                    nc.scalar.activation(eLC[:, bass.ds(i, 1), o:o + n].rearrange("p a n -> p (a n)"),
                                         Q[3][:, c0 + C - 1:c0 + C * n:C], ACT.Copy)
                nc.scalar.activation(Q[4], Q[2], ACT.Exp, scale=-1.0).then_inc(S["act_p"], 1)
                t.up("act_p")
                act.wait_ge(S["pool_p"], t.up("pool_p"))
                nc.scalar.activation(Q[1], Q[1], ACT.Exp).then_inc(S["act_p"], 1)
                t.up("act_p")
                t.up("dve_p")

            CB = Bf[:, 9 * T:]
            BK, UV, NT, AB, M, MT, Y = (CB[:, 1024 * j:1024 * j + 1024] for j in range(7))
            P1 = CB[:, 9216:9216 + 512]
            BKUV = CB[:, 0:2048].rearrange("p (j a n) -> p a j n", j=2, a=NPAIR)

            def chunk(c0, dyn):
                def flat(ap):
                    return ap.rearrange("p a n -> p (a n)")
                for g in range(2):
                    act.wait_ge(S["t_done"], t.up("t_done"))
                    for h in range(2):
                        nc.scalar.activation(BKUV[:, 4 * g:4 * g + 4, :, C * h:C * h + C],
                                             ps[:, 4 * g + 2 + h, :].rearrange("p (a j n) -> p a j n", a=4, j=2),
                                             ACT.Copy).then_inc(S["t_ready"], 1)
                    t.up("t_ready", 2)
                for g in range(2):
                    act.wait_ge(S["t_done"], t.up("t_done"))
                    nc.scalar.activation(AB[:, 512 * g:512 * g + 512], ps[:, 4 * g + 2, :], ACT.Copy).then_inc(S["t_ready"], 1)
                    nc.scalar.activation(MT[:, 512 * g:512 * g + 512], ps[:, 4 * g + 3, :], ACT.Copy).then_inc(S["t_ready"], 1)
                    t.up("t_ready", 2)
                for l in range(len(LEVELS)):
                    for g in range(2):
                        act.wait_ge(S["y_done"], t.up("y_done"))
                        nc.scalar.activation(Y[:, 512 * g:512 * g + 512], ps[:, 4 * g, :], ACT.Copy).then_inc(S["y_ready"], 1)
                        t.up("y_ready")
                    if l < len(LEVELS) - 1:
                        for g in range(2):
                            act.wait_ge(S["t_done"], t.up("t_done"))
                            nc.scalar.activation(MT[:, 512 * g:512 * g + 512], ps[:, 4 * g + 2, :],
                                                 ACT.Copy).then_inc(S["t_ready"], 1)
                            t.up("t_ready")
                for g in range(2):
                    act.wait_ge(S["c_done"], t.up("c_done"))
                    nc.scalar.activation(P1[:, 256 * g:256 * g + 256], ps[:, 4 * g + 3, 0:256],
                                         ACT.Copy).then_inc(S["c_ready"], 1)
                    t.up("c_ready")
                for g in range(2):
                    act.wait_ge(S["c_done"], t.up("c_done"))
                    for h in range(2):
                        r = slice(C * h, C * h + C)
                        ins = nc.scalar.activation(
                            UV[:, :].rearrange("p (a n) -> p a n", a=NPAIR)[r, 4 * g:4 * g + 4, C * h:C * h + C],
                            ps[r, 4 * g + 3, 256:512].rearrange("p (a n) -> p a n", a=4), ACT.Copy)
                    ins.then_inc(S["c_ready"], 1)
                    t.up("c_ready")
                for g in range(2):
                    t.up("c_done")
                    act.wait_ge(S["c_done"], t.up("c_done"))
                    dst = A[:, 4 * g:4 * g + 4, bass.ds(c0, C)] if dyn else A[:, 4 * g:4 * g + 4, c0:c0 + C]
                    nc.scalar.activation(dst, ps[:, 4 * g, 0:256].rearrange("p (a n) -> p a n", a=4),
                                         ACT.Copy).then_inc(S["c_in"], 1)

            per = dict(t_done=4 + 2 * (len(LEVELS) - 1), t_ready=8 + 2 * (len(LEVELS) - 1), y_done=2 * len(LEVELS),
                       y_ready=2 * len(LEVELS), c_done=8, c_ready=4)
            with t.loop(NCHUNK, **per) as i:
                chunk(i * C + P0, True)
            chunk(S0, False)

            with t.loop(NPAIR, mm_done=2, read0=1, read1=1, dev_sq=1) as i:
                s, mm, rd = t.unit()
                act.wait_ge(S[f"read{s}"], rd)
                nc.scalar.activation(TM[:, 1, :], TM[:, 0, :], ACT.Square).then_inc(S["dev_sq"], 1)
                t.up("dev_sq")
                s, mm, rd = t.unit()
                act.wait_ge(S["mm_done"], mm)
                nc.scalar.activation(c3(TM[:, 2, :]), pset(s), ACT.Sqrt, scale=1.0 / C,
                                     bias=eps[:, 1:2]).then_inc(S[f"read{s}"], 1)
            channel_mixer()

        @block.vector
        def _(dve):
            t = Tally(dve)

            def step(ins):
                ins.then_inc(S["dve_step"], 1)
                dve.wait_ge(S["dve_step"], t.up("dve_step"))

            def stt(out, in0, scalar, in1, op0, op1):
                return nc.vector.scalar_tensor_tensor(out=out, in0=in0, scalar=scalar, in1=in1, op0=op0, op1=op1)

            def sum_squares():
                for j in range(KT):
                    dve.wait_ge(S["sq_ready"], t.up("sq_ready"))
                    if j == 0:
                        ins = nc.vector.tensor_copy(TM[:, 2, :], TM[:, 0, :])
                    else:
                        dve.wait_ge(S["sq_used"], t.val("sq_used"))
                        ins = nc.vector.tensor_tensor(TM[:, 2, :], TM[:, 2, :], TM[:, j % 2, :], ALU.add)
                    ins.then_inc(S["sq_used"], 1)
                    t.up("sq_used")

            def rstd():
                s, mm, rd = t.unit()
                dve.wait_ge(S[f"read{s}"], rd)
                step(nc.vector.reciprocal(TM[:, 3, :], TM[:, 3, :]))

            def pre_norm(gain):
                sum_squares()
                rstd()
                for j in range(KT):
                    stt(A[:, j, :], H[:, j, :], v1(gain, j), TM[:, 3, :], ALU.mult, ALU.mult).then_inc(S["normed"], 1)
                    t.up("normed")

            def post_norm(gain):
                sum_squares()
                rstd()
                for j in range(KT):
                    stt(A[:, j, :], A[:, j, :], v1(gain, j), TM[:, 3, :], ALU.mult, ALU.mult).then_inc(S["normed"], 1)
                    dve.wait_ge(S["normed"], t.up("normed"))
                    nc.vector.tensor_tensor(H[:, j, :], H[:, j, :], A[:, j, :], ALU.add).then_inc(S["h_ready"], 1)
                    t.up("h_ready")

            dve.wait_ge(S["setup"], 96)
            nc.vector.memset(eps[:, 0:1], NORM_EPS)
            nc.vector.memset(eps[:, 1:2], GN_EPS).then_inc(S["setup"], 1)
            nc.vector.tensor_scalar(mub[:, :, :], vec[:, V["mu0"]:V["mu0"] + 6, :], -1.0, 1.0, ALU.mult,
                                    ALU.add).then_inc(S["setup"], 1)
            nc.vector.tensor_scalar(kab[:, :], vec[:, V["ka"], :], -1.0, 1.0, ALU.mult, ALU.add).then_inc(S["setup"], 1)
            nc.vector.tensor_copy(lvl[:, :, :].rearrange("p a n -> p (a n)"), TM[:, 3, 0:len(LEVELS) * P])
            nc.vector.tensor_copy(identb[:, :], k("ident"))
            nc.vector.tensor_copy(causb[:, :], cst[:, 3 * P:4 * P + C]).then_inc(S["setup"], 1)
            dve.wait_ge(S["x_in"], 16 * KT)
            dve.wait_ge(S["setup"], 100)
            pre_norm("pre0")
            t.skip(9 + 8)
            s, mm, rd = t.unit()
            dve.wait_ge(S["mm_done"], mm)
            nc.vector.tensor_scalar(c3(B[0:HF, 21, :]), pset(s)[0:HF], bf[:, 0:1], None,
                                    ALU.add).then_inc(S[f"read{s}"], 1)
            for c in range(NA):
                s, mm, rd = t.unit()
                dve.wait_ge(S[f"read{s}"], rd)
                s, mm, rd = t.unit()
                dve.wait_ge(S["mm_done"], mm)
                if c:
                    dve.wait_ge(S["conv_out"], 32 * c)
                nc.vector.tensor_tensor(c3(TM[:, 1, :]), pset(s), c3(TM[:, 0, :]), ALU.mult).then_inc(S[f"read{s}"], 1)
                dve.wait_ge(S[f"read{s}"], rd)
                nc.vector.memset(TM[:, 1, 0:PAD], 0.0).then_inc(S["dve_step"], 1)
                t.up("dve_step")
                nc.vector.tensor_copy(TM[:, 1, S0 - PAD:S0], convs[:, c, :]).then_inc(S["tm_free"], 1)
                dve.wait_ge(S["tm_free"], t.up("tm_free"))
                n = T - PAD
                step(nc.vector.tensor_scalar(TM[:, 2, PAD:T], TM[:, 1, 0:n], convw[:, 0, c:c + 1], None, ALU.mult))
                step(stt(TM[:, 2, PAD:T], TM[:, 1, 1:n + 1], convw[:, 1, c:c + 1], TM[:, 2, PAD:T], ALU.mult, ALU.add))
                step(stt(TM[:, 2, PAD:T], TM[:, 1, 2:T], convw[:, 2, c:c + 1], TM[:, 2, PAD:T], ALU.mult, ALU.add))
                step(nc.vector.memset(TM[:, 2, 0:PAD], 0.0))
                s, mm, rd = t.unit()
                dve.wait_ge(S["mm_done"], mm)
                nc.vector.tensor_tensor(c3(B[:, 8 + c, :]), pset(s), c3(TM[:, 2, :]), ALU.mult).then_inc(S[f"read{s}"], 1)
                dve.wait_ge(S[f"read{s}"], rd)
            z, e = B[0:HF, 21, :], Af[0:HF, 0:T]
            nc.vector.memset(B[:, 12:16, 0:PAD], 0.0)
            nc.vector.memset(B[:, 12:16, S0 - PAD:S0], 0.0).then_inc(S["dve_p"], 1)
            t.up("dve_p")
            dve.wait_ge(S["act_p"], t.up("act_p"))
            lf, zero = Af[0:HF, T:2 * T], Af[0:HF, 2 * T:2 * T + NALL]
            full, cum = Af[0:HF, 5000:5000 + NALL], Tf[0:HF, 0:NALL]
            cump = Tf[0:HF, NALL:NALL + SEQ]
            step(stt(lf, z, 0.0, e, ALU.min, ALU.subtract))
            step(nc.vector.memset(zero, 0.0))
            dve.wait_ge(S["cum_in"], t.up("cum_in", 16))
            step(nc.vector.tensor_copy(full[:, PAST:NALL], lf[:, S0:T]))
            nc.vector.tensor_tensor_scan(cump, lf[:, P0:P0 + SEQ], zero[:, 0:SEQ], 0.0, ALU.add, ALU.subtract)
            step(nc.vector.tensor_tensor_scan(cum, full, zero, 0.0, ALU.add, ALU.subtract))
            step(nc.vector.tensor_scalar(cump, cump, -8.0, None, ALU.mult))
            nc.vector.tensor_scalar(cum, cum, -8.0, None, ALU.mult).then_inc(S["cum_ready"], 1)

            E0 = 2 * T + 1024 + 2048
            OT = Tf[:, 2048:2048 + P]
            bc = Af[:, 2 * T + 1024:2 * T + 1024 + 2048].rearrange("p (h n) -> p h n", h=2)

            def out_scaled(u, dst, src, turned):
                dve.wait_ge(S["e_ready"], t.up("e_ready"))
                step(nc.vector.reciprocal(mx[:, 6 + u % 2:7 + u % 2], mx[:, 4 + u % 2:5 + u % 2]))
                dve.wait_ge(S["o_done"], t.up("o_done"))
                if turned:
                    dve.wait_ge(S["ot_done"], t.val("ot_done"))
                nc.vector.tensor_scalar(dst, src, mx[:, 6 + u % 2:7 + u % 2], None, ALU.mult).then_inc(S["o_read"], 1)
                t.up("o_read")

            sc = ps[:, :, :].rearrange("p b n -> p (b n)")
            with t.loop(4, s_done=16, s_read=16, p_ready=16, e_ready=16, o_done=16, o_read=16, ot_done=8, ptd=16,
                        dve_step=16, kv_in=32) as i:
                dve.wait_ge(S["kv_in"], t.up("kv_in", 32))
                for u in range(17):
                    if u < 16:
                        qb, h = u // 2, u % 2
                        n = P * (qb + 1)
                        if u >= 2:
                            dve.wait_ge(S["pt_done"], t.val("ptd", -1))
                        t.up("ptd")
                        dve.wait_ge(S["s_done"], t.up("s_done"))
                        dve.sem_inc(S["held"], 1)
                        E = Af[:, E0 + 1024 * h:E0 + 1024 * h + n]
                        nc.vector.tensor_tensor_reduce(out=E, in0=sc[:, 1024 * h:1024 * h + n], in1=bc[:, h, 0:n],
                                                       scale=1.0, scalar=-3e38, op0=ALU.add, op1=ALU.max,
                                                       accum_out=mx[:, 2 * h:2 * h + 1]).then_inc(S["s_read"], 1)
                        dve.wait_ge(S["s_read"], t.up("s_read"))
                        nc.vector.tensor_scalar(mx[:, 2 * h + 1:2 * h + 2], mx[:, 2 * h:2 * h + 1], -0.125, None,
                                                ALU.mult).then_inc(S["p_ready"], 1)
                        t.up("p_ready")
                    if u > 0:
                        w = u - 1
                        out_scaled(w, OT[:, C * (w % 2):C * (w % 2) + C], ps[:, 6 + w % 2, 0:C], w // 2)
                        if w % 2:
                            t.up("ot_done")
            Es = Af[:, 2 * PAST:2 * PAST + NALL]
            bcs = Af[:, 2 * PAST + NALL:2 * PAST + 2 * NALL]
            OTs = Tf[:, 2304 + 2 * P + C:2304 + 3 * P]
            with t.loop(4, s_done=3, s_read=3, p_ready=1, e_ready=1, o_done=1, o_read=1, ot_done=1, dve_step=1,
                        kv_in=64) as i:
                dve.wait_ge(S["kv_in"], t.up("kv_in", 64))
                for piece in range(3):
                    n = 1024 if piece < 2 else C
                    dve.wait_ge(S["s_done"], t.up("s_done"))
                    dve.sem_inc(S["held"], 1)
                    nc.vector.tensor_tensor_reduce(out=Es[:, 1024 * piece:1024 * piece + n],
                                                   in0=sc[:, 1024 * (piece % 2):1024 * (piece % 2) + n],
                                                   in1=bcs[:, 1024 * piece:1024 * piece + n], scale=1.0,
                                                   scalar=-3e38 if piece == 0 else mx[:, 0:1],
                                                   op0=ALU.add, op1=ALU.max, accum_out=mx[:, 0:1]).then_inc(S["s_read"], 1)
                    dve.wait_ge(S["s_read"], t.up("s_read"))
                nc.vector.tensor_scalar(mx[:, 1:2], mx[:, 0:1], -0.125, None, ALU.mult).then_inc(S["p_ready"], 1)
                t.up("p_ready")
                out_scaled(0, OTs, ps[:, 6, 0:C], 0)
                t.up("ot_done")
            t.skip(KT)

            def channel_mixer(l):
                post_norm(f"post{l}")
                pre_norm(f"fpre{l}")
                with t.loop(NF // 2, mm_done=4, read0=2, read1=2) as i:
                    for j in range(2):
                        s, mm, rd = t.unit()
                        dve.wait_ge(S[f"read{s}"], rd)
                        s, mm, rd = t.unit()
                        dve.wait_ge(S["mm_done"], mm)
                        nc.vector.tensor_tensor(c3(B[:, bass.ds(i * 2 + j, 1), :].rearrange("p a n -> p (a n)")),
                                                pset(s), c3(TM[:, j, :]), ALU.mult).then_inc(S[f"read{s}"], 1)
                t.skip(KT)
                post_norm(f"fpost{l}")
                pre_norm(f"ple{l}")
                with t.loop(KT // 2, mm_done=4, read0=2, read1=2, h_ready=2) as i:
                    for j in range(2):
                        s, mm, rd = t.unit()
                        dve.wait_ge(S[f"read{s}"], rd)
                        s, mm, rd = t.unit()
                        dve.wait_ge(S["mm_done"], mm)
                        nc.vector.tensor_tensor(c3(TM[:, j, :]), pset(s), c3(TM[:, j, :]), ALU.mult).then_inc(S[f"read{s}"], 1)
                        dve.wait_ge(S[f"read{s}"], rd)
                        nc.vector.tensor_tensor(H[:, bass.ds(i * 2 + j, 1), :].rearrange("p a n -> p (a n)"),
                                                H[:, bass.ds(i * 2 + j, 1), :].rearrange("p a n -> p (a n)"),
                                                TM[:, j, :], ALU.add).then_inc(S["h_ready"], 1)
                        t.up("h_ready")

            channel_mixer(0)
            if stop < 2:
                return

            pre_norm("pre1")
            dve.wait_ge(S["normed"], t.val("normed"))
            for g, c in enumerate((S0 - PAD - 1, T - 1)):
                ins = nc.vector.tensor_copy(last[:, g, :], A[:, :, c:c + 1].rearrange("p a n -> p (a n)"))
            ins.then_inc(S["shift_in"], 1)
            nc.vector.memset(A[:, :, P0 - 1:P0], 0.0)
            nc.vector.tensor_copy(A[:, :, S0 - 1:S0].rearrange("p a n -> p (a n)"), vec[:, V["shift"], :]).then_inc(S["dve_p"], 1)
            dve.wait_ge(S["dve_p"], t.up("dve_p"))
            mm0 = t.n["mm_done"]
            read_by = [mm0 + 1, mm0 + 10, mm0 + 19, mm0 + 35, mm0 + 43, mm0 + 51]
            nc.vector.memset(B[:, 0:16, 0:1], 0.0).then_inc(S["dve_step"], 1)
            dve.wait_ge(S["dve_step"], t.up("dve_step"))
            for order, n in enumerate((1, 4, 5, 0, 2, 3)):
                b = order % 2
                if order >= 2:
                    dve.wait_ge(S["mm_done"], read_by[order - 2])
                for kt in range(KT):
                    j = t.n.get("xn_tmp", 0) % 2
                    dve.wait_ge(S["xn_tmp"], t.up("xn_tmp"))
                    stt(B[:, 8 * b + kt, 1:T], A[:, kt, 0:T - 1], vec[:, V["mu0"] + n, kt:kt + 1], TM[:, j, 1:T],
                        ALU.mult, ALU.add).then_inc(S["xn_ready"], 1)
                    t.up("xn_ready")
            t.skip(51)

            L = {n: B[:, 1 + j, :] for j, n in enumerate(("r", "k", "v", "w", "a"))}
            Q = [B[:, 8 + j, :] for j in range(8)]
            reset = B[:, 16, :]
            dve.wait_ge(S["mm_done"], read_by[5])
            step(nc.vector.memset(reset, 1.0))
            nc.vector.memset(reset[:, P0:P0 + SEQ:C], 0.0)
            nc.vector.memset(reset[:, S0:S0 + 1], 0.0)
            step(nc.vector.memset(A[:, :, :], 0.0))
            with t.loop(NPAIR, l_in=80, act_p=4, dve_p=2, mm_done=2, read0=1, read1=1, dve_step=9, rk_ready=1) as i:
                dve.wait_ge(S["l_in"], t.up("l_in", 80))
                step(nc.vector.tensor_scalar(Q[5], L["a"], vec[:, V["ka"], bass.ds(i, 1)], kab[:, bass.ds(i, 1)], ALU.mult, ALU.add))
                step(nc.vector.tensor_tensor(Q[5], Q[5], L["k"], ALU.mult))
                stt(TM[:, 2, :], L["r"], vec[:, V["rk"], bass.ds(i, 1)], Q[5], ALU.mult, ALU.mult).then_inc(S["rk_ready"], 1)
                t.up("rk_ready")
                dve.wait_ge(S["act_p"], t.up("act_p"))
                nc.vector.tensor_tensor_scan(Q[2], reset, Q[1], 0.0, ALU.mult, ALU.add).then_inc(S["dve_p"], 1)
                t.up("dve_p")
                s, mm, rd = t.unit()
                dve.wait_ge(S[f"read{s}"], rd)
                step(nc.vector.tensor_scalar(TM[:, 3, :], TM[:, 3, :], L2_EPS, None, ALU.max))
                step(nc.vector.reciprocal(TM[:, 3, :], TM[:, 3, :]))
                step(nc.vector.tensor_tensor(Q[0], Q[0], TM[:, 3, :], ALU.mult))
                step(nc.vector.tensor_tensor(Q[7], Q[0], L["a"], ALU.mult))
                dve.wait_ge(S["act_p"], t.up("act_p"))
                step(nc.vector.tensor_tensor(L["r"], L["r"], Q[3], ALU.mult))
                dve.wait_ge(S["act_p"], t.up("act_p"))
                step(nc.vector.tensor_tensor(Q[7], Q[7], Q[4], ALU.mult))
                step(nc.vector.tensor_tensor(Q[5], Q[5], Q[4], ALU.mult))
                s, mm, rd = t.unit()
                dve.wait_ge(S["mm_done"], mm)
                nc.vector.tensor_tensor(c3(L["v"]), pset(s), c3(L["v"]), ALU.mult).then_inc(S[f"read{s}"], 1)
                dve.wait_ge(S["act_p"], t.up("act_p"))
                stt(Q[6], Q[0], -1.0, Q[1], ALU.mult, ALU.mult).then_inc(S["dve_p"], 1)
                t.up("dve_p")

            ZF = Bf[:, 0:4608]
            ZV = ZF[:, 3072:4608].rearrange("p (a n) -> p a n", a=NPAIR)
            CB = Bf[:, 9 * T:]
            NT, M = (CB[:, 1024 * j:1024 * j + 1024].rearrange("p (a n) -> p a n", a=NPAIR) for j in (2, 4))
            G = CB[:, 7168:7168 + 2048].rearrange("p (a h n) -> p a h n", a=NPAIR, h=2)
            ST = CB[:, 9728:9728 + 1024].rearrange("p (a n) -> p a n", a=NPAIR)
            dve.wait_ge(S["b_out"], 80 * NPAIR)
            nc.vector.memset(ZV, 0.0)
            nc.vector.memset(NT, 0.0)
            nc.vector.memset(ST, 0.0).then_inc(S["st_ready"], 1)

            def four(ap, n=P):
                return ap.rearrange("p (a n) -> p a n", a=1).to_broadcast([P, 4, n])

            def chunk(c):
                for g in range(2):
                    dve.wait_ge(S["g_done"], t.up("g_done"))
                    for h, mask in enumerate(("gram_even", "gram_odd")):
                        ins = nc.vector.tensor_tensor(G[:, 4 * g:4 * g + 4, h, :], ps[:, 4 * g + h, :].rearrange("p (a n) -> p a n", a=4),
                                                      four(k(mask)), ALU.mult)
                    ins.then_inc(S["g_ready"], 1)
                    t.up("g_ready")
                for l in range(len(LEVELS)):
                    for g in range(2):
                        dve.wait_ge(S["z_done"], t.up("z_done"))
                        dve.sem_inc(S["held"], 1)
                        nc.vector.copy_predicated(M[:, 4 * g:4 * g + 4, :], four(lvl[:, l, :]),
                                                  ps[:, 4 * g + 1, :].rearrange("p (a n) -> p a n", a=4)).then_inc(S["m_ready"], 1)
                        t.up("m_ready")
                t.up("c_done", 4)
                for g in range(2):
                    t.up("c_done")
                    dve.wait_ge(S["c_done"], t.up("c_done"))
                    for h in range(2):
                        r = slice(C * h, C * h + C)
                        st = ST[r, 4 * g:4 * g + 4, C * h:C * h + C]
                        step(nc.vector.tensor_tensor(st, ps[r, 4 * g + 1, 0:256].rearrange("p (a n) -> p a n", a=4), st, ALU.add))
                        ins = nc.vector.tensor_tensor(st, st, eLC[r, 4 * g:4 * g + 4, c].to_broadcast([C, 4, C]), ALU.mult)
                        if h == 0:
                            ins.then_inc(S["dve_step"], 1)
                            t.up("dve_step")
                    ins.then_inc(S["c_in"], 1)

            per = dict(g_done=2, g_ready=2, z_done=2 * len(LEVELS), m_ready=2 * len(LEVELS), c_done=8, dve_step=6)
            with t.loop(NCHUNK, **per) as i:
                chunk(bass.ds(i, 1))
            chunk(slice(NCHUNK, NCHUNK + 1))

            with t.loop(NPAIR, mm_done=2, read0=1, read1=1, gn_in=32, dve_step=3) as i:
                dve.wait_ge(S["gn_in"], t.up("gn_in", 32))
                s, mm, rd = t.unit()
                dve.wait_ge(S["mm_done"], mm)
                stt(c3(TM[:, 0, :]), pset(s), -1.0 / C, c3(A[:, bass.ds(i, 1), :].rearrange("p a n -> p (a n)")),
                    ALU.mult, ALU.add).then_inc(S[f"read{s}"], 1)
                s, mm, rd = t.unit()
                dve.wait_ge(S[f"read{s}"], rd)
                step(nc.vector.reciprocal(TM[:, 2, :], TM[:, 2, :]))
                step(stt(TM[:, 0, :], TM[:, 0, :], vec[:, V["lnw"], bass.ds(i, 1)], TM[:, 2, :], ALU.mult, ALU.mult))
                step(stt(TM[:, 0, :], TM[:, 0, :], vec[:, V["lnb"], bass.ds(i, 1)], B[:, 0, :], ALU.add, ALU.add))
                nc.vector.tensor_tensor(B[:, bass.ds(i + 8, 1), :].rearrange("p a n -> p (a n)"), TM[:, 0, :], B[:, 1, :],
                                        ALU.mult).then_inc(S["gn_ready"], 1)
            t.skip(KT)
            channel_mixer(1)

        @block.gpsimd
        def _(pool):
            t = Tally(pool)

            def store(dst, src):
                pool.dma_start(dst, src).then_inc(S["out_done"], 16)
                t.up("out_done", 16)

            t.skip(1)
            Vt = Bf[:, 16 * T:16 * T + 9 * 512].rearrange("p (b n) -> p b n", b=9)
            t.skip(9)
            pool.wait_ge(S["read0"], t.val("read0"))
            pool.wait_ge(S["read1"], t.val("read1"))
            store(O["v_p"], Vt[:, 0:8, :])
            store(O["v_s"], Vt[0:DEC, 8, :])
            n_v = t.n["out_done"]
            t.skip(8)
            pool.wait_ge(S["read0"], t.val("read0"))
            pool.wait_ge(S["read1"], t.val("read1"))
            store(O["k"], B[:, 4:8, :])
            t.skip(1)
            for c in range(NA):
                pool.wait_ge(S["tm_free"], t.up("tm_free"))
                pool.dma_start(O["conv"][:, c, 0:2], TM[:, 1, S0 - 2 * PAD:S0 - PAD]).then_inc(S["conv_out"], 16)
                pool.dma_start(O["conv"][:, c, 2:4], TM[:, 1, T - 2:T]).then_inc(S["conv_out"], 16)
                t.skip(3)
            pool.wait_ge(S["conv_out"], 32 * NA)
            pool.wait_ge(S["mm_done"], t.val("mm_done"))
            pool.dma_start(Af[0:HF, 5000:5000 + PAST], I["clogf"]).then_inc(S["cum_in"], 16)
            pool.wait_ge(S["cum_ready"], 1)
            store(O["logf"], Af[0:HF, T:2 * T])
            pool.dma_start(d_cum, Tf[0:HF, NALL:NALL + SEQ]).then_inc(S["cum_out"], 16)
            pool.dma_start(d_cums, Tf[0:HF, 0:NALL]).then_inc(S["cum_out"], 16)
            pool.wait_ge(S["cum_out"], 32)
            pool.wait_ge(S["out_done"], t.val("out_done"))

            bc = Af[:, 2 * T + 1024:2 * T + 1024 + 2048].rearrange("p (h n) -> p h n", h=2)
            Vs = Af[:, 2 * T:2 * T + 1024].rearrange("p (b n) -> p b n", b=8)
            d_c = d_cum.rearrange("(a h) n -> a h n", h=2)
            d_cs = d_cums.rearrange("(a h) n -> a h n", h=2)
            with t.loop(4, kv_in=32, staged=1, ot_read=8) as i:
                for h in range(2):
                    pool.dma_start(bc[:, h, :], d_c[bass.ds(i, 1), h, :].to_broadcast([P, SEQ])).then_inc(S["kv_in"], 16)
                nc.gpsimd.tensor_copy(Af[:, 0:T], B[:, bass.ds(i, 1), :].rearrange("p a n -> p (a n)"))
                nc.gpsimd.tensor_copy(Af[:, T:2 * T], B[:, bass.ds(i + 4, 1), :].rearrange("p a n -> p (a n)"))
                nc.gpsimd.tensor_copy(Vs, Vt[:, 0:8, bass.ds(i * P, P)]).then_inc(S["staged"], 1)
                t.up("staged")
                t.up("kv_in", 32)
                pool.wait_ge(S["ot_read"], t.up("ot_read", 8))
                pool.sem_inc(S["held"], 1)
            sm = Tf[:, 2304:]
            nc.gpsimd.memset(sm[:, 0:P], 0.0).then_inc(S["pool_step"], 1)
            pool.wait_ge(S["pool_step"], t.up("pool_step"))
            pool.sem_inc(S["held"], 1)
            kc = I["ck"]
            with t.loop(4, kv_in=64, staged=1, ot_read=1, pool_step=2) as i:
                pool.dma_start(Af[:, 0:PAST], kc[:, bass.ds(i, 1), :].rearrange("p a n -> p (a n)")).then_inc(S["kv_in"], 16)
                pool.dma_start(Af[:, PAST:2 * PAST].rearrange("p (b n) -> p b n", b=16),
                               I["cv"][:, :, bass.ds(i * P, P)]).then_inc(S["kv_in"], 16)
                for h in range(2):
                    src = d_cs[bass.ds(i, 1), h, :].to_broadcast([C, NALL])
                    pool.dma_start(Af[C * h:C * h + C, 2 * PAST + NALL:2 * PAST + 2 * NALL], src).then_inc(S["kv_in"], 16)
                nc.gpsimd.tensor_copy(sm[0:C, 0:C], B[0:C, bass.ds(i, 1), S0:T].rearrange("p a n -> p (a n)"))
                nc.gpsimd.tensor_copy(sm[C:P, C:P], B[C:P, bass.ds(i, 1), S0:T].rearrange("p a n -> p (a n)")).then_inc(S["pool_step"], 1)
                pool.wait_ge(S["pool_step"], t.up("pool_step"))
                pool.sem_inc(S["held"], 1)
                nc.gpsimd.tensor_copy(sm[:, P:P + C], B[:, bass.ds(i + 4, 1), S0:T].rearrange("p a n -> p (a n)")).then_inc(S["pool_step"], 1)
                pool.wait_ge(S["pool_step"], t.up("pool_step"))
                pool.sem_inc(S["held"], 1)
                nc.gpsimd.tensor_copy(sm[0:DEC, P + C:2 * P + C], Vt[0:DEC, 8, bass.ds(i * P, P)]).then_inc(S["staged"], 1)
                t.up("staged")
                t.up("kv_in", 64)
                pool.wait_ge(S["ot_read"], t.up("ot_read"))
                pool.sem_inc(S["held"], 1)

            def finish_y():
                pool.wait_ge(S["h_ready"], 48)
                pool.sem_inc(S["held"], 1)
                store(O["y"], H[:, :, :])
                pool.wait_ge(S["out_done"], t.val("out_done"))

            if stop < 2:
                pool.wait_ge(S["h_ready"], 24)
                pool.sem_inc(S["held"], 1)
                store(O["y"], H[:, :, :])
                pool.wait_ge(S["out_done"], t.val("out_done"))
                return

            pool.wait_ge(S["shift_in"], 1)
            store(O["shift"], last[:, :, :])

            UPTO = 1 + 9 + 8 + 1 + 3 * NA + KT + 2 + 2 * NF + KT + 2 + 2 * KT + 1
            t.n["mm_done"], t.n["read0"], t.n["read1"] = UPTO, (UPTO + 1) // 2, UPTO // 2

            def keep(name):
                with t.loop(2, mm_done=4, read0=2, read1=2, xs0=16, xs1=16, xs2=16, xs3=16) as i:
                    for j in range(4):
                        s, mm, rd = t.unit()
                        pool.wait_ge(S[f"read{s}"], rd)
                        pool.sem_inc(S["held"], 1)
                        pool.dma_start(d_x[name][bass.ds(i * 4 + j, 1)].rearrange("a p n -> (a p) n"),
                                       B[:, 18 + j, :]).then_inc(S[f"xs{j}"], 16)
                        t.up(f"xs{j}", 16)

            for name in "wag":
                t.skip(1)
                keep(name)
            for name in "rkv":
                keep(name)
            for j in range(4):
                pool.wait_ge(S[f"xs{j}"], t.val(f"xs{j}"))
            pool.wait_ge(S["mm_done"], t.val("mm_done"))

            L = {n: B[:, 1 + j, :] for j, n in enumerate(("r", "k", "v", "w", "a"))}
            Q = [B[:, 8 + j, :] for j in range(8)]
            t.n["dve_p"] = 2
            with t.loop(NPAIR, l_in=80, dve_p=2, pool_p=1, b_out=80) as i:
                for n in ("r", "k", "v", "w", "a"):
                    pool.dma_start(L[n], d_x[n][bass.ds(i, 1)].rearrange("a p n -> (a p) n")).then_inc(S["l_in"], 16)
                t.up("l_in", 80)
                pool.wait_ge(S["dve_p"], t.val("dve_p", 1))
                pool.sem_inc(S["held"], 1)
                nc.gpsimd.tensor_tensor(Q[1], Q[2], Q[1], ALU.subtract).then_inc(S["pool_p"], 1)
                t.up("pool_p")
                pool.wait_ge(S["dve_p"], t.val("dve_p", 2))
                pool.sem_inc(S["held"], 1)
                t.up("dve_p", 2)
                for n, src in (("bh", Q[7]), ("kh", Q[5]), ("ah", Q[6]), ("rh", L["r"]), ("bonus", L["v"])):
                    pool.dma_start(d_x[n][bass.ds(i, 1)].rearrange("a p n -> (a p) n"), src).then_inc(S["b_out"], 16)
                pool.wait_ge(S["b_out"], t.up("b_out", 80))
                pool.sem_inc(S["held"], 1)

            ZF = Bf[:, 0:4608]
            ZB, ZA, ZV = (ZF[:, 1536 * j:1536 * j + 1536].rearrange("p (a n) -> p a n", a=NPAIR) for j in range(3))
            CB = Bf[:, 9 * T:]
            NT, M = (CB[:, 1024 * j:1024 * j + 1024].rearrange("p (a n) -> p a n", a=NPAIR) for j in (2, 4))
            G = CB[:, 7168:7168 + 2048].rearrange("p (a h n) -> p a h n", a=NPAIR, h=2)
            ST = CB[:, 9728:9728 + 1024].rearrange("p (a n) -> p a n", a=NPAIR)

            def four(ap, n=P):
                return ap.rearrange("p (a n) -> p a n", a=1).to_broadcast([P, 4, n])

            def chunk(c0):
                cols = c0 if isinstance(c0, slice) else bass.ds(c0, C)
                for n, dst in (("bh", ZB[:, :, 0:C]), ("kh", ZB[:, :, C:P]), ("bh", ZB[:, :, P:P + C]),
                               ("ah", ZA[:, :, 0:C]), ("rh", ZA[:, :, C:P]), ("ah", ZA[:, :, P:P + C]),
                               ("v", ZV[:, :, C:P])):
                    pool.dma_start(dst, d_x[n].rearrange("a p n -> p a n")[:, :, cols]).then_inc(S["zi"], 16)
                for g in range(2):
                    a = slice(4 * g, 4 * g + 4)
                    pool.wait_ge(S["g_ready"], t.up("g_ready"))
                    pool.sem_inc(S["held"], 1)
                    nc.gpsimd.tensor_copy(NT[0:C, a, 0:C], G[0:C, a, 0, 0:C])
                    nc.gpsimd.tensor_copy(NT[C:P, a, C:P], G[C:P, a, 1, C:P]).then_inc(S["pool_step"], 1)
                    pool.wait_ge(S["pool_step"], t.up("pool_step"))
                    pool.sem_inc(S["held"], 1)
                    nc.gpsimd.tensor_tensor(M[:, a, :], NT[:, a, :], four(k("level0")), ALU.mult).then_inc(S["pool_step"], 1)
                    pool.wait_ge(S["pool_step"], t.up("pool_step"))
                    pool.sem_inc(S["held"], 1)
                    nc.gpsimd.tensor_tensor(M[:, a, :], M[:, a, :], four(k("ident")), ALU.add).then_inc(S["m_first"], 1)
                    pool.wait_ge(S["m_first"], t.up("m_first"))
                pool.wait_ge(S["c_in"], t.up("c_in", 4))
                pool.sem_inc(S["held"], 1)

            pool.wait_ge(S["st_ready"], 1)
            with t.loop(NCHUNK, g_ready=2, pool_step=4, m_first=2, c_in=4) as i:
                chunk(i * C + P0)
            for h in range(2):
                r = slice(C * h, C * h + C)
                store(O["wkv"][r, 0], ST[r, :, C * h:C * h + C])
            pool.wait_ge(S["out_done"], t.val("out_done"))
            for h in range(2):
                r = slice(C * h, C * h + C)
                pool.dma_start(ST[r, :, C * h:C * h + C], I["wkv"][r]).then_inc(S["state_in"], 16)
            chunk(slice(S0, T))
            for h in range(2):
                r = slice(C * h, C * h + C)
                store(O["wkv"][r, 1], ST[r, :, C * h:C * h + C])

            with t.loop(NPAIR, gn_in=32, gn_ready=1) as i:
                for j, n in enumerate(("bonus", "g")):
                    pool.dma_start(B[:, j, :], d_x[n][bass.ds(i, 1)].rearrange("a p n -> (a p) n")).then_inc(S["gn_in"], 16)
                t.up("gn_in", 32)
                pool.wait_ge(S["gn_ready"], t.up("gn_ready"))
                pool.sem_inc(S["held"], 1)
            finish_y()


def shape_constants():
    i = np.arange(P)
    eye = np.eye(P, dtype=np.float32)
    pair = (i[:, None] // C == i[None, :] // C).astype(np.float32)
    causal = np.where(i[None, :] > i[:, None], np.float32(NEG), np.float32(0))
    c = np.arange(C)
    causal2 = np.where(c[None, :] > (i % C)[:, None], np.float32(NEG), np.float32(0))
    strict = (c[:, None] < c[None, :]).astype(np.float32)
    incl = (c[:, None] <= c[None, :]).astype(np.float32)
    gram_even = np.block([[strict, incl], [strict, incl]])
    gram_odd = np.block([[incl, strict], [incl, strict]])

    def level(n):
        same = i[:, None] // (2 * n) == i[None, :] // (2 * n)
        return same & (i[:, None] % (2 * n) < n) & (i[None, :] % (2 * n) >= n)

    cst = np.concatenate([eye, np.ones((P, P), np.float32), pair, causal, causal2, gram_even, gram_odd,
                          level(1).astype(np.float32)], 1)
    lvl = np.stack([level(n) for n in LEVELS], 1).astype(np.float32).reshape(P, -1)
    return np.ascontiguousarray(cst), np.ascontiguousarray(lvl)


def kernel(**inputs):
    import concourse.bacc as bacc
    from concourse.bass_utils import run_bass_kernel_spmd

    X = {n: np.asarray(a) for n, a in inputs.items()}

    def feature_major(prompt, sample):
        n = prompt.shape[1] // P
        out = np.zeros((P, n, T), np.float32)
        out[:, :, P0:P0 + SEQ] = prompt.T.reshape(n, P, SEQ).transpose(1, 0, 2)
        out[:, :, S0:] = sample.T.reshape(n, P, DEC).transpose(1, 0, 2)
        return out

    def tiles(w, cols=P):
        kk, m = w.shape
        return w.reshape(kk // P, P, m // cols, cols).transpose(2, 1, 0, 3).reshape(m // cols, P, -1)

    def columns(v):
        return v.reshape(-1, P).T

    def laced(*ws):
        return np.stack(ws, 1).reshape(-1, *ws[0].shape[1:])

    cst, lvl = shape_constants()
    w_in = X["e_w_in"][0]
    ax, ab, ac = (w_in[:, DA * j:DA * j + DA] for j in range(3))
    rows = {"mu%d" % n: X["r_mu"][0, n] for n in range(6)}
    for n in range(2):
        for short, name in (("pre", "mix_norm_pre"), ("post", "mix_norm_post"), ("fpre", "ffn_norm_pre"),
                            ("fpost", "ffn_norm_post"), ("ple", "ple_norm")):
            rows[f"{short}{n}"] = X[name][n]
    for short, name in (("w0", "r_w0"), ("a0", "r_a0"), ("kk", "r_k_k"), ("ka", "r_k_a"), ("lnw", "r_ln_w"),
                        ("lnb", "r_ln_b")):
        rows[short] = X[name][0]
    rows["rk"] = X["r_r_k"][0].reshape(-1)
    rows["shift"] = X["state_shift"][0, 0]
    down = [X["f_w_down"][l].reshape(2, HALF, P, KT, P).transpose(3, 0, 2, 1, 4).reshape(2 * KT, P, SLOT)
            for l in range(2)]
    arrays = {
        "cst": cst, "lvl": lvl, "vecs": np.stack([columns(rows[n]) for n in VEC], 1),
        "convw": np.stack([columns(X["e_conv_w"][0, j]) for j in range(3)], 1),
        "convs": np.stack([columns(X["state_conv"][0, 0, j]) for j in range(2)], 2),
        "bf": X["e_b_f"][0].reshape(HF, 1),
        "x": feature_major(X["x_prompt"][0], X["x_sample"][0]),
        "p": np.stack([feature_major(X["p_prompt"][l, 0], X["p_sample"][l, 0]) for l in range(2)]),
        "wv": tiles(w_in[:, 3 * DA + 1024:3 * DA + 1536], 512)[0],
        "wqk": tiles(w_in[:, 3 * DA:3 * DA + 1024]),
        "wf": tiles(w_in[:, 3 * DA + 1536:], HF)[0],
        "wconv": laced(tiles(ax), tiles(ac), tiles(ab)),
        "wout": tiles(X["e_w_out"][0]),
        "wgu": np.stack([laced(tiles(X["f_w_gate"][l]), tiles(X["f_w_up"][l])) for l in range(2)]),
        "wdown": np.stack(down),
        "wpg": np.stack([tiles(X["ple_gate"][l]) for l in range(2)]),
        "wpp": np.stack([tiles(X["ple_proj"][l]) for l in range(2)]),
        "clogf": X["cache_logf"][0, 0].T,
        "ck": X["cache_k"][0, 0].reshape(PAST, NA, P).transpose(2, 1, 0),
        "cv": X["cache_v"][0, 0].reshape(PAST // P, P, 512).transpose(1, 0, 2),
        "lw1": tiles(X["r_w1"][0], C)[0], "lw2": X["r_w2"][0], "la1": tiles(X["r_a1"][0], C)[0], "la2": X["r_a2"][0],
        "lg1": tiles(X["r_g1"][0])[0], "lg2": X["r_g2"][0],
        "wrkv": np.concatenate([tiles(X[n][0]) for n in ("r_w_r", "r_w_k", "r_w_v")]),
        "wo": tiles(X["r_w_o"][0]),
        "wkv": X["state_wkv"][0, 0].reshape(NPAIR, 2, C, C).transpose(1, 3, 0, 2).reshape(P, NPAIR, C),
    }
    shapes = {"y": (P, KT, T), "k": (P, NA, T), "v_p": (P, 8, 512), "v_s": (DEC, 512), "logf": (HF, T),
              "conv": (P, NA, 4), "shift": (P, 2, KT), "wkv": (P, 2, NPAIR, C)}

    nc = bacc.Bacc("TRN2", target_bir_lowering=False, num_devices=1)
    feed, ins = {}, {}
    for n, a in arrays.items():
        a = np.ascontiguousarray(a)
        feed["in_" + n] = a
        ins[n] = nc.dram_tensor("in_" + n, a.shape, mybir.dt.from_np(a.dtype), kind="ExternalInput").ap()
    outs = {n: nc.dram_tensor("out_" + n, s, F32, kind="ExternalOutput").ap() for n, s in shapes.items()}
    build_trunk(nc, ins, outs)
    res = run_bass_kernel_spmd(nc, [feed], core_ids=[0]).results[0]
    got = {n: res["out_" + n] for n in shapes}

    def tokens(a):
        flat = a.transpose(1, 0, 2).reshape(-1, T).T
        return flat[P0:P0 + SEQ], flat[S0:]

    y_p, y_s = tokens(got["y"])
    k_p, k_s = tokens(got["k"])
    v_p = got["v_p"].transpose(1, 0, 2).reshape(SEQ, 512)
    conv = got["conv"].transpose(1, 0, 2).reshape(DA, 4).T
    shift = got["shift"].transpose(1, 2, 0).reshape(2, D)
    wkv = got["wkv"].reshape(2, C, 2, NPAIR, C).transpose(2, 3, 0, 4, 1).reshape(2, HR, C, C)
    lf = got["logf"].T
    heads = lambda a, n: np.ascontiguousarray(a).reshape(1, 1, n, HF, C)
    groups = []
    for g, (n, y, kk, vv, c0) in enumerate(((SEQ, y_p, k_p, v_p, P0), (DEC, y_s, k_s, got["v_s"], S0))):
        groups.append((np.ascontiguousarray(y)[None], heads(kk, n), heads(vv, n),
                       np.ascontiguousarray(lf[c0:c0 + n]).reshape(1, 1, n, HF),
                       np.ascontiguousarray(conv[2 * g:2 * g + 2]).reshape(1, 1, 2, DA),
                       np.ascontiguousarray(shift[g]).reshape(1, 1, D),
                       np.ascontiguousarray(wkv[g]).reshape(1, 1, HR, C, C)))
    (yp, *prompt), (ys, *sample) = groups
    return (yp, ys, *prompt, *sample)
```

```python
from contextlib import ExitStack, contextmanager

import numpy as np

import concourse.bass as bass
from concourse import mybir

F32 = mybir.dt.float32
F32R = mybir.dt.float32r
BF16 = mybir.dt.bfloat16
U8 = mybir.dt.uint8
ALU = mybir.AluOpType
ACT = mybir.ActivationFunctionType
AX_X = mybir.AxisListType.X

P = 128
D = 1024
KT = D // P
SEQ, DEC, PAST = 1024, 64, 2048
PAD = 2
P0 = PAD
S0 = PAD + SEQ + PAD
T = S0 + DEC
NCH = 3
CH = T // NCH
assert NCH * CH == T and CH <= 512
DA = 512
NA = DA // P
HF = 8
DFF = 2816
NF = DFF // P
HALF = NF // 2
PLE = 256
NP_ = PLE // P
HR = 16
NPAIR = HR // 2
C = 64
NCHUNK = SEQ // C
NALL = PAST + DEC
NORM_EPS, GN_EPS, L2_EPS = 1e-6, 64e-5, 1e-12
NEG = -1e30
DECAY = float(np.exp(-0.5))
SLOTS = 4
SLOT = HALF * P

MIXER = 4 * (NF // 2) + 2 * KT + 2 * KT
CHUNKS = [3 * 8 + 5, 3 * 8 + 5 + MIXER + 6 + 4 * KT]
NORMED = [2 * KT, 7 * KT]

VEC = ["pre0", "pre1", "post0", "post1", "fpre0", "fpre1", "fpost0", "fpost1", "ple0", "ple1",
       "mu0", "mu1", "mu2", "mu3", "mu4", "mu5", "w0", "a0", "kk", "ka", "rk", "lnw", "lnb", "shift"]
V = {n: i for i, n in enumerate(VEC)}
NV = len(VEC)
CST = {"ident": (0, P), "ones": (P, P), "pair": (2 * P, P), "causal": (3 * P, P), "causal2": (4 * P, C),
       "gram_even": (4 * P + C, P), "gram_odd": (5 * P + C, P), "ident2": (6 * P + C, C)}
NCST = 6 * P + 2 * C
LEVELS = (1, 2, 4, 8, 16, 32)
NL = len(LEVELS) - 1


class Tally:

    def __init__(self, engine):
        self.engine, self.n, self.per, self.i = engine, {}, {}, None

    def val(self, name, off=0):
        base = self.n.get(name, 0) + off
        if self.per.get(name):
            return self.i * self.per[name] + base
        return base

    def some(self, name, off=0):
        return bool(self.per.get(name)) or self.n.get(name, 0) + off > 0

    def up(self, name, k=1):
        self.n[name] = self.n.get(name, 0) + k
        return self.val(name)

    @contextmanager
    def loop(self, times, **per):
        before = dict(self.n)
        with self.engine.Fori(0, times) as i:
            self.i, self.per = i, per
            yield i
        for name in self.n.keys() | per.keys():
            moved = self.n.get(name, 0) - before.get(name, 0)
            assert moved == per.get(name, 0), (self.engine, name, moved, per.get(name, 0))
            self.n[name] = self.n.get(name, 0) + moved * (times - 1)
        self.i, self.per = None, {}

    def unit(self):
        s = self.n.get("mm_done", 0) % 2
        return s, self.up("mm_done"), self.up(f"read{s}")

    def skip(self, units):
        for _ in range(units):
            self.unit()

    def chunk(self):
        slot = self.n.get("chunk", 0) % SLOTS
        self.up("chunk")
        return slot, self.up(f"w{slot}", 16)

    def skip_chunks(self, chunks):
        for _ in range(chunks):
            self.chunk()


def build_trunk(nc, I, O, stop=99):
    ctx = ExitStack()
    with ctx:
        def sb(name, shape, dt=F32):
            return ctx.enter_context(nc.sbuf_tensor(name, shape, dt))

        def sem(name):
            return ctx.enter_context(nc.semaphore(name))

        def scratch(name, shape):
            return nc.dram_tensor(name, shape, F32, kind="Internal").ap()

        with ExitStack() as rounded:
            Hr, Ar, Br, Wr, TMr = (rounded.enter_context(nc.sbuf_tensor(n, shape, F32R)) for n, shape in (
                ("H_r", [P, KT, T]), ("A_r", [P, KT, T]), ("B_r", [P, NF, T]), ("W_r", [P, SLOTS, SLOT]),
                ("TM_r", [P, 4, T])))
        H = sb("H", [P, KT, T])
        A = sb("A", [P, KT, T])
        B = sb("B", [P, NF, T])
        W = sb("W", [P, SLOTS, SLOT])
        TM = sb("TM", [P, 4, T])
        cst = sb("cst", [P, NCST])
        vec = sb("vec", [P, NV, KT])
        convw = sb("convw", [P, 3, NA])
        convs = sb("convs", [P, NA, 2])
        bf = sb("bf", [HF, 1])
        mub = sb("mub", [P, 6, KT])
        kab = sb("kab", [P, KT])
        eps = sb("eps", [P, 2])
        last = sb("last", [P, 2, KT])
        identb = sb("identb", [P, P], BF16)
        causb = sb("causb", [P, P + C], BF16)
        lvl = sb("lvl", [P, len(LEVELS), C], U8)
        mx = sb("mx", [P, 8])
        ps = ctx.enter_context(nc.psum_tensor("ps", [P, 8, 512], F32))

        Af = A[:, :, :].rearrange("p a n -> p (a n)")
        Bf = B[:, :, :].rearrange("p a n -> p (a n)")
        Tf = TM[:, :, :].rearrange("p a n -> p (a n)")

        def wh_of(m):
            return TMr[:, 2 + m % 2, 0:KT * P]

        Lb = [{n: B[:, 4 * u + j, :] for j, n in enumerate("rkwa")} for u in range(2)]
        key2 = [A[:, 0, :], A[:, 1, :]]
        tmpA, cumL, expL, expnL, reset = A[:, 2, :], A[:, 3, :], B[:, 17, :], TM[:, 0, :], B[:, 16, :]
        bk_out = A[:, 4:6, :].rearrange("p a n -> p (a n)")[:, 0:(NCHUNK + 1) * P]
        ar_out = A[:, 6:8, :].rearrange("p a n -> p (a n)")[:, 0:(NCHUNK + 1) * P]

        Z = [[Bf[:, 4608 * u + 1536 * j:4608 * u + 1536 * j + 1536].rearrange("p (a n) -> p a n", a=NPAIR)
              for j in range(3)] for u in range(2)]
        BK, UV, BKUV, Gs, Ms, AB = [], [], [], [], [], []
        o_ = 9 * T
        for _ in range(2):
            BK.append(Bf[:, o_:o_ + NPAIR * P].rearrange("p (a n) -> p a n", a=NPAIR))
            UV.append(Bf[:, o_ + NPAIR * P:o_ + 2 * NPAIR * P].rearrange("p (a n) -> p a n", a=NPAIR))
            BKUV.append(Bf[:, o_:o_ + 2 * NPAIR * P].rearrange("p (j a n) -> p a j n", j=2, a=NPAIR))
            o_ += 2 * NPAIR * P
            for part, w_ in ((Gs, 2 * P), (AB, C), (Ms, P)):
                part.append(Bf[:, o_:o_ + NPAIR * w_].rearrange("p (a n) -> p a n", a=NPAIR))
                o_ += NPAIR * w_
        P1 = Bf[:, o_:o_ + NPAIR * C].rearrange("p (a n) -> p a n", a=NPAIR)
        assert o_ + NPAIR * C <= NF * T
        ST = Tf[:, 0:NPAIR * P].rearrange("p (a n) -> p a n", a=NPAIR)
        MT, Y = (Tf[:, NPAIR * (P + C * j):NPAIR * (P + C * j + C)].rearrange("p (a n) -> p a n", a=NPAIR)
                 for j in range(2))

        def four_of(bank, half):
            return ps[:, bank, 256 * half:256 * half + 256].rearrange("p (a n) -> p a n", a=4)

        eLC = sb("eLC", [P, NPAIR, NCHUNK + 1])

        def k(name):
            o, n = CST[name]
            return cst[:, o:o + n]

        def v1(name, kt):
            return vec[:, V[name], kt:kt + 1]

        def c3(ap):
            return ap.rearrange("p (c n) -> p c n", c=NCH)

        def pset(s):
            return ps[:, NCH * s:NCH * s + NCH, 0:CH]

        d_cum = scratch("d_cum", [HF, SEQ])
        d_cums = scratch("d_cums", [HF, NALL])
        d_x = {n: scratch(f"d_{n}", [NPAIR, P, T]) for n in
               ("w", "a", "g", "r", "k", "sum")}
        d_h = scratch("d_h", [P, KT, T])
        d_bk = scratch("d_bk", [NPAIR, P, (NCHUNK + 1) * P])
        d_ar = scratch("d_ar", [NPAIR, P, (NCHUNK + 1) * P])
        d_v = scratch("d_v", [NPAIR, P, (NCHUNK + 1) * C])

        names = ["setup", "held", "x_in", "mm_done", "read0", "read1", "w_used", "wl_ready", "xh_ready", "xl_ready", "h_out", "h_in", "sq_ready", "sq_used", "rs_ready",
                 "normed", "h_ready", "pe_step", "act_step", "dve_step", "pool_step", "out_done",
                 "wv_in", "v_ready", "tm_free", "ax_ready", "gate_ready", "p_in",
                 "cum_ready", "cum_out", "cum_in", "stage_in", "staged", "s_done", "s_read", "p_ready", "e_ready",
                 "pt_done", "pt_read", "o_done", "o_read", "ot_done", "ot_read", "kv_in", "attn_pair",
                 "xn_ready", "xn_tmp", "xv0", "xv1", "xv2", "xv3", "xs0", "xs1", "xs2", "xs3", "key_sq", "rk_ready", "gn_in", "dev_sq",
                 "b_out", "key_scaled", "sum_out", "pair_done", "pair_stored", "sum_stored", "rn_used", "l_in0", "l_in1", "gn_in0", "gn_in1", "mean_in", "gn_used", "shift_in", "conv_out",
                 "zi0", "zi1", "z_dup", "g_done", "g_ready", "m_init", "tok_done", "tok_read", "n_done", "n_ready", "mt_done", "mt_ready", "a_done", "a_ready", "u_done", "u_ready", "st_done", "oo_done", "m_ready", "m0_ready", "y_done", "y_ready",
                 "z_done", "c_done", "c_ready", "c_u", "c_st", "c_in", "chunk_done", "st_ready", "state_in", "state_out", "pa_done", "pb_done",
                 "o_all", "l_in", "l_out", "dve_p", "act_p", "pool_p", "gn_ready"]
        S = {n: sem(n) for n in names}
        for j in range(SLOTS):
            S[f"w{j}"] = sem(f"w{j}")
        block = ctx.enter_context(nc.Block())


        @block.sync
        def _(sp):
            t = Tally(sp)

            def chunk(src, n, rows=P):
                w = t.n.get("chunk", 0)
                slot = w % SLOTS
                t.up("chunk")
                if t.some("chunk", -3):
                    sp.wait_ge(S["w_used"], t.val("chunk", -3))
                sp.dma_start(W[0:rows, slot, 0:n], src).then_inc(S[f"w{slot}"], 16)

            for dst, src in ((cst[:, :], I["cst"]), (vec[:, :, :], I["vecs"]), (convw[:, :, :], I["convw"]),
                             (convs[:, :, :], I["convs"]), (bf[:, :], I["bf"]), (TM[:, 3, 0:len(LEVELS) * C], I["lvl"])):
                sp.dma_start(dst, src).then_inc(S["setup"], 16)
            for j in range(KT):
                sp.dma_start(H[:, j, :], I["x"][:, j, :]).then_inc(S["x_in"], 16)
            sp.dma_start(Bf[:, 8 * T:8 * T + KT * 512], I["wv"]).then_inc(S["wv_in"], 16)

            for j in range(2 * NA):
                chunk(I["wqk"][j], KT * P)
            chunk(I["wf"], KT * HF)
            for j in range(3 * NA):
                chunk(I["wconv"][j], KT * P)
            with t.loop(2, chunk=4) as i:
                for j in range(4):
                    chunk(I["wout"][bass.ds(i * 4 + j, 1)].rearrange("a p n -> (a p) n"), KT * P)

            def channel_mixer(l):
                with t.loop(NF // 2, chunk=4) as i:
                    for j in range(4):
                        chunk(I["wgu"][l, bass.ds(i * 4 + j, 1)].rearrange("a p n -> (a p) n"), KT * P)
                with t.loop(KT // 2, chunk=4) as i:
                    for j in range(4):
                        chunk(I["wdown"][l, bass.ds(i * 4 + j, 1)].rearrange("a p n -> (a p) n"), SLOT)
                t.up("p_in", 16)
                sp.wait_ge(S["normed"], KT * (5 * l + 3) + 1)
                sp.dma_start(B[:, 0:NP_, :], I["p"][l]).then_inc(S["p_in"], 16)
                with t.loop(KT // 2, chunk=4) as i:
                    for j in range(2):
                        chunk(I["wpg"][l, bass.ds(i * 2 + j, 1)].rearrange("a p n -> (a p) n"), KT * P)
                        chunk(I["wpp"][l, bass.ds(i * 2 + j, 1)].rearrange("a p n -> (a p) n"), NP_ * P)

            channel_mixer(0)
            if stop < 2:
                return
            chunk(I["lw1"], KT * C)
            chunk(I["lw2"], D, C)
            chunk(I["la1"], KT * C)
            chunk(I["la2"], D, C)
            chunk(I["lg1"], KT * P)
            chunk(I["lg2"], D)
            with t.loop(3 * KT // 4, chunk=4) as i:
                for j in range(4):
                    chunk(I["wrkv"][bass.ds(i * 4 + j, 1)].rearrange("a p n -> (a p) n"), KT * P)
            with t.loop(2, chunk=4) as i:
                for j in range(4):
                    chunk(I["wo"][bass.ds(i * 4 + j, 1)].rearrange("a p n -> (a p) n"), KT * P)
            channel_mixer(1)

        @block.tensor
        def _(pe):
            t = Tally(pe)

            def first_use(ins):
                ins.then_inc(S["w_used"], 1)

            def unit(chunks, xs, cols=P, rows=P, ws=None):
                s, mm, rd = t.unit()
                pe.wait_ge(S[f"read{s}"], t.val(f"read{s}", -1))
                n, total = 0, sum(chunks)
                for count in chunks:
                    w = t.n.get("chunk", 0)
                    slot = w % SLOTS
                    t.up("chunk")
                    t.up("w_used")
                    pe.wait_ge(S[f"w{slot}"], t.up(f"w{slot}", 16))
                    for j in range(count):
                        for c in range(NCH):
                            ins = nc.tensor.matmul(
                                ps[0:cols, NCH * s + c, 0:CH], W[0:rows, slot, j * cols:(j + 1) * cols],
                                xs[n][0:rows, c * CH:(c + 1) * CH], start=(n == 0), stop=(n == total - 1))
                            if j == 0 and c == 0:
                                first_use(ins)
                        n += 1
                ins.then_inc(S["mm_done"], 1)

            def split_unit(xh, xl, cols=P):
                s, mm, rd = t.unit()
                pe.wait_ge(S[f"read{s}"], t.val(f"read{s}", -1))
                m = t.n.get("wl_ready", 0)
                slot, _ = t.chunk()
                t.up("w_used")
                pe.wait_ge(S["wl_ready"], t.up("wl_ready"))
                wh, wl = wh_of(m), Wr[:, slot, 0:KT * P]
                for j in range(KT):
                    for n, (w, x) in enumerate(((wh, xh), (wh, xl), (wl, xh))):
                        for c in range(NCH):
                            ins = nc.tensor.matmul(ps[0:cols, NCH * s + c, 0:CH], w[:, j * cols:(j + 1) * cols],
                                                   x[j][:, c * CH:(c + 1) * CH],
                                                   start=(j == 0 and n == 0), stop=(j == KT - 1 and n == 2))
                            if j == 0 and n == 0 and c == 0:
                                first_use(ins)
                ins.then_inc(S["mm_done"], 1)

            def sums(lhs, x):
                s, mm, rd = t.unit()
                if t.some(f"read{s}", -1):
                    pe.wait_ge(S[f"read{s}"], t.val(f"read{s}", -1))
                for c in range(NCH):
                    ins = nc.tensor.matmul(ps[:, NCH * s + c, 0:CH], lhs, x[:, c * CH:(c + 1) * CH],
                                           start=True, stop=True)
                ins.then_inc(S["mm_done"], 1)

            def norm():
                pe.wait_ge(S["sq_used"], t.up("sq_used", KT))
                sums(k("ones"), TM[:, 2, :])

            def wait_normed():
                pe.wait_ge(S["normed"], t.up("normed", KT))

            xs = [A[:, j, :] for j in range(KT)]

            def dense8(count):
                with t.loop(count // 4, chunk=4, w_used=4, mm_done=4, read0=2, read1=2, w0=16, w1=16, w2=16, w3=16):
                    for j in range(4):
                        unit([KT], xs)

            pe.wait_ge(S["setup"], 96)
            norm()
            wait_normed()
            pe.wait_ge(S["wv_in"], 16)
            wv = Bf[:, 8 * T:8 * T + KT * 512].rearrange("p (k n) -> p k n", k=KT)
            for tt in range(9):
                s, mm, rd = t.unit()
                if t.some(f"read{s}", -1):
                    pe.wait_ge(S[f"read{s}"], t.val(f"read{s}", -1))
                c0, n = (P0 + P * tt, P) if tt < 8 else (S0, DEC)
                for j in range(KT):
                    ins = nc.tensor.matmul(ps[0:n, NCH * s, :], A[:, j, c0:c0 + n], wv[:, j, :],
                                           start=(j == 0), stop=(j == KT - 1))
                ins.then_inc(S["mm_done"], 1)
            dense8(8)
            unit([KT], xs, cols=HF)
            for j in range(3 * NA):
                unit([KT], xs)

            def s_set(u):
                return ps[:, 2 * (u % 2):2 * (u % 2) + 2, :]

            PTp = [ps[:, 4 + b, :] for b in range(2)]
            Qs = Af[:, 0:T]
            Ks = Af[:, T:2 * T]
            Vs = Af[:, 2 * T:2 * T + 1024].rearrange("p (b n) -> p b n", b=8)
            PTs = Tf[:, 0:2048].rearrange("p (u n) -> p u n", u=2)

            def scores(u):
                qb, h = u // 2, u % 2
                r = slice(C * h, C * h + C)
                nk = P * (qb + 1)
                if u >= 2:
                    pe.wait_ge(S["s_read"], t.val("s_done", -1))
                st = s_set(u)
                for n0 in range(0, nk, 512):
                    n1 = min(nk, n0 + 512)
                    nc.tensor.matmul(st[:, n0 // 512, 0:n1 - n0], Qs[r, P0 + P * qb:P0 + P * qb + P],
                                     Ks[r, P0 + n0:P0 + n1], start=True, stop=True)
                o = (nk - P) % 512
                nc.tensor.matmul(st[:, (nk - P) // 512, o:o + P], identb[:, :], causb[:, 0:P],
                                 start=False, stop=True, skip_group_check=True).then_inc(S["s_done"], 1)
                t.up("s_done")

            def values(u):
                qb, h = u // 2, u % 2
                pe.wait_ge(S["e_ready"], t.up("e_ready"))
                E = Af[:, 2 * T + 1024 + 2048 + 1024 * (u % 2):][:, 0:1024]
                for b in range(qb + 1):
                    ins = nc.tensor.transpose(PTp[b // 4][:, P * (b % 4):P * (b % 4) + P], E[:, P * b:P * b + P],
                                              k("ident"))
                ins.then_inc(S["pt_done"], 1)
                pe.wait_ge(S["pt_read"], t.up("pt_done"))
                if u >= 2:
                    pe.wait_ge(S["o_read"], t.val("o_done", -1))
                if h == 0 and qb:
                    pe.wait_ge(S["ot_read"], t.val("ot_done"))
                for b in range(qb + 1):
                    ins = nc.tensor.matmul(ps[:, 6 + h, 0:C], PTs[:, 0, P * b:P * b + P],
                                           Vs[:, b, C * h:C * h + C], start=(b == 0), stop=(b == qb))
                ins.then_inc(S["o_done"], 1)
                t.up("o_done")

            def turn(n, qb):
                pe.wait_ge(S["o_read"], t.val("o_done"))
                OT = Tf[:, 2048:2048 + P]
                ins = nc.tensor.transpose(ps[0:n, 6, 0:P], OT[:, 0:n], k("ident"))
                ins.then_inc(S["ot_done"], 1)
                t.up("ot_done")

            pe.wait_ge(S["read0"], t.val("read0"))
            pe.wait_ge(S["read1"], t.val("read1"))
            with t.loop(4, s_done=16, e_ready=16, pt_done=16, o_done=16, ot_done=8, staged=1):
                pe.wait_ge(S["staged"], t.up("staged"))
                scores(0)
                for u in range(16):
                    if u < 15:
                        scores(u + 1)
                    values(u)
                    if u % 2:
                        turn(P, u // 2)

            t.up("kv_in", 128)
            Kc = Af[:, 0:PAST]
            Vc = Af[:, PAST:2 * PAST].rearrange("p (b n) -> p b n", b=16)
            Es = Af[:, 2 * PAST:2 * PAST + NALL]
            sm = Tf[:, 2304:]
            Qn, Kn, Vn, OTs = sm[:, 0:P], sm[:, P:P + C], sm[:, P + C:2 * P + C], sm[:, 2 * P + C:3 * P]
            PTl = Tf[:, 0:17 * P]
            with t.loop(4, s_done=3, e_ready=1, pt_done=3, o_done=1, ot_done=1, staged=1, kv_in=64):
                pe.wait_ge(S["staged"], t.up("staged"))
                pe.wait_ge(S["kv_in"], t.up("kv_in", 64))
                for piece in range(3):
                    pe.wait_ge(S["s_read"], t.val("s_done", -1))
                    st = ps[:, 2 * (piece % 2):2 * (piece % 2) + 2, :]
                    if piece < 2:
                        for n in range(2):
                            ins = nc.tensor.matmul(st[:, n, :], Qn, Kc[:, 1024 * piece + 512 * n:1024 * piece + 512 * n + 512],
                                                   start=True, stop=True)
                    else:
                        nc.tensor.matmul(st[:, 0, 0:C], Qn, Kn, start=True, stop=False)
                        ins = nc.tensor.matmul(st[:, 0, 0:C], identb[:, :], causb[:, P:P + C], start=False, stop=True)
                    ins.then_inc(S["s_done"], 1)
                    t.up("s_done")
                pe.wait_ge(S["e_ready"], t.up("e_ready"))
                for part in range(3):
                    pe.wait_ge(S["pt_read"], t.val("pt_done"))
                    pe.sem_inc(S["held"], 1)
                    for b in range(8 * part, min(17, 8 * part + 8)):
                        n = P if b < 16 else C
                        ins = nc.tensor.transpose(PTp[b % 8 // 4][0:n, P * (b % 4):P * (b % 4) + P],
                                                  Es[:, P * b:P * b + n], k("ident"))
                    ins.then_inc(S["pt_done"], 1)
                    t.up("pt_done")
                pe.wait_ge(S["pt_read"], t.val("pt_done"))
                pe.wait_ge(S["o_read"], t.val("o_done"))
                for h in range(2):
                    r = slice(C * h, C * h + C)
                    for b in range(17):
                        n = P if b < 16 else C
                        vb = Vc[:, b, C * h:C * h + C] if b < 16 else Vn[0:C, C * h:C * h + C]
                        ins = nc.tensor.matmul(ps[r, 6, 0:C], PTl[0:n, P * b + C * h:P * b + C * h + C], vb,
                                               start=(b == 0), stop=(b == 16), skip_group_check=True)
                ins.then_inc(S["o_done"], 1)
                t.up("o_done")
                pe.wait_ge(S["o_read"], t.val("o_done"))
                pe.wait_ge(S["ot_read"], t.val("ot_done"))
                pe.sem_inc(S["held"], 1)
                nc.tensor.transpose(ps[0:C, 7, 0:P], OTs, k("ident")).then_inc(S["ot_done"], 1)
                t.up("ot_done")
            pe.wait_ge(S["ot_read"], t.val("ot_done"))

            xs = [B[:, 8 + j, :] for j in range(KT)]
            dense8(KT)

            def channel_mixer():
                norm()
                t.up("normed", KT)
                norm()
                t.up("normed", KT)
                pe.wait_ge(S["xl_ready"], t.up("xl_ready", KT))
                xl, xh = ([x[:, j, :] for j in range(KT)] for x in (Ar, Hr))
                with t.loop(2 * NF // 4, chunk=4, w_used=4, wl_ready=4, mm_done=4, read0=2, read1=2,
                            w0=16, w1=16, w2=16, w3=16):
                    for j in range(4):
                        split_unit(xh, xl)
                pe.wait_ge(S["read0"], t.val("read0"))
                pe.wait_ge(S["read1"], t.val("read1"))
                mid = [B[:, j, :] for j in range(NF)]
                with t.loop(KT // 2, chunk=4, w_used=4, mm_done=2, read0=1, read1=1, w0=16, w1=16, w2=16, w3=16):
                    for j in range(2):
                        unit([HALF, HALF], mid)
                norm()
                t.up("normed", KT)
                norm()
                t.up("normed", KT)
                pe.wait_ge(S["xl_ready"], t.up("xl_ready", KT))
                pe.wait_ge(S["p_in"], t.up("p_in", 16))
                xh = [Br[:, NP_ + j, :] for j in range(KT)]
                with t.loop(KT // 2, chunk=4, w_used=4, wl_ready=2, mm_done=4, read0=2, read1=2,
                            w0=16, w1=16, w2=16, w3=16):
                    for j in range(2):
                        split_unit(xh, xl)
                        unit([NP_], [B[:, 0, :], B[:, 1, :]])

            channel_mixer()
            if stop < 2:
                return

            norm()
            t.up("normed", KT)
            X = [[B[:, 8 * b + j, :] for j in range(KT)] for b in range(2)]

            def lora(b, first, rows, out):
                pe.wait_ge(S["xn_ready"], t.up("xn_ready", KT))
                unit([KT], X[b], cols=rows)
                s = (t.n["mm_done"] - 1) % 2
                pe.wait_ge(S[f"read{s}"], t.val(f"read{s}"))
                w = t.n.get("chunk", 0)
                slot = w % SLOTS
                t.up("chunk")
                t.up("w_used")
                pe.wait_ge(S[f"w{slot}"], t.up(f"w{slot}", 16))
                for m in range(KT):
                    s, mm, rd = t.unit()
                    pe.wait_ge(S[f"read{s}"], t.val(f"read{s}", -1))
                    for c in range(NCH):
                        ins = nc.tensor.matmul(ps[:, NCH * s + c, 0:CH], W[0:rows, slot, m * P:(m + 1) * P],
                                               out[0:rows, c * CH:(c + 1) * CH], start=True, stop=True)
                        if m == 0 and c == 0:
                            first_use(ins)
                    ins.then_inc(S["mm_done"], 1)

            lora(0, 0, C, B[:, 16, :])
            lora(1, 0, C, B[:, 17, :])
            lora(0, 0, P, B[:, 16, :])
            for n in range(2):
                pe.wait_ge(S["xn_ready"], t.up("xn_ready", KT))
                xs = X[(n + 1) % 2]
                dense8(KT)
            pe.wait_ge(S["xn_ready"], t.up("xn_ready", KT))
            xs = X[1]
            with t.loop(2, mm_done=12, read0=6, read1=6, key_sq=4, rk_ready=4, chunk=4, w_used=4, w0=16, w1=16, w2=16, w3=16):
                for u in range(4):
                    pe.wait_ge(S["key_sq"], t.up("key_sq"))
                    sums(k("pair"), TM[:, 1, :])
                    unit([KT], xs)
                    pe.wait_ge(S["rk_ready"], t.up("rk_ready"))
                    sums(k("pair"), TM[:, 2, :])

            for s in range(2):
                pe.wait_ge(S[f"read{s}"], t.val(f"read{s}"))

            def heads(g):
                return ((4 * g + a, a, h, slice(C * h, C * h + C)) for a in range(4) for h in range(2))

            def gram(u, g):
                ZB, ZA, ZV = Z[u]
                for p, a, h, r in heads(g):
                    ins = nc.tensor.matmul(ps[:, 4 + 2 * g + h, P * a:P * a + P],
                                           ZB[r, p, C * h:C * h + P], ZA[r, p, C * h:C * h + P],
                                           start=True, stop=True)
                ins.then_inc(S["g_done"], 1)

            def token_major(u, g):
                ZB, ZA, ZV = Z[u]
                pe.wait_ge(S["g_ready"], t.up("g_ready"))
                pe.sem_inc(S["held"], 1)
                for p, a, h, r in heads(g):
                    for j, z in enumerate((ZB, ZV)):
                        o = P * a + C * j
                        ins = nc.tensor.transpose(ps[:, 4 + 2 * g + h, o:o + C],
                                                  z[r, p, C * h:C * h + P], k("ident")[r, r])
                ins.then_inc(S["tok_done"], 1)

            def turn_n(u):
                for g in range(2):
                    pe.wait_ge(S["tok_read"], t.up("tok_read", 2))
                    pe.sem_inc(S["held"], 1)
                    for p, a, h, r in heads(g):
                        if h:
                            ins = nc.tensor.transpose(ps[:, 4 + 2 * g, P * a:P * a + P], Gs[u][:, p, C:C + P],
                                                      k("ident"))
                    ins.then_inc(S["n_done"], 1)

            def chunk(u, more=True):
                ZB, ZA, ZV = Z[u]
                G, M, bk, uv = Gs[u], Ms[u], BK[u], UV[u]
                for l in range(NL):
                    for g in range(2):
                        pe.wait_ge(S["m0_ready" if l == 0 else "m_ready"], t.up("m0_ready" if l == 0 else "m_ready"))
                        if l == 1:
                            pe.wait_ge(S["a_ready"], t.up("a_ready"))
                        pe.sem_inc(S["held"], 1)
                        for p, a, h, r in heads(g):
                            if h:
                                ins = nc.tensor.transpose(ps[:, 2 * g + 1, P * a:P * a + P], M[:, p, :], k("ident"))
                        ins.then_inc(S["mt_done"], 1)
                        if l == 0:
                            pe.wait_ge(S["n_ready"], t.up("n_ready"))
                            pe.sem_inc(S["held"], 1)
                        for p, a, h, r in heads(g):
                            ins = nc.tensor.matmul(ps[r, 2 * g, C * a:C * a + C], AB[u][r, p, :], M[r, p, r],
                                                   start=True, stop=True)
                        ins.then_inc(S["y_done"], 1)
                    for g in range(2):
                        pe.wait_ge(S["mt_ready"], t.up("mt_ready"))
                        pe.wait_ge(S["y_ready"], t.up("y_ready"))
                        pe.sem_inc(S["held"], 1)
                        for p, a, h, r in heads(g):
                            ins = nc.tensor.matmul(ps[r, 2 * g, 256 + C * a:256 + C * a + C], MT[r, p, :], Y[r, p, :],
                                                   start=True, stop=True)
                        ins.then_inc(S["z_done"], 1)
                    if l == 0:
                        for g in range(2):
                            for p, a, h, r in heads(g):
                                o = 256 + C * a
                                nc.tensor.matmul(ps[r, 2 * g + 1, o:o + C], G[:, p, P * h + C - C * h:P * h + P - C * h],
                                                 uv[:, p, r], start=True, stop=False, skip_group_check=True)
                                ins = nc.tensor.matmul(ps[r, 2 * g + 1, o:o + C], ZA[:, p, C:2 * C],
                                                       ST[:, p, r], start=False, stop=True, skip_group_check=True)
                            ins.then_inc(S["a_done"], 1)
                    elif more and l < 3:
                        if l == 1:
                            pe.wait_ge(S["z_dup"], t.up("z_dup"))
                            pe.sem_inc(S["held"], 1)
                        gram(1 - u, l - 1)
                    elif more:
                        token_major(1 - u, l - 3)
                for g in range(2):
                    pe.wait_ge(S["m_ready"], t.up("m_ready"))
                    pe.sem_inc(S["held"], 1)
                    for p, a, h, r in heads(g):
                        o = 256 + C * a
                        ins = nc.tensor.matmul(ps[r, 2 * g + 1, o:o + C], M[r, p, r], P1[r, p, :],
                                               start=True, stop=True)
                    ins.then_inc(S["u_done"], 1)
                for g in range(2):
                    pe.wait_ge(S["u_ready"], t.up("u_ready"))
                    for p, a, h, r in heads(g):
                        o = C * a
                        nc.tensor.matmul(ps[r, 2 * g, o:o + C], uv[:, p, r], G[:, p, P * h + C * h:P * h + C * h + C],
                                         start=True, stop=False, skip_group_check=True)
                        ins = nc.tensor.matmul(ps[r, 2 * g, o:o + C], ST[:, p, r], ZA[:, p, 0:C],
                                               start=False, stop=True, skip_group_check=True)
                    ins.then_inc(S["oo_done"], 1)
                    for p, a, h, r in heads(g):
                        o = C * a
                        ins = nc.tensor.matmul(ps[r, 2 * g + 1, o:o + C], bk[:, p, r], uv[:, p, r],
                                               start=True, stop=True, skip_group_check=True)
                    ins.then_inc(S["st_done"], 1)
                if more:
                    turn_n(1 - u)
                pe.wait_ge(S["c_in"], t.up("c_in", 4))

            per = dict(z_dup=2, tok_read=8, n_ready=4, m0_ready=4, m_ready=4 * NL, mt_ready=4 * NL, y_ready=4 * NL,
                       a_ready=4, u_ready=4, c_in=8, g_ready=4)
            pe.wait_ge(S["st_ready"], 1)
            t.up("c_in", 4)
            pe.wait_ge(S["z_dup"], t.up("z_dup"))
            for g in range(2):
                gram(0, g)
            for g in range(2):
                token_major(0, g)
            turn_n(0)
            with t.loop(NCHUNK // 2, **per):
                chunk(0)
                chunk(1)
            pe.wait_ge(S["state_in"], 32)
            chunk(0, more=False)

            def mean(i):
                sums(k("pair"), A[:, i, :])

            mean(0)
            for i in range(NPAIR):
                if i + 1 < NPAIR:
                    mean(i + 1)
                pe.wait_ge(S["dev_sq"], t.up("dev_sq"))
                sums(k("pair"), TM[:, 1, :])
            pe.wait_ge(S["gn_ready"], NPAIR)
            xs = [B[:, 8 + j, :] for j in range(KT)]
            dense8(KT)
            channel_mixer()

        @block.scalar
        def _(act):
            t = Tally(act)

            def square(src, needs=None):
                j = t.n.get("sq_ready", 0) % 2
                if t.some("sq_ready", -1):
                    act.wait_ge(S["sq_used"], t.val("sq_ready", -1))
                nc.scalar.activation(TM[:, j, :], src, ACT.Square).then_inc(S["sq_ready"], 1)
                t.up("sq_ready")

            def root(scale=1.0 / D, e=0):
                s, mm, rd = t.unit()
                act.wait_ge(S["mm_done"], mm)
                nc.scalar.activation(c3(TM[:, 3, :]), pset(s), ACT.Sqrt, scale=scale,
                                     bias=eps[:, e:e + 1]).then_inc(S[f"read{s}"], 1)

            def copy_unit(dst, cols=P, func=ACT.Copy, **kw):
                s, mm, rd = t.unit()
                act.wait_ge(S["mm_done"], mm)
                nc.scalar.activation(c3(dst)[0:cols], pset(s)[0:cols], func, **kw).then_inc(S[f"read{s}"], 1)
                return s, rd

            act.wait_ge(S["setup"], 96 + 4)
            act.wait_ge(S["x_in"], 16 * KT)
            for j in range(KT):
                square(H[:, j, :])
            root()
            Vt = Bf[:, 16 * T:16 * T + 9 * 512].rearrange("p (b n) -> p b n", b=9)
            for tt in range(9):
                s, mm, rd = t.unit()
                act.wait_ge(S["mm_done"], mm)
                n = P if tt < 8 else DEC
                nc.scalar.activation(Vt[0:n, tt, :], ps[0:n, NCH * s, :], ACT.Copy).then_inc(S[f"read{s}"], 1)
            with t.loop(2, mm_done=4, read0=2, read1=2) as i:
                for j in range(4):
                    copy_unit(B[:, bass.ds(i * 4 + j, 1), :].rearrange("p a n -> p (a n)"))
            t.skip(1)
            for c in range(NA):
                if t.some("ax_ready"):
                    act.wait_ge(S["tm_free"], t.val("ax_ready"))
                s, mm, rd = t.unit()
                act.wait_ge(S["mm_done"], mm)
                nc.scalar.activation(c3(TM[:, 0, :]), pset(s), ACT.Copy).then_inc(S[f"read{s}"], 1)
                t.up("ax_ready")
                t.skip(2)

            z, e = B[0:HF, 21, :], Af[0:HF, 0:T]
            act.wait_ge(S["dve_p"], t.up("dve_p"))
            act.wait_ge(S["mm_done"], t.val("mm_done"))
            nc.scalar.activation(e, z, ACT.Abs).then_inc(S["act_step"], 1)
            act.wait_ge(S["act_step"], t.up("act_step"))
            nc.scalar.activation(e, e, ACT.Exp, scale=-1.0).then_inc(S["act_step"], 1)
            act.wait_ge(S["act_step"], t.up("act_step"))
            nc.scalar.activation(e, e, ACT.Ln, bias=1.0).then_inc(S["act_p"], 1)
            t.up("act_p")

            E0 = 2 * T + 1024 + 2048
            PTs = Tf[:, 0:2048].rearrange("p (u n) -> p u n", u=2)
            PTp = ps[:, 4:6, :].rearrange("p b n -> p (b n)")
            PTl = Tf[:, 0:17 * P]
            OT = Tf[:, 2048:2048 + P]
            Vpair = Bf[:, 16 * T:16 * T + 9 * 512].rearrange("p (b h n) -> p b h n", b=9, h=4)

            def exp(u, n, E):
                act.wait_ge(S["p_ready"], t.up("p_ready"))
                nc.scalar.activation(E, E, ACT.Exp, scale=0.125, bias=mx[:, 2 * u + 1:2 * u + 2],
                                     accum_out=mx[:, 4 + u:5 + u]).then_inc(S["e_ready"], 1)
                t.up("e_ready")

            def turned(u, n):
                act.wait_ge(S["pt_done"], t.up("pt_done"))
                if u:
                    act.wait_ge(S["o_done"], t.val("o_done"))
                nc.scalar.activation(PTs[:, 0, 0:n], PTp[:, 0:n], ACT.Copy).then_inc(S["pt_read"], 1)
                t.up("pt_read")

            with t.loop(4, p_ready=16, e_ready=16, pt_done=16, pt_read=16, o_done=16, ot_done=8, ot_read=8) as i:
                exp(0, P, Af[:, E0:E0 + P])
                for u in range(16):
                    if u < 15:
                        n1 = P * ((u + 1) // 2 + 1)
                        exp((u + 1) % 2, n1, Af[:, E0 + 1024 * ((u + 1) % 2):][:, 0:n1])
                    turned(u, P * (u // 2 + 1))
                    t.up("o_done")
                    if u % 2:
                        act.wait_ge(S["ot_done"], t.up("ot_done"))
                        qb = u // 2
                        nc.scalar.activation(B[:, bass.ds(i + 12, 1), P0 + P * qb:P0 + P * qb + P].rearrange("p a n -> p (a n)"),
                                             ps[:, 6, 0:P], ACT.Copy).then_inc(S["ot_read"], 1)
                        t.up("ot_read")
            Es = Af[:, 2 * PAST:2 * PAST + NALL]
            with t.loop(4, p_ready=1, e_ready=1, pt_done=3, pt_read=3, o_done=1, ot_done=1, ot_read=1) as i:
                exp(0, NALL, Es)
                for part in range(3):
                    act.wait_ge(S["pt_done"], t.up("pt_done"))
                    act.wait_ge(S["o_done"], t.val("o_done"))
                    if part < 2:
                        nc.scalar.activation(PTl[:, 1024 * part:1024 * part + 1024], PTp[:, :],
                                             ACT.Copy).then_inc(S["pt_read"], 1)
                    else:
                        nc.scalar.activation(PTl[0:C, 2048:2048 + P], PTp[0:C, 0:P],
                                             ACT.Copy).then_inc(S["pt_read"], 1)
                    t.up("pt_read")
                t.up("o_done")
                act.wait_ge(S["ot_done"], t.up("ot_done"))
                for h in range(2):
                    ins = nc.scalar.activation(
                        B[C * h:C * h + C, bass.ds(i + 12, 1), S0:T].rearrange("p a n -> p (a n)"),
                        ps[0:C, 7, C * h:C * h + C], ACT.Copy)
                ins.then_inc(S["ot_read"], 1)
                t.up("ot_read")

            def output_tiles(count):
                for j in range(count):
                    s, mm, rd = t.unit()
                    act.wait_ge(S["mm_done"], mm)
                    nc.scalar.activation(c3(A[:, j, :]), pset(s), ACT.Copy).then_inc(S[f"read{s}"], 1)
                    act.wait_ge(S[f"read{s}"], rd)
                    square(A[:, j, :])

            def post_and_pre():
                root()
                for j in range(KT):
                    act.wait_ge(S["h_ready"], t.up("h_ready"))
                    square(H[:, j, :])
                root()

            def upper(dst):
                for j in range(KT):
                    act.wait_ge(S["normed"], t.up("normed"))
                    nc.scalar.activation(dst[j], A[:, j, :], ACT.Copy).then_inc(S["xh_ready"], 1)

            def channel_mixer(l):
                output_tiles(KT)
                post_and_pre()
                t.n["normed"] = NORMED[l]
                act.wait_ge(S["h_out"], KT * 16 * (l + 1))
                upper([Hr[:, j, :] for j in range(KT)])
                with t.loop(NF // 2, mm_done=4, read0=2, read1=2) as i:
                    for j in range(2):
                        s, mm, rd = t.unit()
                        act.wait_ge(S["mm_done"], mm)
                        act.wait_ge(S[f"read{1 - s}"], t.val(f"read{1 - s}", -1))
                        nc.scalar.activation(c3(TM[:, j, :]), pset(s), ACT.Silu).then_inc(S[f"read{s}"], 1)
                        t.skip(1)
                output_tiles(KT)
                post_and_pre()
                t.n["normed"] = NORMED[l] + 2 * KT
                upper([Br[:, NP_ + j, :] for j in range(KT)])
                with t.loop(KT // 2, mm_done=4, read0=2, read1=2, h_ready=2) as i:
                    for j in range(2):
                        s, mm, rd = t.unit()
                        act.wait_ge(S["mm_done"], mm)
                        act.wait_ge(S["h_ready"], t.val("h_ready", -1))
                        nc.scalar.activation(c3(TM[:, j, :]), pset(s), ACT.Sigmoid).then_inc(S[f"read{s}"], 1)
                        t.up("h_ready")
                        t.skip(1)

            channel_mixer(0)
            if stop < 2:
                return

            act.wait_ge(S["h_ready"], t.val("h_ready"))
            for j in range(KT):
                square(H[:, j, :])
            root()
            act.wait_ge(S["dve_p"], t.up("dve_p"))

            def mix(n):
                for kt in range(KT):
                    j = t.n.get("xn_tmp", 0) % 2
                    if t.some("xn_tmp", -1):
                        act.wait_ge(S["xn_ready"], t.val("xn_tmp", -1))
                    nc.scalar.activation(TM[:, j, :], A[:, kt, :], ACT.Copy,
                                         scale=mub[:, n, kt:kt + 1]).then_inc(S["xn_tmp"], 1)
                    t.up("xn_tmp")

            def stage_first(func, bias):
                for n in range(KT):
                    j = n % 4
                    s, mm, rd = t.unit()
                    act.wait_ge(S["mm_done"], mm)
                    if n >= 4:
                        t.up(f"xs{j}", 16)
                        act.wait_ge(S[f"xs{j}"], t.val(f"xs{j}"))
                    nc.scalar.activation(c3(B[:, 18 + j, :]), pset(s), func,
                                         bias=v1(bias, n)).then_inc(S[f"read{s}"], 1)

            def stage(func=ACT.Copy, bias=None):
                with t.loop(2, mm_done=4, read0=2, read1=2, xs0=16, xs1=16, xs2=16, xs3=16) as i:
                    for j in range(4):
                        s, mm, rd = t.unit()
                        act.wait_ge(S["mm_done"], mm)
                        act.wait_ge(S[f"xs{j}"], t.val(f"xs{j}"))
                        t.up(f"xs{j}", 16)
                        kw = dict(bias=vec[:, V[bias], bass.ds(i * 4 + j, 1)]) if bias else {}
                        nc.scalar.activation(c3(B[:, 18 + j, :]), pset(s), func, **kw).then_inc(S[f"read{s}"], 1)

            def hidden(slot, rows, func):
                s, mm, rd = t.unit()
                act.wait_ge(S["mm_done"], mm)
                nc.scalar.activation(c3(B[:, slot, :])[0:rows], pset(s)[0:rows], func).then_inc(S[f"read{s}"], 1)

            mix(1)
            hidden(16, C, ACT.Tanh)
            mix(4)
            stage_first(ACT.Sigmoid, "w0")
            for j in range(4):
                t.up(f"xs{j}", 16)
            hidden(17, C, ACT.Copy)
            mix(5)
            stage(ACT.Sigmoid, bias="a0")
            hidden(16, P, ACT.Sigmoid)
            mix(0)
            stage()
            mix(2)
            stage()
            mix(3)
            stage()

            act.wait_ge(S["xn_ready"], t.val("xn_tmp"))
            with t.loop(2, l_in0=2 * 64, l_in1=2 * 64, act_p=16, dve_p=8, mm_done=12, read0=6, read1=6, key_scaled=4,
                        key_sq=4, rn_used=4, xs0=16, xs1=16, xs2=16, xs3=16) as i:
                for u in range(4):
                    pair, key, L = i * 4 + u, key2[u % 2], Lb[u % 2]
                    act.wait_ge(S[f"l_in{u % 2}"], t.up(f"l_in{u % 2}", 64))
                    nc.scalar.activation(key, L["k"], ACT.Copy,
                                         scale=vec[:, V["kk"], bass.ds(pair, 1)]).then_inc(S["key_scaled"], 1)
                    act.wait_ge(S["key_scaled"], t.up("key_scaled"))
                    nc.scalar.activation(TM[:, 1, :], key, ACT.Square).then_inc(S["key_sq"], 1)
                    t.up("key_sq")
                    nc.scalar.activation(L["w"], L["w"], ACT.Copy, scale=-DECAY).then_inc(S["act_p"], 1)
                    t.up("act_p")
                    s, mm, rd = t.unit()
                    act.wait_ge(S["mm_done"], mm)
                    act.wait_ge(S["rn_used"], t.up("rn_used"))
                    nc.scalar.activation(c3(TM[:, 3, :]), pset(s), ACT.Sqrt).then_inc(S[f"read{s}"], 1)
                    act.wait_ge(S["dve_p"], t.up("dve_p"))
                    nc.scalar.activation(expL, cumL, ACT.Exp).then_inc(S["act_p"], 1)
                    nc.scalar.activation(expnL, cumL, ACT.Exp, scale=-1.0).then_inc(S["act_p"], 1)
                    act.wait_ge(S["act_p"], t.up("act_p"))
                    t.up("act_p")
                    for c0, n, o in ((P0, NCHUNK, 0), (S0, 1, NCHUNK)):
                        nc.scalar.activation(eLC[:, bass.ds(pair, 1), o:o + n].rearrange("p a n -> p (a n)"),
                                             expL[:, c0 + C - 1:c0 + C * n:C], ACT.Copy)
                    act.wait_ge(S["dve_p"], t.up("dve_p"))
                    nc.scalar.activation(L["w"], L["w"], ACT.Exp).then_inc(S["act_p"], 1)
                    t.up("act_p")
                    s, mm, rd = t.unit()
                    act.wait_ge(S["mm_done"], mm)
                    act.wait_ge(S[f"xs{u}"], t.val(f"xs{u}"))
                    t.up(f"xs{u}", 16)
                    nc.scalar.activation(c3(B[:, 18 + u, :]), pset(s), ACT.Copy).then_inc(S[f"read{s}"], 1)
                    s, mm, rd = t.unit()
                    act.wait_ge(S["mm_done"], mm)
                    nc.scalar.activation(c3(TM[:, 2, :]), pset(s), ACT.Copy).then_inc(S[f"read{s}"], 1)

            def onto_diagonals(dst, src, g):
                for h in range(2):
                    r = slice(C * h, C * h + C)
                    ins = nc.scalar.activation(dst[r, 4 * g:4 * g + 4, r], src[r].rearrange("p (a n) -> p a n", a=4),
                                               ACT.Copy)
                return ins

            def off_diagonals(dst, bank, g):
                for h in range(2):
                    r = slice(C * h, C * h + C)
                    ins = nc.scalar.activation(dst[r, 4 * g:4 * g + 4, :],
                                               ps[r, bank, :].rearrange("p (a n) -> p a n", a=4)[:, :, r], ACT.Copy)
                return ins

            def token_major(u, g):
                act.wait_ge(S["tok_done"], t.up("tok_done"))
                for h in range(2):
                    nc.scalar.activation(BKUV[u][:, 4 * g:4 * g + 4, :, C * h:C * h + C],
                                         ps[:, 4 + 2 * g + h, :].rearrange("p (a j n) -> p a j n", a=4, j=2),
                                         ACT.Copy).then_inc(S["tok_read"], 1)

            def turn_n(u):
                for g in range(2):
                    act.wait_ge(S["n_done"], t.up("n_done"))
                    off_diagonals(AB[u], 4 + 2 * g, g).then_inc(S["n_ready"], 1)

            def chunk(u, c0, more=True):
                for l in range(NL):
                    for g in range(2):
                        act.wait_ge(S["mt_done"], t.up("mt_done"))
                        off_diagonals(MT, 2 * g + 1, g).then_inc(S["mt_ready"], 1)
                    if l == 0:
                        for g in range(2):
                            act.wait_ge(S["a_done"], t.up("a_done"))
                            nc.scalar.activation(P1[:, 4 * g:4 * g + 4, :], four_of(2 * g + 1, 1),
                                                 ACT.Copy).then_inc(S["a_ready"], 1)
                    if l >= 3 and more:
                        token_major(1 - u, l - 3)
                for g in range(2):
                    act.wait_ge(S["u_done"], t.up("u_done"))
                    onto_diagonals(UV[u], ps[:, 2 * g + 1, 256:512], g).then_inc(S["u_ready"], 1)
                for g in range(2):
                    act.wait_ge(S["oo_done"], t.up("oo_done"))
                    dst = A[:, 4 * g:4 * g + 4, c0:c0 + C] if isinstance(c0, int) else A[:, 4 * g:4 * g + 4, bass.ds(c0, C)]
                    nc.scalar.activation(dst, four_of(2 * g, 0), ACT.Copy).then_inc(S["c_in"], 1)
                if more:
                    turn_n(1 - u)

            act.wait_ge(S["st_ready"], 1)
            for g in range(2):
                token_major(0, g)
            turn_n(0)
            with t.loop(NCHUNK // 2, tok_done=4, n_done=4, mt_done=4 * NL, a_done=4, u_done=4, oo_done=4) as i:
                chunk(0, i * (2 * C) + P0)
                chunk(1, i * (2 * C) + (P0 + C))
            chunk(0, S0, more=False)

            def mean(i):
                t.unit()

            mean(0)
            for i in range(NPAIR):
                if i + 1 < NPAIR:
                    mean(i + 1)
                if i == 0:
                    act.wait_ge(S["state_out"], 1)
                act.wait_ge(S["mean_in"], i + 1)
                if i:
                    act.wait_ge(S["mm_done"], mm)
                nc.scalar.activation(TM[:, 1, :], B[:, 6 + i % 2, :], ACT.Square).then_inc(S["dev_sq"], 1)
                s, mm, rd = t.unit()
                act.wait_ge(S["mm_done"], mm)
                if i:
                    act.wait_ge(S["gn_used"], i)
                nc.scalar.activation(c3(TM[:, 2, :]), pset(s), ACT.Sqrt, scale=1.0 / C,
                                     bias=eps[:, 1:2]).then_inc(S[f"read{s}"], 1)
            channel_mixer(1)

        @block.vector
        def _(dve):
            t = Tally(dve)

            def step(ins):
                ins.then_inc(S["dve_step"], 1)
                dve.wait_ge(S["dve_step"], t.up("dve_step"))

            def stt(out, in0, scalar, in1, op0, op1):
                return nc.vector.scalar_tensor_tensor(out=out, in0=in0, scalar=scalar, in1=in1, op0=op0, op1=op1)

            def sum_squares():
                for j in range(KT):
                    dve.wait_ge(S["sq_ready"], t.up("sq_ready"))
                    if j == 0:
                        ins = nc.vector.tensor_copy(TM[:, 2, :], TM[:, 0, :])
                    else:
                        dve.wait_ge(S["sq_used"], t.val("sq_used"))
                        ins = nc.vector.tensor_tensor(TM[:, 2, :], TM[:, 2, :], TM[:, j % 2, :], ALU.add)
                    ins.then_inc(S["sq_used"], 1)
                    t.up("sq_used")

            def rstd():
                s, mm, rd = t.unit()
                dve.wait_ge(S[f"read{s}"], rd)
                step(nc.vector.reciprocal(TM[:, 3, :], TM[:, 3, :]))

            def pre_norm(gain):
                sum_squares()
                rstd()
                for j in range(KT):
                    stt(A[:, j, :], H[:, j, :], v1(gain, j), TM[:, 3, :], ALU.mult, ALU.mult).then_inc(S["normed"], 1)
                    t.up("normed")

            def split_chunk(off=0, n=KT * P):
                m = t.n.get("wl_ready", 0)
                slot, landed = t.chunk()
                dve.wait_ge(S["mm_done"], t.val("mm_done", off))
                dve.wait_ge(S[f"w{slot}"], landed)
                w, wh = W[:, slot, 0:n], wh_of(m)[:, 0:n]
                step(nc.vector.tensor_copy(wh, w))
                nc.vector.tensor_tensor(Wr[:, slot, 0:n], w, wh, ALU.subtract).then_inc(S["wl_ready"], 1)
                t.up("wl_ready")

            def pre_norm_split(gain, xh):
                sum_squares()
                split_chunk(1)
                rstd()
                for j in range(KT + 1):
                    if j < KT:
                        stt(A[:, j, :], H[:, j, :], v1(gain, j), TM[:, 3, :], ALU.mult, ALU.mult).then_inc(S["normed"], 1)
                        t.up("normed")
                    if j:
                        dve.wait_ge(S["xh_ready"], t.up("xh_ready"))
                        nc.vector.tensor_tensor(Ar[:, j - 1, :], A[:, j - 1, :], xh[j - 1], ALU.subtract).then_inc(S["xl_ready"], 1)
                        t.up("xl_ready")

            def post_norm(gain):
                sum_squares()
                rstd()
                if t.some("h_in"):
                    dve.wait_ge(S["h_in"], t.val("h_in"))
                for j in range(KT):
                    stt(A[:, j, :], A[:, j, :], v1(gain, j), TM[:, 3, :], ALU.mult, ALU.mult).then_inc(S["normed"], 1)
                    dve.wait_ge(S["normed"], t.up("normed"))
                    nc.vector.tensor_tensor(H[:, j, :], H[:, j, :], A[:, j, :], ALU.add).then_inc(S["h_ready"], 1)
                    t.up("h_ready")

            dve.wait_ge(S["setup"], 96)
            nc.vector.memset(eps[:, 0:1], NORM_EPS)
            nc.vector.memset(eps[:, 1:2], GN_EPS).then_inc(S["setup"], 1)
            nc.vector.tensor_scalar(mub[:, :, :], vec[:, V["mu0"]:V["mu0"] + 6, :], -1.0, 1.0, ALU.mult,
                                    ALU.add).then_inc(S["setup"], 1)
            nc.vector.tensor_scalar(kab[:, :], vec[:, V["ka"], :], -1.0, 1.0, ALU.mult, ALU.add).then_inc(S["setup"], 1)
            nc.vector.tensor_copy(lvl[:, :, :].rearrange("p a n -> p (a n)"), TM[:, 3, 0:len(LEVELS) * C])
            nc.vector.tensor_copy(identb[:, :], k("ident"))
            nc.vector.tensor_copy(causb[:, :], cst[:, 3 * P:4 * P + C]).then_inc(S["setup"], 1)
            dve.wait_ge(S["x_in"], 16 * KT)
            dve.wait_ge(S["setup"], 100)
            pre_norm("pre0")
            t.skip(9 + 8)
            s, mm, rd = t.unit()
            dve.wait_ge(S["mm_done"], mm)
            nc.vector.tensor_scalar(c3(B[0:HF, 21, :]), pset(s)[0:HF], bf[:, 0:1], None,
                                    ALU.add).then_inc(S[f"read{s}"], 1)
            for c in range(NA):
                s, mm, rd = t.unit()
                dve.wait_ge(S[f"read{s}"], rd)
                s, mm, rd = t.unit()
                dve.wait_ge(S["mm_done"], mm)
                if c:
                    dve.wait_ge(S["conv_out"], 32 * c)
                nc.vector.tensor_tensor(c3(TM[:, 1, :]), pset(s), c3(TM[:, 0, :]), ALU.mult).then_inc(S[f"read{s}"], 1)
                dve.wait_ge(S[f"read{s}"], rd)
                nc.vector.memset(TM[:, 1, 0:PAD], 0.0).then_inc(S["dve_step"], 1)
                t.up("dve_step")
                nc.vector.tensor_copy(TM[:, 1, S0 - PAD:S0], convs[:, c, :]).then_inc(S["tm_free"], 1)
                dve.wait_ge(S["tm_free"], t.up("tm_free"))
                n = T - PAD
                step(nc.vector.tensor_scalar(TM[:, 2, PAD:T], TM[:, 1, 0:n], convw[:, 0, c:c + 1], None, ALU.mult))
                step(stt(TM[:, 2, PAD:T], TM[:, 1, 1:n + 1], convw[:, 1, c:c + 1], TM[:, 2, PAD:T], ALU.mult, ALU.add))
                step(stt(TM[:, 2, PAD:T], TM[:, 1, 2:T], convw[:, 2, c:c + 1], TM[:, 2, PAD:T], ALU.mult, ALU.add))
                step(nc.vector.memset(TM[:, 2, 0:PAD], 0.0))
                s, mm, rd = t.unit()
                dve.wait_ge(S["mm_done"], mm)
                nc.vector.tensor_tensor(c3(B[:, 8 + c, :]), pset(s), c3(TM[:, 2, :]), ALU.mult).then_inc(S[f"read{s}"], 1)
                dve.wait_ge(S[f"read{s}"], rd)
            z, e = B[0:HF, 21, :], Af[0:HF, 0:T]
            nc.vector.memset(B[:, 12:16, 0:PAD], 0.0)
            nc.vector.memset(B[:, 12:16, S0 - PAD:S0], 0.0).then_inc(S["dve_p"], 1)
            t.up("dve_p")
            dve.wait_ge(S["act_p"], t.up("act_p"))
            lf, zero = Af[0:HF, T:2 * T], Af[0:HF, 2 * T:2 * T + NALL]
            full, cum = Af[0:HF, 5000:5000 + NALL], Tf[0:HF, 0:NALL]
            cump = Tf[0:HF, NALL:NALL + SEQ]
            step(stt(lf, z, 0.0, e, ALU.min, ALU.subtract))
            step(nc.vector.memset(zero, 0.0))
            dve.wait_ge(S["cum_in"], t.up("cum_in", 16))
            step(nc.vector.tensor_copy(full[:, PAST:NALL], lf[:, S0:T]))
            nc.vector.tensor_tensor_scan(cump, lf[:, P0:P0 + SEQ], zero[:, 0:SEQ], 0.0, ALU.add, ALU.subtract)
            step(nc.vector.tensor_tensor_scan(cum, full, zero, 0.0, ALU.add, ALU.subtract))
            step(nc.vector.tensor_scalar(cump, cump, -8.0, None, ALU.mult))
            nc.vector.tensor_scalar(cum, cum, -8.0, None, ALU.mult).then_inc(S["cum_ready"], 1)

            E0 = 2 * T + 1024 + 2048
            OT = Tf[:, 2048:2048 + P]
            bc = Af[:, 2 * T + 1024:2 * T + 1024 + 2048].rearrange("p (h n) -> p h n", h=2)

            def out_scaled(u, dst, src, turned):
                dve.wait_ge(S["e_ready"], t.up("e_ready"))
                step(nc.vector.reciprocal(mx[:, 6 + u % 2:7 + u % 2], mx[:, 4 + u % 2:5 + u % 2]))
                dve.wait_ge(S["o_done"], t.up("o_done"))
                if turned:
                    dve.wait_ge(S["ot_done"], t.val("ot_done"))
                nc.vector.tensor_scalar(dst, src, mx[:, 6 + u % 2:7 + u % 2], None, ALU.mult).then_inc(S["o_read"], 1)
                t.up("o_read")

            sc = ps[:, :, :].rearrange("p b n -> p (b n)")
            with t.loop(4, s_done=16, s_read=16, p_ready=16, e_ready=16, o_done=16, o_read=16, ot_done=8, ptd=16,
                        dve_step=16, kv_in=32) as i:
                dve.wait_ge(S["kv_in"], t.up("kv_in", 32))
                for u in range(17):
                    if u < 16:
                        qb, h = u // 2, u % 2
                        n = P * (qb + 1)
                        if u >= 2:
                            dve.wait_ge(S["pt_done"], t.val("ptd", -1))
                        t.up("ptd")
                        dve.wait_ge(S["s_done"], t.up("s_done"))
                        dve.sem_inc(S["held"], 1)
                        E = Af[:, E0 + 1024 * h:E0 + 1024 * h + n]
                        nc.vector.tensor_tensor_reduce(out=E, in0=sc[:, 1024 * h:1024 * h + n], in1=bc[:, h, 0:n],
                                                       scale=1.0, scalar=-3e38, op0=ALU.add, op1=ALU.max,
                                                       accum_out=mx[:, 2 * h:2 * h + 1]).then_inc(S["s_read"], 1)
                        dve.wait_ge(S["s_read"], t.up("s_read"))
                        nc.vector.tensor_scalar(mx[:, 2 * h + 1:2 * h + 2], mx[:, 2 * h:2 * h + 1], -0.125, None,
                                                ALU.mult).then_inc(S["p_ready"], 1)
                        t.up("p_ready")
                    if u > 0:
                        w = u - 1
                        out_scaled(w, OT[:, C * (w % 2):C * (w % 2) + C], ps[:, 6 + w % 2, 0:C], w // 2)
                        if w % 2:
                            t.up("ot_done")
            Es = Af[:, 2 * PAST:2 * PAST + NALL]
            bcs = Af[:, 2 * PAST + NALL:2 * PAST + 2 * NALL]
            OTs = Tf[:, 2304 + 2 * P + C:2304 + 3 * P]
            with t.loop(4, s_done=3, s_read=3, p_ready=1, e_ready=1, o_done=1, o_read=1, ot_done=1, dve_step=1,
                        kv_in=64) as i:
                dve.wait_ge(S["kv_in"], t.up("kv_in", 64))
                for piece in range(3):
                    n = 1024 if piece < 2 else C
                    dve.wait_ge(S["s_done"], t.up("s_done"))
                    dve.sem_inc(S["held"], 1)
                    nc.vector.tensor_tensor_reduce(out=Es[:, 1024 * piece:1024 * piece + n],
                                                   in0=sc[:, 1024 * (piece % 2):1024 * (piece % 2) + n],
                                                   in1=bcs[:, 1024 * piece:1024 * piece + n], scale=1.0,
                                                   scalar=-3e38 if piece == 0 else mx[:, 0:1],
                                                   op0=ALU.add, op1=ALU.max, accum_out=mx[:, 0:1]).then_inc(S["s_read"], 1)
                    dve.wait_ge(S["s_read"], t.up("s_read"))
                nc.vector.tensor_scalar(mx[:, 1:2], mx[:, 0:1], -0.125, None, ALU.mult).then_inc(S["p_ready"], 1)
                t.up("p_ready")
                out_scaled(0, OTs, ps[:, 6, 0:C], 0)
                t.up("ot_done")
            t.skip(KT)

            def channel_mixer(l):
                post_norm(f"post{l}")
                t.n["chunk"] = t.n["w0"] = t.n["w1"] = t.n["w2"] = t.n["w3"] = 0
                t.skip_chunks(CHUNKS[l])
                pre_norm_split(f"fpre{l}", [Hr[:, j, :] for j in range(KT)])

                def mid_tiles(i, last):
                    for j in range(2):
                        split_chunk()
                        if not (last and j == 1):
                            split_chunk(1)
                        s, mm, rd = t.unit()
                        dve.wait_ge(S[f"read{s}"], rd)
                        s, mm, rd = t.unit()
                        dve.wait_ge(S["mm_done"], mm)
                        dst = B[:, NF - 2 + j, :] if last else B[:, bass.ds(i * 2 + j, 1), :].rearrange("p a n -> p (a n)")
                        nc.vector.tensor_tensor(c3(dst), pset(s), c3(TM[:, j, :]), ALU.mult).then_inc(S[f"read{s}"], 1)

                with t.loop(NF // 2 - 1, mm_done=4, read0=2, read1=2, chunk=4, w0=16, w1=16, w2=16, w3=16, wl_ready=4,
                            dve_step=4) as i:
                    mid_tiles(i, False)
                mid_tiles(None, True)
                t.skip(KT)
                t.skip_chunks(2 * KT)
                t.up("h_in", 16)
                post_norm(f"fpost{l}")
                pre_norm_split(f"ple{l}", [Br[:, NP_ + j, :] for j in range(KT)])
                t.skip_chunks(1)

                def ple_tiles(i, last):
                    for j in range(2):
                        if not (last and j == 1):
                            split_chunk()
                            t.skip_chunks(1)
                        s, mm, rd = t.unit()
                        dve.wait_ge(S[f"read{s}"], rd)
                        s, mm, rd = t.unit()
                        dve.wait_ge(S["mm_done"], mm)
                        nc.vector.tensor_tensor(c3(TM[:, j, :]), pset(s), c3(TM[:, j, :]), ALU.mult).then_inc(S[f"read{s}"], 1)
                        dve.wait_ge(S[f"read{s}"], rd)
                        h = H[:, KT - 2 + j, :] if last else H[:, bass.ds(i * 2 + j, 1), :].rearrange("p a n -> p (a n)")
                        nc.vector.tensor_tensor(h, h, TM[:, j, :], ALU.add).then_inc(S["h_ready"], 1)
                        t.up("h_ready")

                with t.loop(KT // 2 - 1, mm_done=4, read0=2, read1=2, h_ready=2, chunk=4, w0=16, w1=16, w2=16, w3=16,
                            wl_ready=2, dve_step=2) as i:
                    ple_tiles(i, False)
                ple_tiles(None, True)

            channel_mixer(0)
            if stop < 2:
                return

            pre_norm("pre1")
            dve.wait_ge(S["normed"], t.val("normed"))
            for g, c in enumerate((S0 - PAD - 1, T - 1)):
                ins = nc.vector.tensor_copy(last[:, g, :], A[:, :, c:c + 1].rearrange("p a n -> p (a n)"))
            ins.then_inc(S["shift_in"], 1)
            nc.vector.memset(A[:, :, P0 - 1:P0], 0.0)
            nc.vector.tensor_copy(A[:, :, S0 - 1:S0].rearrange("p a n -> p (a n)"), vec[:, V["shift"], :]).then_inc(S["dve_p"], 1)
            dve.wait_ge(S["dve_p"], t.up("dve_p"))
            mm0 = t.n["mm_done"]
            read_by = [mm0 + 1, mm0 + 10, mm0 + 19, mm0 + 35, mm0 + 43, mm0 + 51]
            nc.vector.memset(B[:, 0:16, 0:1], 0.0).then_inc(S["dve_step"], 1)
            dve.wait_ge(S["dve_step"], t.up("dve_step"))
            for order, n in enumerate((1, 4, 5, 0, 2, 3)):
                b = order % 2
                if order >= 2:
                    dve.wait_ge(S["mm_done"], read_by[order - 2])
                for kt in range(KT):
                    j = t.n.get("xn_tmp", 0) % 2
                    dve.wait_ge(S["xn_tmp"], t.up("xn_tmp"))
                    stt(B[:, 8 * b + kt, 1:T], A[:, kt, 0:T - 1], vec[:, V["mu0"] + n, kt:kt + 1], TM[:, j, 1:T],
                        ALU.mult, ALU.add).then_inc(S["xn_ready"], 1)
                    t.up("xn_ready")
            t.skip(43)

            dve.wait_ge(S["mm_done"], read_by[4])
            step(nc.vector.memset(reset, 1.0))
            nc.vector.memset(reset[:, P0:P0 + SEQ:C], 0.0)
            step(nc.vector.memset(reset[:, S0:S0 + 1], 0.0))

            def chunks(ap, n=P, o=0):
                v = ap.rearrange("p (c n) -> p c n", n=n)
                return v[:, 0:NCHUNK, o:o + C], v[:, NCHUNK, o:o + C]

            def tokens(ap):
                return ap[:, P0:P0 + SEQ].rearrange("p (c n) -> p c n", n=C), ap[:, S0:T]

            dve.sem_inc(S["rn_used"], 1)
            t.up("rn_used")
            with t.loop(2, l_in0=2 * 64, l_in1=2 * 64, act_p=16, dve_p=8, mm_done=12, read0=6, read1=6, dve_step=20,
                        key_scaled=4, rk_ready=4, rn_used=4, pair_stored=4, sum_stored=4, pair_done=4) as i:
                for u in range(4):
                    pair, key, L = i * 4 + u, key2[u % 2], Lb[u % 2]
                    dve.wait_ge(S[f"l_in{u % 2}"], t.up(f"l_in{u % 2}", 64))
                    step(nc.vector.tensor_scalar(tmpA, L["a"], vec[:, V["ka"], bass.ds(pair, 1)],
                                                 kab[:, bass.ds(pair, 1)], ALU.mult, ALU.add))
                    dve.wait_ge(S["key_scaled"], t.up("key_scaled"))
                    step(nc.vector.tensor_tensor(L["k"], tmpA, L["k"], ALU.mult))
                    dve.wait_ge(S["sum_stored"], t.up("sum_stored"))
                    stt(TM[:, 2, :], L["r"], vec[:, V["rk"], bass.ds(pair, 1)], L["k"], ALU.mult,
                        ALU.mult).then_inc(S["rk_ready"], 1)
                    t.up("rk_ready")
                    dve.wait_ge(S["act_p"], t.up("act_p"))
                    nc.vector.tensor_tensor_scan(cumL, reset, L["w"], 0.0, ALU.mult, ALU.add).then_inc(S["dve_p"], 1)
                    dve.wait_ge(S["dve_p"], t.up("dve_p"))
                    nc.vector.tensor_tensor(L["w"], cumL, L["w"], ALU.subtract).then_inc(S["dve_p"], 1)
                    t.up("dve_p")
                    s, mm, rd = t.unit()
                    dve.wait_ge(S[f"read{s}"], rd)
                    step(nc.vector.tensor_scalar(TM[:, 3, :], TM[:, 3, :], L2_EPS, None, ALU.max))
                    step(nc.vector.reciprocal(TM[:, 3, :], TM[:, 3, :]))
                    nc.vector.tensor_tensor(key, key, TM[:, 3, :], ALU.mult).then_inc(S["rn_used"], 1)
                    dve.wait_ge(S["rn_used"], t.up("rn_used"))
                    step(nc.vector.tensor_tensor(tmpA, key, L["a"], ALU.mult))
                    dve.wait_ge(S["pair_stored"], t.up("pair_stored"))
                    dve.wait_ge(S["act_p"], t.up("act_p"))
                    for dst, x, y in zip(chunks(ar_out, o=C), tokens(L["r"]), tokens(expL)):
                        nc.vector.tensor_tensor(dst, x, y, ALU.mult)
                    dve.wait_ge(S["act_p"], t.up("act_p"))
                    for dst, x, y in zip(chunks(bk_out), tokens(tmpA), tokens(expnL)):
                        nc.vector.tensor_tensor(dst, x, y, ALU.mult)
                    for dst, x, y in zip(chunks(bk_out, o=C), tokens(L["k"]), tokens(expnL)):
                        nc.vector.tensor_tensor(dst, x, y, ALU.mult)
                    dve.wait_ge(S["act_p"], t.up("act_p"))
                    for dst, x, y in zip(chunks(ar_out), tokens(key), tokens(L["w"])):
                        ins = stt(dst, x, -1.0, y, ALU.mult, ALU.mult)
                    ins.then_inc(S["pair_done"], 1)
                    dve.wait_ge(S["pair_done"], t.up("pair_done"))
                    t.skip(2)

            dve.wait_ge(S["pair_stored"], t.up("pair_stored"))
            dve.wait_ge(S["mm_done"], t.val("mm_done"))
            for u in range(2):
                nc.vector.memset(Z[u][2], 0.0)
            for c in (0, S0 - PAD):
                nc.vector.memset(A[:, :, c:c + PAD], 0.0)

            def four(ap, n=C):
                return ap.rearrange("p (a n) -> p a n", a=1).to_broadcast([ap.shape[0], 4, n])

            def init_m(u):
                for h in range(2):
                    r = slice(C * h, C * h + C)
                    ins = nc.vector.tensor_copy(Ms[u][r, :, r], k("ident2")[r].rearrange("p (a n) -> p a n", a=1)
                                                .to_broadcast([C, NPAIR, C]))
                ins.then_inc(S["m_init"], 1)

            for u in range(2):
                ins = nc.vector.memset(Ms[u], 0.0)
            step(ins)
            init_m(0)
            nc.vector.memset(ST, 0.0).then_inc(S["st_ready"], 1)
            dve.wait_ge(S["st_ready"], 1)
            for j in range(4):
                dve.sem_inc(S["c_in"], 1)

            def gram(u, g):
                dve.wait_ge(S["g_done"], t.up("g_done"))
                dve.sem_inc(S["held"], 1)
                for h in range(2):
                    r = slice(C * h, C * h + C)
                    bank = ps[:, 4 + 2 * g + h, :].rearrange("p (a n) -> p a n", a=4)
                    ins = nc.vector.copy_predicated(Ms[u][r, 4 * g:4 * g + 4, r], four(lvl[r, 0, :]), bank[r, :, C - C * h:P - C * h])
                ins.then_inc(S["m0_ready"], 1)
                for h, mask in enumerate(("gram_even", "gram_odd")):
                    bank = ps[:, 4 + 2 * g + h, :].rearrange("p (a n) -> p a n", a=4)
                    ins = nc.vector.tensor_tensor(Gs[u].rearrange("p a (h n) -> p a h n", h=2)[:, 4 * g:4 * g + 4, h, :],
                                                  bank, four(k(mask), P), ALU.mult)
                ins.then_inc(S["g_ready"], 1)

            def chunk(u, c, more=True):
                M = Ms[u]
                if more:
                    init_m(1 - u)
                for l in range(1, NL + 1):
                    for g in range(2):
                        dve.wait_ge(S["y_done"], t.up("y_done"))
                        nc.vector.tensor_copy(Y[:, 4 * g:4 * g + 4, :], four_of(2 * g, 0)).then_inc(S["y_ready"], 1)
                    for g in range(2):
                        dve.wait_ge(S["z_done"], t.up("z_done"))
                        dve.sem_inc(S["held"], 1)
                        for h in range(2):
                            r = slice(C * h, C * h + C)
                            ins = nc.vector.copy_predicated(M[r, 4 * g:4 * g + 4, r], four(lvl[r, l, :]),
                                                            four_of(2 * g, 1)[r])
                        ins.then_inc(S["m_ready"], 1)
                    if more and l in (2, 3):
                        if l == 2:
                            dve.wait_ge(S["m_init"], t.up("m_init"))
                        gram(1 - u, l - 2)
                for g in range(2):
                    dve.wait_ge(S["st_done"], t.up("st_done"))
                    for h in range(2):
                        r = slice(C * h, C * h + C)
                        st = ST[r, 4 * g:4 * g + 4, r]
                        ins = nc.vector.tensor_tensor(st, four_of(2 * g + 1, 0)[r], st, ALU.add)
                    step(ins)
                    for h in range(2):
                        r = slice(C * h, C * h + C)
                        st = ST[r, 4 * g:4 * g + 4, r]
                        ins = nc.vector.tensor_tensor(st, st, eLC[r, 4 * g:4 * g + 4, c].to_broadcast([C, 4, C]), ALU.mult)
                    ins.then_inc(S["c_in"], 1)

            dve.wait_ge(S["m_init"], t.up("m_init"))
            for g in range(2):
                gram(0, g)
            per = dict(g_done=4, m_init=2, y_done=4 * NL, z_done=4 * NL, st_done=4, dve_step=4)
            with t.loop(NCHUNK // 2, **per) as i:
                chunk(0, bass.ds(i * 2, 1))
                chunk(1, bass.ds(i * 2 + 1, 1))
            chunk(0, slice(NCHUNK, NCHUNK + 1), more=False)

            def mean(i):
                s, mm, rd = t.unit()
                dve.wait_ge(S["mm_done"], mm)
                if i >= 2:
                    dve.wait_ge(S["gn_ready"], i - 1)
                stt(c3(B[:, 6 + i % 2, :]), pset(s), -1.0 / C, c3(A[:, i, :]), ALU.mult, ALU.add).then_inc(S[f"read{s}"], 1)
                dve.wait_ge(S[f"read{s}"], rd)
                dve.sem_inc(S["mean_in"], 1)

            mean(0)
            for i in range(NPAIR):
                if i + 1 < NPAIR:
                    mean(i + 1)
                bonus, vv, gate = (B[:, 3 * (i % 2) + j, :] for j in range(3))
                dev, out = B[:, 6 + i % 2, :], B[:, 8 + i, :]
                dve.wait_ge(S[f"gn_in{i % 2}"], t.up(f"gn_in{i % 2}", 64))
                step(nc.vector.tensor_tensor(vv, bonus, vv, ALU.mult))
                s, mm, rd = t.unit()
                dve.wait_ge(S[f"read{s}"], rd)
                step(nc.vector.reciprocal(TM[:, 3, :], TM[:, 2, :]))
                stt(dev, dev, v1("lnw", i), TM[:, 3, :], ALU.mult, ALU.mult).then_inc(S["gn_used"], 1)
                dve.wait_ge(S["gn_used"], i + 1)
                step(stt(dev, dev, v1("lnb", i), vv, ALU.add, ALU.add))
                nc.vector.tensor_tensor(out, dev, gate, ALU.mult).then_inc(S["gn_ready"], 1)
            t.skip(KT)
            channel_mixer(1)

        @block.gpsimd
        def _(pool):
            t = Tally(pool)

            def store(dst, src):
                pool.dma_start(dst, src).then_inc(S["out_done"], 16)
                t.up("out_done", 16)

            t.skip(1)
            Vt = Bf[:, 16 * T:16 * T + 9 * 512].rearrange("p (b n) -> p b n", b=9)
            t.skip(9)
            pool.wait_ge(S["read0"], t.val("read0"))
            pool.wait_ge(S["read1"], t.val("read1"))
            store(O["v_p"], Vt[:, 0:8, :])
            store(O["v_s"], Vt[0:DEC, 8, :])
            n_v = t.n["out_done"]
            t.skip(8)
            pool.wait_ge(S["read0"], t.val("read0"))
            pool.wait_ge(S["read1"], t.val("read1"))
            store(O["k"], B[:, 4:8, :])
            t.skip(1)
            for c in range(NA):
                pool.wait_ge(S["tm_free"], t.up("tm_free"))
                pool.dma_start(O["conv"][:, c, 0:2], TM[:, 1, S0 - 2 * PAD:S0 - PAD]).then_inc(S["conv_out"], 16)
                pool.dma_start(O["conv"][:, c, 2:4], TM[:, 1, T - 2:T]).then_inc(S["conv_out"], 16)
                t.skip(3)
            pool.wait_ge(S["conv_out"], 32 * NA)
            pool.wait_ge(S["mm_done"], t.val("mm_done"))
            pool.dma_start(Af[0:HF, 5000:5000 + PAST], I["clogf"]).then_inc(S["cum_in"], 16)
            pool.wait_ge(S["cum_ready"], 1)
            store(O["logf"], Af[0:HF, T:2 * T])
            pool.dma_start(d_cum, Tf[0:HF, NALL:NALL + SEQ]).then_inc(S["cum_out"], 16)
            pool.dma_start(d_cums, Tf[0:HF, 0:NALL]).then_inc(S["cum_out"], 16)
            pool.wait_ge(S["cum_out"], 32)
            pool.wait_ge(S["out_done"], t.val("out_done"))

            bc = Af[:, 2 * T + 1024:2 * T + 1024 + 2048].rearrange("p (h n) -> p h n", h=2)
            Vs = Af[:, 2 * T:2 * T + 1024].rearrange("p (b n) -> p b n", b=8)
            d_c = d_cum.rearrange("(a h) n -> a h n", h=2)
            d_cs = d_cums.rearrange("(a h) n -> a h n", h=2)
            with t.loop(4, kv_in=32, staged=1, ot_read=8) as i:
                for h in range(2):
                    pool.dma_start(bc[:, h, :], d_c[bass.ds(i, 1), h, :].to_broadcast([P, SEQ])).then_inc(S["kv_in"], 16)
                nc.gpsimd.tensor_copy(Af[:, 0:T], B[:, bass.ds(i, 1), :].rearrange("p a n -> p (a n)"))
                nc.gpsimd.tensor_copy(Af[:, T:2 * T], B[:, bass.ds(i + 4, 1), :].rearrange("p a n -> p (a n)"))
                nc.gpsimd.tensor_copy(Vs, Vt[:, 0:8, bass.ds(i * P, P)]).then_inc(S["staged"], 1)
                t.up("staged")
                t.up("kv_in", 32)
                pool.wait_ge(S["ot_read"], t.up("ot_read", 8))
                pool.sem_inc(S["held"], 1)
            sm = Tf[:, 2304:]
            nc.gpsimd.memset(sm[:, 0:P], 0.0).then_inc(S["pool_step"], 1)
            pool.wait_ge(S["pool_step"], t.up("pool_step"))
            pool.sem_inc(S["held"], 1)
            kc = I["ck"]
            with t.loop(4, kv_in=64, staged=1, ot_read=1, pool_step=2) as i:
                pool.dma_start(Af[:, 0:PAST], kc[:, bass.ds(i, 1), :].rearrange("p a n -> p (a n)")).then_inc(S["kv_in"], 16)
                pool.dma_start(Af[:, PAST:2 * PAST].rearrange("p (b n) -> p b n", b=16),
                               I["cv"][:, :, bass.ds(i * P, P)]).then_inc(S["kv_in"], 16)
                for h in range(2):
                    src = d_cs[bass.ds(i, 1), h, :].to_broadcast([C, NALL])
                    pool.dma_start(Af[C * h:C * h + C, 2 * PAST + NALL:2 * PAST + 2 * NALL], src).then_inc(S["kv_in"], 16)
                nc.gpsimd.tensor_copy(sm[0:C, 0:C], B[0:C, bass.ds(i, 1), S0:T].rearrange("p a n -> p (a n)"))
                nc.gpsimd.tensor_copy(sm[C:P, C:P], B[C:P, bass.ds(i, 1), S0:T].rearrange("p a n -> p (a n)")).then_inc(S["pool_step"], 1)
                pool.wait_ge(S["pool_step"], t.up("pool_step"))
                pool.sem_inc(S["held"], 1)
                nc.gpsimd.tensor_copy(sm[:, P:P + C], B[:, bass.ds(i + 4, 1), S0:T].rearrange("p a n -> p (a n)")).then_inc(S["pool_step"], 1)
                pool.wait_ge(S["pool_step"], t.up("pool_step"))
                pool.sem_inc(S["held"], 1)
                nc.gpsimd.tensor_copy(sm[0:DEC, P + C:2 * P + C], Vt[0:DEC, 8, bass.ds(i * P, P)]).then_inc(S["staged"], 1)
                t.up("staged")
                t.up("kv_in", 64)
                pool.wait_ge(S["ot_read"], t.up("ot_read"))
                pool.sem_inc(S["held"], 1)

            def lend_h(l):
                for j in range(KT):
                    pool.wait_ge(S["h_ready"], 24 * l + j + 1)
                    pool.dma_start(d_h[:, j, :], H[:, j, :]).then_inc(S["h_out"], 16)
                pool.wait_ge(S["mm_done"], t.val("mm_done") + KT + 2 + 2 * NF)
                pool.wait_ge(S["h_out"], 16 * KT * (l + 1))
                pool.dma_start(H[:, :, :], d_h).then_inc(S["h_in"], 16)
                t.skip(KT + 2 + 2 * NF + KT + 2 + 2 * KT)

            def finish_y():
                pool.wait_ge(S["h_ready"], 48)
                pool.sem_inc(S["held"], 1)
                store(O["y"], H[:, :, :])
                pool.wait_ge(S["out_done"], t.val("out_done"))

            lend_h(0)
            if stop < 2:
                pool.wait_ge(S["h_ready"], 24)
                pool.sem_inc(S["held"], 1)
                store(O["y"], H[:, :, :])
                pool.wait_ge(S["out_done"], t.val("out_done"))
                return

            pool.wait_ge(S["shift_in"], 1)
            store(O["shift"], last[:, :, :])

            UPTO = 1 + 9 + 8 + 1 + 3 * NA + KT + 2 + 2 * NF + KT + 2 + 2 * KT + 1
            t.n["mm_done"], t.n["read0"], t.n["read1"] = UPTO, (UPTO + 1) // 2, UPTO // 2

            def keep(name):
                with t.loop(2, mm_done=4, read0=2, read1=2, xs0=16, xs1=16, xs2=16, xs3=16) as i:
                    for j in range(4):
                        s, mm, rd = t.unit()
                        pool.wait_ge(S[f"read{s}"], rd)
                        pool.sem_inc(S["held"], 1)
                        pool.dma_start(d_x[name][bass.ds(i * 4 + j, 1)].rearrange("a p n -> (a p) n"),
                                       B[:, 18 + j, :]).then_inc(S[f"xs{j}"], 16)
                        t.up(f"xs{j}", 16)

            for name in "wag":
                t.skip(1)
                keep(name)
            for name in "rk":
                keep(name)
            for j in range(4):
                pool.wait_ge(S[f"xs{j}"], t.val(f"xs{j}"))
            pool.wait_ge(S["mm_done"], t.val("mm_done"))

            def load_pair(i):
                for n in "rkwa":
                    pool.dma_start(Lb[i % 2][n], d_x[n][i]).then_inc(S[f"l_in{i % 2}"], 16)

            load_pair(0)
            load_pair(1)
            pool.sem_inc(S["sum_stored"], 1)
            pool.sem_inc(S["pair_stored"], 1)
            for i in range(NPAIR):
                t.skip(1)
                s, mm, rd = t.unit()
                pool.wait_ge(S[f"read{s}"], rd)
                j = i % 4
                pool.dma_start(d_v[i, :, 0:SEQ], B[:, 18 + j, P0:P0 + SEQ]).then_inc(S[f"xv{j}"], 16)
                pool.dma_start(d_v[i, :, SEQ:SEQ + C], B[:, 18 + j, S0:T]).then_inc(S[f"xs{j}"], 16)
                t.up(f"xs{j}", 16)
                s, mm, rd = t.unit()
                pool.wait_ge(S[f"read{s}"], rd)
                pool.dma_start(d_x["sum"][i], TM[:, 2, :]).then_inc(S["sum_out"], 16)
                pool.wait_ge(S["sum_out"], 16 * i + 16)
                pool.sem_inc(S["sum_stored"], 1)
                pool.wait_ge(S["pair_done"], i + 1)
                pool.dma_start(d_bk[i], bk_out).then_inc(S["b_out"], 16)
                pool.dma_start(d_ar[i], ar_out).then_inc(S["b_out"], 16)
                if i + 2 < NPAIR:
                    load_pair(i + 2)
                pool.wait_ge(S["b_out"], 32 * i + 32)
                pool.sem_inc(S["pair_stored"], 1)
            for j in range(4):
                pool.wait_ge(S[f"xs{j}"], t.val(f"xs{j}"))
                pool.wait_ge(S[f"xv{j}"], 32)

            pool.wait_ge(S["st_ready"], 1)
            t.up("c_in", 4)
            t.up("zi1", 0)

            def load_chunk(u, c):
                ZB, ZA, ZV = Z[u]
                for src, dst, n in ((d_bk, ZB[:, :, 0:P], P), (d_ar, ZA[:, :, C:C + P], P), (d_v, ZV[:, :, C:P], C)):
                    cols = slice(c * n, c * n + n) if isinstance(c, int) else bass.ds(c * n, n)
                    pool.dma_start(dst, src.rearrange("a p n -> p a n")[:, :, cols]).then_inc(S[f"zi{u}"], 16)
                pool.wait_ge(S[f"zi{u}"], t.up(f"zi{u}", 48))
                pool.sem_inc(S["held"], 1)
                nc.gpsimd.tensor_copy(ZB[:, :, P:P + C], ZB[:, :, 0:C])
                nc.gpsimd.tensor_copy(ZA[:, :, 0:C], ZA[:, :, P:P + C]).then_inc(S["z_dup"], 1)

            load_chunk(0, 0)
            with t.loop(NCHUNK // 2, c_in=8, zi0=48, zi1=48) as i:
                for u in range(2):
                    pool.wait_ge(S["c_in"], t.val("c_in"))
                    pool.sem_inc(S["held"], 1)
                    t.up("c_in", 4)
                    load_chunk(1 - u, i * 2 + (u + 1))
            pool.wait_ge(S["c_in"], t.val("c_in"))
            for h in range(2):
                r = slice(C * h, C * h + C)
                store(O["wkv"][r, 0], ST[r, :, C * h:C * h + C])
            pool.wait_ge(S["out_done"], t.val("out_done"))
            for h in range(2):
                r = slice(C * h, C * h + C)
                pool.dma_start(ST[r, :, C * h:C * h + C], I["wkv"][r]).then_inc(S["state_in"], 16)
            pool.wait_ge(S["c_in"], t.up("c_in", 4))
            for h in range(2):
                r = slice(C * h, C * h + C)
                store(O["wkv"][r, 1], ST[r, :, C * h:C * h + C])

            for i in range(NPAIR):
                if i == 2:
                    pool.wait_ge(S["out_done"], t.val("out_done"))
                    pool.sem_inc(S["state_out"], 1)
                if i >= 2:
                    pool.wait_ge(S["gn_ready"], i - 1)
                sm_, vv, gate = (B[:, 3 * (i % 2) + j, :] for j in range(3))
                done = S[f"gn_in{i % 2}"]
                pool.dma_start(sm_, d_x["sum"][i]).then_inc(done, 16)
                pool.dma_start(vv[:, P0:P0 + SEQ], d_v[i, :, 0:SEQ]).then_inc(done, 16)
                pool.dma_start(vv[:, S0:T], d_v[i, :, SEQ:SEQ + C]).then_inc(done, 16)
                pool.dma_start(gate, d_x["g"][i]).then_inc(done, 16)
            t.skip(2 * NPAIR)
            lend_h(1)
            finish_y()


def shape_constants():
    i = np.arange(P)
    eye = np.eye(P, dtype=np.float32)
    pair = (i[:, None] // C == i[None, :] // C).astype(np.float32)
    causal = np.where(i[None, :] > i[:, None], np.float32(NEG), np.float32(0))
    c = np.arange(C)
    causal2 = np.where(c[None, :] > (i % C)[:, None], np.float32(NEG), np.float32(0))
    strict = (c[:, None] < c[None, :]).astype(np.float32)
    incl = (c[:, None] <= c[None, :]).astype(np.float32)
    gram_even = np.block([[incl, strict], [incl, strict]])
    gram_odd = np.block([[strict, incl], [strict, incl]])

    def level(n):
        same = (i[:, None] % C) // (2 * n) == i[None, :] // (2 * n)
        return (same & (i[:, None] % (2 * n) < n) & (i[None, :] % (2 * n) >= n))[:, :C]

    cst = np.concatenate([eye, np.ones((P, P), np.float32), pair, causal, causal2, gram_even, gram_odd,
                          np.vstack([eye[:C, :C]] * 2)], 1)
    lvl = np.stack([level(n) for n in LEVELS], 1).astype(np.float32).reshape(P, -1)
    return np.ascontiguousarray(cst), np.ascontiguousarray(lvl)


def kernel(**inputs):
    import concourse.bacc as bacc
    from concourse.bass_utils import run_bass_kernel_spmd

    X = {n: np.asarray(a) for n, a in inputs.items()}

    def feature_major(prompt, sample):
        n = prompt.shape[1] // P
        out = np.zeros((P, n, T), np.float32)
        out[:, :, P0:P0 + SEQ] = prompt.T.reshape(n, P, SEQ).transpose(1, 0, 2)
        out[:, :, S0:] = sample.T.reshape(n, P, DEC).transpose(1, 0, 2)
        return out

    def tiles(w, cols=P):
        kk, m = w.shape
        return w.reshape(kk // P, P, m // cols, cols).transpose(2, 1, 0, 3).reshape(m // cols, P, -1)

    def columns(v):
        return v.reshape(-1, P).T

    def laced(*ws):
        return np.stack(ws, 1).reshape(-1, *ws[0].shape[1:])

    cst, lvl = shape_constants()
    w_in = X["e_w_in"][0]
    ax, ab, ac = (w_in[:, DA * j:DA * j + DA] for j in range(3))
    rows = {"mu%d" % n: X["r_mu"][0, n] for n in range(6)}
    for n in range(2):
        for short, name in (("pre", "mix_norm_pre"), ("post", "mix_norm_post"), ("fpre", "ffn_norm_pre"),
                            ("fpost", "ffn_norm_post"), ("ple", "ple_norm")):
            rows[f"{short}{n}"] = X[name][n]
    for short, name in (("w0", "r_w0"), ("a0", "r_a0"), ("kk", "r_k_k"), ("ka", "r_k_a"), ("lnw", "r_ln_w"),
                        ("lnb", "r_ln_b")):
        rows[short] = X[name][0]
    rows["rk"] = X["r_r_k"][0].reshape(-1)
    rows["shift"] = X["state_shift"][0, 0]
    down = [X["f_w_down"][l].reshape(2, HALF, P, KT, P).transpose(3, 0, 2, 1, 4).reshape(2 * KT, P, SLOT)
            for l in range(2)]
    arrays = {
        "cst": cst, "lvl": lvl, "vecs": np.stack([columns(rows[n]) for n in VEC], 1),
        "convw": np.stack([columns(X["e_conv_w"][0, j]) for j in range(3)], 1),
        "convs": np.stack([columns(X["state_conv"][0, 0, j]) for j in range(2)], 2),
        "bf": X["e_b_f"][0].reshape(HF, 1),
        "x": feature_major(X["x_prompt"][0], X["x_sample"][0]),
        "p": np.stack([feature_major(X["p_prompt"][l, 0], X["p_sample"][l, 0]) for l in range(2)]),
        "wv": tiles(w_in[:, 3 * DA + 1024:3 * DA + 1536], 512)[0],
        "wqk": tiles(w_in[:, 3 * DA:3 * DA + 1024]),
        "wf": tiles(w_in[:, 3 * DA + 1536:], HF)[0],
        "wconv": laced(tiles(ax), tiles(ac), tiles(ab)),
        "wout": tiles(X["e_w_out"][0]),
        "wgu": np.stack([laced(tiles(X["f_w_gate"][l]), tiles(X["f_w_up"][l])) for l in range(2)]),
        "wdown": np.stack(down),
        "wpg": np.stack([tiles(X["ple_gate"][l]) for l in range(2)]),
        "wpp": np.stack([tiles(X["ple_proj"][l]) for l in range(2)]),
        "clogf": X["cache_logf"][0, 0].T,
        "ck": X["cache_k"][0, 0].reshape(PAST, NA, P).transpose(2, 1, 0),
        "cv": X["cache_v"][0, 0].reshape(PAST // P, P, 512).transpose(1, 0, 2),
        "lw1": tiles(X["r_w1"][0], C)[0], "lw2": X["r_w2"][0], "la1": tiles(X["r_a1"][0], C)[0], "la2": X["r_a2"][0],
        "lg1": tiles(X["r_g1"][0])[0], "lg2": X["r_g2"][0],
        "wrkv": np.concatenate([tiles(X[n][0]) for n in ("r_w_r", "r_w_k", "r_w_v")]),
        "wo": tiles(X["r_w_o"][0]),
        "wkv": X["state_wkv"][0, 0].reshape(NPAIR, 2, C, C).transpose(1, 3, 0, 2).reshape(P, NPAIR, C),
    }
    shapes = {"y": (P, KT, T), "k": (P, NA, T), "v_p": (P, 8, 512), "v_s": (DEC, 512), "logf": (HF, T),
              "conv": (P, NA, 4), "shift": (P, 2, KT), "wkv": (P, 2, NPAIR, C)}

    nc = bacc.Bacc("TRN2", target_bir_lowering=False, num_devices=1)
    feed, ins = {}, {}
    for n, a in arrays.items():
        a = np.ascontiguousarray(a)
        feed["in_" + n] = a
        ins[n] = nc.dram_tensor("in_" + n, a.shape, mybir.dt.from_np(a.dtype), kind="ExternalInput").ap()
    outs = {n: nc.dram_tensor("out_" + n, s, F32, kind="ExternalOutput").ap() for n, s in shapes.items()}
    build_trunk(nc, ins, outs)
    res = run_bass_kernel_spmd(nc, [feed], core_ids=[0]).results[0]
    got = {n: res["out_" + n] for n in shapes}

    def tokens(a):
        flat = a.transpose(1, 0, 2).reshape(-1, T).T
        return flat[P0:P0 + SEQ], flat[S0:]

    y_p, y_s = tokens(got["y"])
    k_p, k_s = tokens(got["k"])
    v_p = got["v_p"].transpose(1, 0, 2).reshape(SEQ, 512)
    conv = got["conv"].transpose(1, 0, 2).reshape(DA, 4).T
    shift = got["shift"].transpose(1, 2, 0).reshape(2, D)
    wkv = got["wkv"].reshape(2, C, 2, NPAIR, C).transpose(2, 3, 0, 4, 1).reshape(2, HR, C, C)
    lf = got["logf"].T
    heads = lambda a, n: np.ascontiguousarray(a).reshape(1, 1, n, HF, C)
    groups = []
    for g, (n, y, kk, vv, c0) in enumerate(((SEQ, y_p, k_p, v_p, P0), (DEC, y_s, k_s, got["v_s"], S0))):
        groups.append((np.ascontiguousarray(y)[None], heads(kk, n), heads(vv, n),
                       np.ascontiguousarray(lf[c0:c0 + n]).reshape(1, 1, n, HF),
                       np.ascontiguousarray(conv[2 * g:2 * g + 2]).reshape(1, 1, 2, DA),
                       np.ascontiguousarray(shift[g]).reshape(1, 1, D),
                       np.ascontiguousarray(wkv[g]).reshape(1, 1, HR, C, C)))
    (yp, *prompt), (ys, *sample) = groups
    return (yp, ys, *prompt, *sample)
```

```python
from contextlib import ExitStack, contextmanager

import numpy as np

import concourse.bass as bass
from concourse import mybir

F32 = mybir.dt.float32
F32R = mybir.dt.float32r
BF16 = mybir.dt.bfloat16
U8 = mybir.dt.uint8
ALU = mybir.AluOpType
ACT = mybir.ActivationFunctionType
AX_X = mybir.AxisListType.X

P = 128
D = 1024
KT = D // P
SEQ, DEC, PAST = 1024, 64, 2048
PAD = 2
P0 = PAD
S0 = PAD + SEQ + PAD
T = S0 + DEC
NCH = 3
CH = T // NCH
assert NCH * CH == T and CH <= 512
DA = 512
NA = DA // P
HF = 8
DFF = 2816
NF = DFF // P
HALF = NF // 2
PLE = 256
NP_ = PLE // P
HR = 16
NPAIR = HR // 2
C = 64
NCHUNK = SEQ // C
NALL = PAST + DEC
NORM_EPS, GN_EPS, L2_EPS = 1e-6, 64e-5, 1e-12
NEG = -1e30
DECAY = float(np.exp(-0.5))
SUMS = 8
SLOTS = 4
SLOT = HALF * P

MIXER = 4 * (NF // 2) + 2 * KT + 2 * KT
CHUNKS = [3 * 8 + 5, 3 * 8 + 5 + MIXER + 6 + 4 * KT]
NORMED = [2 * KT, 7 * KT]

VEC = ["pre0", "pre1", "post0", "post1", "fpre0", "fpre1", "fpost0", "fpost1", "ple0", "ple1",
       "mu0", "mu1", "mu2", "mu3", "mu4", "mu5", "w0", "a0", "kk", "ka", "rk", "lnw", "lnb", "shift"]
V = {n: i for i, n in enumerate(VEC)}
NV = len(VEC)
CST = {"ident": (0, P), "ones": (P, P), "pair": (2 * P, P), "causal": (3 * P, P), "causal2": (4 * P, C),
       "gram_even": (4 * P + C, P), "gram_odd": (5 * P + C, P), "ident2": (6 * P + C, C)}
NCST = 6 * P + 2 * C
LEVELS = (1, 2, 4, 8, 16, 32)
NL = len(LEVELS) - 1


class Tally:

    def __init__(self, engine):
        self.engine, self.n, self.per, self.i = engine, {}, {}, None

    def val(self, name, off=0):
        base = self.n.get(name, 0) + off
        if self.per.get(name):
            return self.i * self.per[name] + base
        return base

    def some(self, name, off=0):
        return bool(self.per.get(name)) or self.n.get(name, 0) + off > 0

    def up(self, name, k=1):
        self.n[name] = self.n.get(name, 0) + k
        return self.val(name)

    @contextmanager
    def loop(self, times, **per):
        before = dict(self.n)
        with self.engine.Fori(0, times) as i:
            self.i, self.per = i, per
            yield i
        for name in self.n.keys() | per.keys():
            moved = self.n.get(name, 0) - before.get(name, 0)
            assert moved == per.get(name, 0), (self.engine, name, moved, per.get(name, 0))
            self.n[name] = self.n.get(name, 0) + moved * (times - 1)
        self.i, self.per = None, {}

    def unit(self):
        s = self.n.get("mm_done", 0) % 2
        return s, self.up("mm_done"), self.up(f"read{s}")

    def skip(self, units):
        for _ in range(units):
            self.unit()

    def chunk(self):
        slot = self.n.get("chunk", 0) % SLOTS
        self.up("chunk")
        return slot, self.up(f"w{slot}", 16)

    def skip_chunks(self, chunks):
        for _ in range(chunks):
            self.chunk()


def build_trunk(nc, I, O, stop=99):
    ctx = ExitStack()
    with ctx:
        def sb(name, shape, dt=F32):
            return ctx.enter_context(nc.sbuf_tensor(name, shape, dt))

        def sem(name):
            return ctx.enter_context(nc.semaphore(name))

        def scratch(name, shape):
            return nc.dram_tensor(name, shape, F32, kind="Internal").ap()

        with ExitStack() as rounded:
            Hr, Ar, Br, Wr, TMr = (rounded.enter_context(nc.sbuf_tensor(n, shape, F32R)) for n, shape in (
                ("H_r", [P, KT, T]), ("A_r", [P, KT, T]), ("B_r", [P, NF, T]), ("W_r", [P, SLOTS, SLOT]),
                ("TM_r", [P, 4, T])))
        H = sb("H", [P, KT, T])
        A = sb("A", [P, KT, T])
        B = sb("B", [P, NF, T])
        W = sb("W", [P, SLOTS, SLOT])
        TM = sb("TM", [P, 4, T])
        cst = sb("cst", [P, NCST])
        vec = sb("vec", [P, NV, KT])
        convw = sb("convw", [P, 3, NA])
        convs = sb("convs", [P, NA, 2])
        bf = sb("bf", [HF, 1])
        mub = sb("mub", [P, 6, KT])
        kab = sb("kab", [P, KT])
        eps = sb("eps", [P, 2])
        last = sb("last", [P, 2, KT])
        identb = sb("identb", [P, P], BF16)
        causb = sb("causb", [P, P + C], BF16)
        lvl = sb("lvl", [P, len(LEVELS), C], U8)
        mx = sb("mx", [P, 12])
        ps = ctx.enter_context(nc.psum_tensor("ps", [P, 8, 512], F32))

        Af = A[:, :, :].rearrange("p a n -> p (a n)")
        Bf = B[:, :, :].rearrange("p a n -> p (a n)")
        Tf = TM[:, :, :].rearrange("p a n -> p (a n)")
        Brf = Br[:, :, :].rearrange("p a n -> p (a n)")

        UPPER = {"first": (Br[:, NF - 1, 0:KT * P], TMr[:, 3, 0:KT * P]),
                 "out": (Br[:, 16, 0:KT * P], Br[:, 17, 0:KT * P]),
                 "mixer": (TMr[:, 2, 0:KT * P], TMr[:, 3, 0:KT * P])}

        def wh_of(t):
            m = t.n.get("wh", 0)
            t.up("wh")
            return UPPER[t.stage][m % 2]

        def enter(t, stage):
            t.stage, t.n["wh"] = stage, 0

        WV = KT * DA
        wv, wvl, wvh = Bf[:, 8 * T:8 * T + WV], Brf[:, 8 * T:8 * T + WV], Brf[:, 12 * T:12 * T + WV]

        Hf = H[:, :, :].rearrange("p a n -> p (a n)")
        QK = [(buf[:, 0:T], buf[:, T:2 * T]) for buf in (Af, Hf)]
        VP = [buf[:, 2 * T:2 * T + SEQ].rearrange("p (b n) -> p b n", b=8) for buf in (Af, Hf)]
        BIAS = [buf[:, 2 * T + SEQ:2 * T + 3 * SEQ].rearrange("p (h n) -> p h n", h=2) for buf in (Af, Hf)]
        EXP = [Af[:, 2 * T + (3 + h) * SEQ:2 * T + (4 + h) * SEQ] for h in range(2)]
        PT = [Tf[:, SEQ * j:SEQ * j + SEQ] for j in range(2)]
        OT = Tf[:, 2 * SEQ:2 * SEQ + P]
        CK = [buf[:, 0:PAST] for buf in (Af, Hf)]
        CV = [buf[:, PAST:2 * PAST].rearrange("p (b n) -> p b n", b=16) for buf in (Af, Hf)]
        EXPS = [buf[:, 2 * PAST:2 * PAST + NALL] for buf in (Af, Hf)]
        BIASS = [buf[:, 2 * PAST + NALL:2 * PAST + 2 * NALL] for buf in (Af, Hf)]
        SM = [Tf[:, 2304 + 3 * P * j:2304 + 3 * P * j + 3 * P] for j in range(2)]
        PTL = Tf[:, 0:17 * P]

        Lb = [{n: B[:, 4 * u + j, :] for j, n in enumerate("rkwa")} for u in range(2)]
        key2 = [A[:, 0, :], A[:, 1, :]]
        tmpA, cumL, expL, expnL, reset = A[:, 2, :], A[:, 3, :], B[:, 17, :], TM[:, 0, :], B[:, 16, :]
        bk_out = A[:, 4:6, :].rearrange("p a n -> p (a n)")[:, 0:(NCHUNK + 1) * P]
        ar_out = A[:, 6:8, :].rearrange("p a n -> p (a n)")[:, 0:(NCHUNK + 1) * P]

        Z = [[Bf[:, 4608 * u + 1536 * j:4608 * u + 1536 * j + 1536].rearrange("p (a n) -> p a n", a=NPAIR)
              for j in range(3)] for u in range(2)]
        BK, UV, BKUV, Gs, Ms, AB = [], [], [], [], [], []
        o_ = 9 * T
        for _ in range(2):
            BK.append(Bf[:, o_:o_ + NPAIR * P].rearrange("p (a n) -> p a n", a=NPAIR))
            UV.append(Bf[:, o_ + NPAIR * P:o_ + 2 * NPAIR * P].rearrange("p (a n) -> p a n", a=NPAIR))
            BKUV.append(Bf[:, o_:o_ + 2 * NPAIR * P].rearrange("p (j a n) -> p a j n", j=2, a=NPAIR))
            o_ += 2 * NPAIR * P
            for part, w_ in ((Gs, 2 * P), (AB, C), (Ms, P)):
                part.append(Bf[:, o_:o_ + NPAIR * w_].rearrange("p (a n) -> p a n", a=NPAIR))
                o_ += NPAIR * w_
        P1 = Bf[:, o_:o_ + NPAIR * C].rearrange("p (a n) -> p a n", a=NPAIR)
        assert o_ + NPAIR * C <= NF * T
        ST = Tf[:, 0:NPAIR * P].rearrange("p (a n) -> p a n", a=NPAIR)
        MT, Y = (Tf[:, NPAIR * (P + C * j):NPAIR * (P + C * j + C)].rearrange("p (a n) -> p a n", a=NPAIR)
                 for j in range(2))

        def four_of(bank, half):
            return ps[:, bank, 256 * half:256 * half + 256].rearrange("p (a n) -> p a n", a=4)

        eLC = sb("eLC", [P, NPAIR, NCHUNK + 1])

        def k(name):
            o, n = CST[name]
            return cst[:, o:o + n]

        def v1(name, kt):
            return vec[:, V[name], kt:kt + 1]

        def c3(ap):
            return ap.rearrange("p (c n) -> p c n", c=NCH)

        def pset(s):
            return ps[:, NCH * s:NCH * s + NCH, 0:CH]

        d_cum = scratch("d_cum", [HF, SEQ])
        d_cums = scratch("d_cums", [HF, NALL])
        d_x = {n: scratch(f"d_{n}", [NPAIR, P, T]) for n in
               ("w", "a", "g", "r", "k", "sum")}
        d_h = scratch("d_h", [P, KT, T])
        d_bk = scratch("d_bk", [NPAIR, P, (NCHUNK + 1) * P])
        d_ar = scratch("d_ar", [NPAIR, P, (NCHUNK + 1) * P])
        d_v = scratch("d_v", [NPAIR, P, (NCHUNK + 1) * C])

        names = ["setup", "held", "x_in", "mm_done", "read0", "read1", "w_used", "wl_ready", "xh_ready", "xl_ready", "h_out", "h_in", "sq_ready", "sq_used", "rs_ready",
                 "normed", "h_ready", "pe_step", "act_step", "dve_step", "pool_step", "out_done",
                 "wv_in", "wv_ready", "v_ready", "tm_free", "ax_ready", "gate_ready", "p_in",
                 "cum_ready", "cum_out", "cum_in", "stage_in", "staged", "s_done", "s_read", "p_ready", "e_ready",
                 "pt_done", "pt_read", "o_done", "o_read", "ot_done", "ot_read", "bias_in0", "bias_in1", "kv_in0", "kv_in1", "attn_pair",
                 "xn_ready", "xn_tmp", "xv0", "xv1", "xv2", "xv3", "xs0", "xs1", "xs2", "xs3", "key_sq", "rk_ready", "gn_in", "dev_sq",
                 "b_out", "key_scaled", "sum_out", "pair_done", "pair_stored", "sum_stored", "rn_used", "l_in0", "l_in1", "gn_in0", "gn_in1", "mean_in", "gn_used", "shift_in", "conv_out",
                 "zi0", "zi1", "z_dup", "g_done", "g_ready", "m_init", "tok_done", "tok_read", "n_done", "n_ready", "mt_done", "mt_ready", "a_done", "a_ready", "u_done", "u_ready", "st_done", "oo_done", "oo_read", "st_read", "m_ready", "m0_ready", "y_done", "y_ready",
                 "z_done", "c_done", "c_ready", "c_u", "c_st", "c_in", "chunk_done", "st_ready", "state_in", "state_out", "pa_done", "pb_done",
                 "o_all", "l_in", "l_out", "dve_p", "act_p", "pool_p", "gn_ready"]
        S = {n: sem(n) for n in names}
        for j in range(SLOTS):
            S[f"w{j}"] = sem(f"w{j}")
        block = ctx.enter_context(nc.Block())


        @block.sync
        def _(sp):
            t = Tally(sp)

            def chunk(src, n, rows=P):
                w = t.n.get("chunk", 0)
                slot = w % SLOTS
                t.up("chunk")
                if t.some("chunk", -3):
                    sp.wait_ge(S["w_used"], t.val("chunk", -3))
                sp.dma_start(W[0:rows, slot, 0:n], src).then_inc(S[f"w{slot}"], 16)

            for dst, src in ((cst[:, :], I["cst"]), (vec[:, :, :], I["vecs"]), (convw[:, :, :], I["convw"]),
                             (convs[:, :, :], I["convs"]), (bf[:, :], I["bf"]), (TM[:, 3, 0:len(LEVELS) * C], I["lvl"])):
                sp.dma_start(dst, src).then_inc(S["setup"], 16)
            for j in range(KT):
                sp.dma_start(H[:, j, :], I["x"][:, j, :]).then_inc(S["x_in"], 16)
            sp.dma_start(Bf[:, 8 * T:8 * T + KT * 512], I["wv"]).then_inc(S["wv_in"], 16)

            for j in range(2 * NA):
                chunk(I["wqk"][j], KT * P)
            chunk(I["wf"], KT * HF)
            for j in range(3 * NA):
                chunk(I["wconv"][j], KT * P)
            with t.loop(2, chunk=4) as i:
                for j in range(4):
                    chunk(I["wout"][bass.ds(i * 4 + j, 1)].rearrange("a p n -> (a p) n"), KT * P)

            def channel_mixer(l):
                with t.loop(NF // 2, chunk=4) as i:
                    for j in range(4):
                        chunk(I["wgu"][l, bass.ds(i * 4 + j, 1)].rearrange("a p n -> (a p) n"), KT * P)
                with t.loop(KT // 2, chunk=4) as i:
                    for j in range(4):
                        chunk(I["wdown"][l, bass.ds(i * 4 + j, 1)].rearrange("a p n -> (a p) n"), SLOT)
                t.up("p_in", 16)
                sp.wait_ge(S["normed"], KT * (5 * l + 3) + 1)
                sp.dma_start(B[:, 0:NP_, :], I["p"][l]).then_inc(S["p_in"], 16)
                with t.loop(KT // 2, chunk=4) as i:
                    for j in range(2):
                        chunk(I["wpg"][l, bass.ds(i * 2 + j, 1)].rearrange("a p n -> (a p) n"), KT * P)
                        chunk(I["wpp"][l, bass.ds(i * 2 + j, 1)].rearrange("a p n -> (a p) n"), NP_ * P)

            channel_mixer(0)
            if stop < 2:
                return
            chunk(I["lw1"], KT * C)
            chunk(I["lw2"], D, C)
            chunk(I["la1"], KT * C)
            chunk(I["la2"], D, C)
            chunk(I["lg1"], KT * P)
            chunk(I["lg2"], D)
            with t.loop(3 * KT // 4, chunk=4) as i:
                for j in range(4):
                    chunk(I["wrkv"][bass.ds(i * 4 + j, 1)].rearrange("a p n -> (a p) n"), KT * P)
            with t.loop(2, chunk=4) as i:
                for j in range(4):
                    chunk(I["wo"][bass.ds(i * 4 + j, 1)].rearrange("a p n -> (a p) n"), KT * P)
            channel_mixer(1)

        @block.tensor
        def _(pe):
            t = Tally(pe)

            def first_use(ins):
                ins.then_inc(S["w_used"], 1)

            def unit(chunks, xs, cols=P, rows=P, ws=None):
                s, mm, rd = t.unit()
                pe.wait_ge(S[f"read{s}"], t.val(f"read{s}", -1))
                n, total = 0, sum(chunks)
                for count in chunks:
                    w = t.n.get("chunk", 0)
                    slot = w % SLOTS
                    t.up("chunk")
                    t.up("w_used")
                    pe.wait_ge(S[f"w{slot}"], t.up(f"w{slot}", 16))
                    for j in range(count):
                        for c in range(NCH):
                            ins = nc.tensor.matmul(
                                ps[0:cols, NCH * s + c, 0:CH], W[0:rows, slot, j * cols:(j + 1) * cols],
                                xs[n][0:rows, c * CH:(c + 1) * CH], start=(n == 0), stop=(n == total - 1))
                            if j == 0 and c == 0:
                                first_use(ins)
                        n += 1
                ins.then_inc(S["mm_done"], 1)

            def split_unit(xh, xl, cols=P, arriving=False):
                s, mm, rd = t.unit()
                pe.wait_ge(S[f"read{s}"], t.val(f"read{s}", -1))
                slot, _ = t.chunk()
                t.up("w_used")
                pe.wait_ge(S["wl_ready"], t.up("wl_ready"))
                wh, wl = wh_of(t), Wr[:, slot, 0:KT * P]
                for j in range(KT):
                    if arriving:
                        pe.wait_ge(S["xl_ready"], t.up("xl_ready"))
                    for n, (w, x) in enumerate(((wh, xh), (wh, xl), (wl, xh))):
                        for c in range(NCH):
                            ins = nc.tensor.matmul(ps[0:cols, NCH * s + c, 0:CH], w[:, j * cols:(j + 1) * cols],
                                                   x[j][:, c * CH:(c + 1) * CH],
                                                   start=(j == 0 and n == 0), stop=(j == KT - 1 and n == 2))
                            if j == 0 and n == 0 and c == 0:
                                first_use(ins)
                ins.then_inc(S["mm_done"], 1)

            def sums(lhs, x):
                s, mm, rd = t.unit()
                if t.some(f"read{s}", -1):
                    pe.wait_ge(S[f"read{s}"], t.val(f"read{s}", -1))
                for c in range(NCH):
                    ins = nc.tensor.matmul(ps[:, NCH * s + c, 0:CH], lhs, x[:, c * CH:(c + 1) * CH],
                                           start=True, stop=True)
                ins.then_inc(S["mm_done"], 1)

            def norm():
                pe.wait_ge(S["sq_used"], t.up("sq_used", KT))
                sums(k("ones"), TM[:, 2, :])

            def norm_direct():
                s, mm, rd = t.unit()
                pe.wait_ge(S[f"read{s}"], t.val(f"read{s}", -1))
                base = t.val("sq_used")
                t.up("sq_used", KT)
                for j in range(KT):
                    pe.wait_ge(S["sq_ready"], base + j + 1)
                    for c in range(NCH):
                        ins = nc.tensor.matmul(ps[:, NCH * s + c, 0:CH], k("ones"), TM[:, j % 2, c * CH:(c + 1) * CH],
                                               start=(j == 0), stop=(j == KT - 1))
                    ins.then_inc(S["sq_used" if j < KT - 1 else "mm_done"], 1)
                pe.wait_ge(S["mm_done"], mm)
                pe.sem_inc(S["sq_used"], 1)

            def wait_normed():
                pe.wait_ge(S["normed"], t.up("normed", KT))

            xl, xh = ([x[:, j, :] for j in range(KT)] for x in (Ar, Hr))

            def split_units(count, xh, xl):
                for j in range(4):
                    split_unit(xh, xl, arriving=(j == 0))
                with t.loop(count // 4 - 1, chunk=4, w_used=4, wl_ready=4, wh=4, mm_done=4, read0=2, read1=2,
                            w0=16, w1=16, w2=16, w3=16):
                    for j in range(4):
                        split_unit(xh, xl)

            def dense8(count):
                with t.loop(count // 4, chunk=4, w_used=4, mm_done=4, read0=2, read1=2, w0=16, w1=16, w2=16, w3=16):
                    for j in range(4):
                        unit([KT], xs)

            pe.wait_ge(S["setup"], 96)
            norm_direct()
            t.up("normed", KT)
            pe.wait_ge(S["wv_ready"], 1)
            wvh3, wvl3 = (w.rearrange("p (k n) -> p k n", k=KT) for w in (wvh, wvl))
            for tt in range(9):
                s, mm, rd = t.unit()
                if t.some(f"read{s}", -1):
                    pe.wait_ge(S[f"read{s}"], t.val(f"read{s}", -1))
                c0, n = (P0 + P * tt, P) if tt < 8 else (S0, DEC)
                for j in range(KT):
                    if tt == 0:
                        pe.wait_ge(S["xl_ready"], t.up("xl_ready"))
                    for m, (x, w) in enumerate(((xh, wvh3), (xh, wvl3), (xl, wvh3))):
                        ins = nc.tensor.matmul(ps[0:n, NCH * s, :], x[j][:, c0:c0 + n], w[:, j, :],
                                               start=(j == 0 and m == 0), stop=(j == KT - 1 and m == 2))
                ins.then_inc(S["mm_done"], 1)
            enter(t, "first")
            with t.loop(2, chunk=4, w_used=4, wl_ready=4, wh=4, mm_done=4, read0=2, read1=2, w0=16, w1=16, w2=16, w3=16):
                for j in range(4):
                    split_unit(xh, xl)
            split_unit(xh, xl, cols=HF)
            for j in range(3 * NA):
                split_unit(xh, xl)

            def s_set(u):
                return ps[:, 2 * (u % 2):2 * (u % 2) + 2, :]

            PTp = [ps[:, 4 + b, :] for b in range(2)]

            def scores(u, b):
                qb, h = u // 2, u % 2
                r = slice(C * h, C * h + C)
                nk = P * (qb + 1)
                if u >= 2:
                    pe.wait_ge(S["s_read"], t.val("s_done", -1))
                st = s_set(u)
                Qs, Ks = QK[b]
                for n0 in range(0, nk, 512):
                    n1 = min(nk, n0 + 512)
                    nc.tensor.matmul(st[:, n0 // 512, 0:n1 - n0], Qs[r, P0 + P * qb:P0 + P * qb + P],
                                     Ks[r, P0 + n0:P0 + n1], start=True, stop=True)
                o = (nk - P) % 512
                nc.tensor.matmul(st[:, (nk - P) // 512, o:o + P], identb[:, :], causb[:, 0:P],
                                 start=False, stop=True, skip_group_check=True).then_inc(S["s_done"], 1)
                t.up("s_done")

            def turn_exp(u):
                pe.wait_ge(S["e_ready"], t.up("e_ready"))
                for blk in range(u // 2 + 1):
                    ins = nc.tensor.transpose(PTp[blk // 4][:, P * (blk % 4):P * (blk % 4) + P],
                                              EXP[u % 2][:, P * blk:P * blk + P], k("ident"))
                ins.then_inc(S["pt_done"], 1)
                t.up("pt_done")

            def values(u, b):
                qb, h = u // 2, u % 2
                pe.wait_ge(S["pt_read"], t.val("pt_done"))
                if u >= 2:
                    pe.wait_ge(S["o_read"], t.val("o_done", -1))
                if h and qb:
                    pe.wait_ge(S["ot_read"], t.val("ot_done"))
                for blk in range(qb + 1):
                    ins = nc.tensor.matmul(ps[:, 6 + h, 0:C], PT[u % 2][:, P * blk:P * blk + P],
                                           VP[b][:, blk, C * h:C * h + C], start=(blk == 0), stop=(blk == qb))
                ins.then_inc(S["o_done"], 1)
                t.up("o_done")

            def turn():
                pe.wait_ge(S["o_read"], t.val("o_done"))
                nc.tensor.transpose(ps[:, 7, 0:P], OT, k("ident")).then_inc(S["ot_done"], 1)
                t.up("ot_done")

            pe.wait_ge(S["read0"], t.val("read0"))
            pe.wait_ge(S["read1"], t.val("read1"))
            with t.loop(2, s_done=32, e_ready=32, pt_done=32, o_done=32, ot_done=16, staged=2):
                for b in range(2):
                    pe.wait_ge(S["staged"], t.up("staged"))
                    scores(0, b)
                    scores(1, b)
                    for u in range(16):
                        turn_exp(u)
                        if u + 2 < 16:
                            scores(u + 2, b)
                        if u % 2 == 0 and u:
                            turn()
                        values(u, b)
                    turn()

            pe.wait_ge(S["ot_read"], t.val("ot_done"))
            with t.loop(2, s_done=6, e_ready=2, pt_done=6, o_done=2, ot_done=2, staged=2, kv_in0=64, kv_in1=64):
                for b in range(2):
                    Kc, Vc, Es, sm = CK[b], CV[b], EXPS[b], SM[b]
                    Qn, Kn, Vn, OTs = sm[:, 0:P], sm[:, P:P + C], sm[:, P + C:2 * P + C], sm[:, 2 * P + C:3 * P]
                    pe.wait_ge(S["staged"], t.up("staged"))
                    pe.wait_ge(S[f"kv_in{b}"], t.up(f"kv_in{b}", 64))
                    for piece in range(3):
                        pe.wait_ge(S["s_read"], t.val("s_done", -1))
                        st = ps[:, 2 * (piece % 2):2 * (piece % 2) + 2, :]
                        if piece < 2:
                            for n in range(2):
                                ins = nc.tensor.matmul(st[:, n, :], Qn, Kc[:, 1024 * piece + 512 * n:1024 * piece + 512 * n + 512],
                                                       start=True, stop=True)
                        else:
                            nc.tensor.matmul(st[:, 0, 0:C], Qn, Kn, start=True, stop=False)
                            ins = nc.tensor.matmul(st[:, 0, 0:C], identb[:, :], causb[:, P:P + C], start=False, stop=True)
                        ins.then_inc(S["s_done"], 1)
                        t.up("s_done")
                    pe.wait_ge(S["e_ready"], t.up("e_ready"))
                    for part in range(3):
                        pe.wait_ge(S["pt_read"], t.val("pt_done"))
                        pe.sem_inc(S["held"], 1)
                        for blk in range(8 * part, min(17, 8 * part + 8)):
                            n = P if blk < 16 else C
                            ins = nc.tensor.transpose(PTp[blk % 8 // 4][0:n, P * (blk % 4):P * (blk % 4) + P],
                                                      Es[:, P * blk:P * blk + n], k("ident"))
                        ins.then_inc(S["pt_done"], 1)
                        t.up("pt_done")
                    pe.wait_ge(S["pt_read"], t.val("pt_done"))
                    pe.wait_ge(S["o_read"], t.val("o_done"))
                    for h in range(2):
                        r = slice(C * h, C * h + C)
                        for blk in range(17):
                            n = P if blk < 16 else C
                            vb = Vc[:, blk, r] if blk < 16 else Vn[0:C, r]
                            ins = nc.tensor.matmul(ps[r, 6, 0:C], PTL[0:n, P * blk + C * h:P * blk + C * h + C], vb,
                                                   start=(blk == 0), stop=(blk == 16), skip_group_check=True)
                    ins.then_inc(S["o_done"], 1)
                    t.up("o_done")
                    pe.wait_ge(S["o_read"], t.val("o_done"))
                    pe.wait_ge(S["ot_read"], t.val("ot_done"))
                    pe.sem_inc(S["held"], 1)
                    nc.tensor.transpose(ps[0:C, 7, 0:P], OTs, k("ident")).then_inc(S["ot_done"], 1)
                    t.up("ot_done")
            pe.wait_ge(S["ot_read"], t.val("ot_done"))

            def output_projection():
                enter(t, "out")
                split_units(KT, [Br[:, j, :] for j in range(KT)], [Br[:, 8 + j, :] for j in range(KT)])

            output_projection()

            def channel_mixer():
                enter(t, "mixer")
                norm()
                t.up("normed", KT)
                norm_direct()
                t.up("normed", KT)
                xl, xh = ([x[:, j, :] for j in range(KT)] for x in (Ar, Hr))
                split_units(2 * NF, xh, xl)
                pe.wait_ge(S["read0"], t.val("read0"))
                pe.wait_ge(S["read1"], t.val("read1"))
                mid = [B[:, j, :] for j in range(NF)]
                with t.loop(KT // 2, chunk=4, w_used=4, mm_done=2, read0=1, read1=1, w0=16, w1=16, w2=16, w3=16):
                    for j in range(2):
                        unit([HALF, HALF], mid)
                norm()
                t.up("normed", KT)
                norm_direct()
                t.up("normed", KT)
                xh = [Br[:, NP_ + j, :] for j in range(KT)]
                for j in range(2):
                    split_unit(xh, xl, arriving=(j == 0))
                    if j == 0:
                        pe.wait_ge(S["p_in"], t.up("p_in", 16))
                    unit([NP_], [B[:, 0, :], B[:, 1, :]])
                with t.loop(KT // 2 - 1, chunk=4, w_used=4, wl_ready=2, wh=2, mm_done=4, read0=2, read1=2,
                            w0=16, w1=16, w2=16, w3=16):
                    for j in range(2):
                        split_unit(xh, xl)
                        unit([NP_], [B[:, 0, :], B[:, 1, :]])

            channel_mixer()
            if stop < 2:
                return

            norm_direct()
            t.up("normed", KT)
            X = [[B[:, 8 * b + j, :] for j in range(KT)] for b in range(2)]

            def lora(b, first, rows, out):
                pe.wait_ge(S["xn_ready"], t.up("xn_ready", KT))
                unit([KT], X[b], cols=rows)
                s = (t.n["mm_done"] - 1) % 2
                pe.wait_ge(S[f"read{s}"], t.val(f"read{s}"))
                w = t.n.get("chunk", 0)
                slot = w % SLOTS
                t.up("chunk")
                t.up("w_used")
                pe.wait_ge(S[f"w{slot}"], t.up(f"w{slot}", 16))
                for m in range(KT):
                    s, mm, rd = t.unit()
                    pe.wait_ge(S[f"read{s}"], t.val(f"read{s}", -1))
                    for c in range(NCH):
                        ins = nc.tensor.matmul(ps[:, NCH * s + c, 0:CH], W[0:rows, slot, m * P:(m + 1) * P],
                                               out[0:rows, c * CH:(c + 1) * CH], start=True, stop=True)
                        if m == 0 and c == 0:
                            first_use(ins)
                    ins.then_inc(S["mm_done"], 1)

            lora(0, 0, C, B[:, 16, :])
            lora(1, 0, C, B[:, 17, :])
            lora(0, 0, P, B[:, 16, :])
            for n in range(2):
                pe.wait_ge(S["xn_ready"], t.up("xn_ready", KT))
                xs = X[(n + 1) % 2]
                dense8(KT)
            pe.wait_ge(S["xn_ready"], t.up("xn_ready", KT))
            xs = X[1]
            with t.loop(2, mm_done=12, read0=6, read1=6, key_sq=4, rk_ready=4, chunk=4, w_used=4, w0=16, w1=16, w2=16, w3=16):
                for u in range(4):
                    pe.wait_ge(S["key_sq"], t.up("key_sq"))
                    sums(k("pair"), TM[:, 1, :])
                    unit([KT], xs)
                    pe.wait_ge(S["rk_ready"], t.up("rk_ready"))
                    sums(k("pair"), TM[:, 2, :])

            for s in range(2):
                pe.wait_ge(S[f"read{s}"], t.val(f"read{s}"))

            def heads(g):
                return ((4 * g + a, a, h, slice(C * h, C * h + C)) for a in range(4) for h in range(2))

            def gram(u, g, pairs=slice(0, 4)):
                ZB, ZA, ZV = Z[u]
                for p, a, h, r in list(heads(g))[2 * pairs.start:2 * pairs.stop]:
                    ins = nc.tensor.matmul(ps[:, 4 + 2 * g + h, P * a:P * a + P],
                                           ZB[r, p, C * h:C * h + P], ZA[r, p, C * h:C * h + P],
                                           start=True, stop=True)
                if pairs.stop == 4:
                    ins.then_inc(S["g_done"], 1)

            def token_major(u, g):
                ZB, ZA, ZV = Z[u]
                pe.wait_ge(S["g_ready"], t.up("g_ready"))
                pe.sem_inc(S["held"], 1)
                for p, a, h, r in heads(g):
                    for j, z in enumerate((ZB, ZV)):
                        o = P * a + C * j
                        ins = nc.tensor.transpose(ps[:, 4 + 2 * g + h, o:o + C],
                                                  z[r, p, C * h:C * h + P], k("ident")[r, r])
                ins.then_inc(S["tok_done"], 1)

            def full_clock(n):
                for _ in range(n):
                    nc.tensor.matmul(ps[:, 0, :], k("ident"), cst[:, 0:4 * P], start=True, stop=True)

            def turn_n(u, groups=(0, 1)):
                for g in groups:
                    pe.wait_ge(S["tok_read"], t.up("tok_read", 2))
                    pe.sem_inc(S["held"], 1)
                    for p, a, h, r in heads(g):
                        if h:
                            ins = nc.tensor.transpose(ps[:, 4 + 2 * g, P * a:P * a + P], Gs[u][:, p, C:C + P],
                                                      k("ident"))
                    ins.then_inc(S["n_done"], 1)

            def state_and_values(g, ZA, G, uv):
                for p, a, h, r in heads(g):
                    o = 256 + C * a
                    nc.tensor.matmul(ps[r, 2 * g + 1, o:o + C], G[:, p, P * h + C - C * h:P * h + P - C * h],
                                     uv[:, p, r], start=True, stop=False, skip_group_check=True)
                    ins = nc.tensor.matmul(ps[r, 2 * g + 1, o:o + C], ZA[:, p, C:2 * C],
                                           ST[:, p, r], start=False, stop=True, skip_group_check=True)
                ins.then_inc(S["a_done"], 1)

            def chunk(u, more=True):
                ZB, ZA, ZV = Z[u]
                G, M, bk, uv = Gs[u], Ms[u], BK[u], UV[u]
                for l in range(NL):
                    for g in range(2):
                        pe.wait_ge(S["m0_ready" if l == 0 else "m_ready"], t.up("m0_ready" if l == 0 else "m_ready"))
                        if l == 1:
                            pe.wait_ge(S["a_ready"], t.up("a_ready"))
                        pe.sem_inc(S["held"], 1)
                        for p, a, h, r in heads(g):
                            if h:
                                ins = nc.tensor.transpose(ps[:, 2 * g + 1, P * a:P * a + P], M[:, p, :], k("ident"))
                        ins.then_inc(S["mt_done"], 1)
                        if l == 0:
                            pe.wait_ge(S["n_ready"], t.up("n_ready"))
                            pe.sem_inc(S["held"], 1)
                        for p, a, h, r in heads(g):
                            ins = nc.tensor.matmul(ps[r, 2 * g, C * a:C * a + C], AB[u][r, p, :], M[r, p, r],
                                                   start=True, stop=True)
                        ins.then_inc(S["y_done"], 1)
                    if more and l == 2:
                        pe.wait_ge(S["z_dup"], t.up("z_dup"))
                        pe.sem_inc(S["held"], 1)
                        gram(1 - u, 0)
                    elif more and l == 3:
                        gram(1 - u, 1, slice(2, 4))
                    elif more and l == 4:
                        token_major(1 - u, 1)
                    for g in range(2):
                        pe.wait_ge(S["mt_ready"], t.up("mt_ready"))
                        if l == 0 and g == 0:
                            pe.wait_ge(S["c_in"], t.up("c_in", 2))
                            state_and_values(0, ZA, G, uv)
                        pe.wait_ge(S["y_ready"], t.up("y_ready"))
                        pe.sem_inc(S["held"], 1)
                        for p, a, h, r in heads(g):
                            ins = nc.tensor.matmul(ps[r, 2 * g, 256 + C * a:256 + C * a + C], MT[r, p, :], Y[r, p, :],
                                                   start=True, stop=True)
                        ins.then_inc(S["z_done"], 1)
                    if l == 0:
                        state_and_values(1, ZA, G, uv)
                    elif more and l == 2:
                        gram(1 - u, 1, slice(0, 2))
                    elif more and l == 3:
                        token_major(1 - u, 0)
                if more:
                    turn_n(1 - u, (0,))
                for g in range(2):
                    pe.wait_ge(S["m_ready"], t.up("m_ready"))
                    pe.sem_inc(S["held"], 1)
                    for p, a, h, r in heads(g):
                        o = 256 + C * a
                        ins = nc.tensor.matmul(ps[r, 2 * g + 1, o:o + C], M[r, p, r], P1[r, p, :],
                                               start=True, stop=True)
                    ins.then_inc(S["u_done"], 1)
                for g in range(2):
                    pe.wait_ge(S["u_ready"], t.up("u_ready"))
                    for p, a, h, r in heads(g):
                        o = C * a
                        nc.tensor.matmul(ps[r, 2 * g, o:o + C], uv[:, p, r], G[:, p, P * h + C * h:P * h + C * h + C],
                                         start=True, stop=False, skip_group_check=True)
                        ins = nc.tensor.matmul(ps[r, 2 * g, o:o + C], ST[:, p, r], ZA[:, p, 0:C],
                                               start=False, stop=True, skip_group_check=True)
                    ins.then_inc(S["oo_done"], 1)
                    for p, a, h, r in heads(g):
                        o = C * a
                        ins = nc.tensor.matmul(ps[r, 2 * g + 1, o:o + C], bk[:, p, r], uv[:, p, r],
                                               start=True, stop=True, skip_group_check=True)
                    ins.then_inc(S["st_done"], 1)
                if more:
                    turn_n(1 - u, (1,))
                pe.wait_ge(S["oo_read"], t.up("oo_read", 2))
                pe.wait_ge(S["st_read"], t.up("st_read", 2))

            per = dict(z_dup=2, tok_read=8, n_ready=4, m0_ready=4, m_ready=4 * NL, mt_ready=4 * NL, y_ready=4 * NL,
                       a_ready=4, u_ready=4, c_in=4, oo_read=4, st_read=4, g_ready=4)
            pe.wait_ge(S["st_ready"], 1)
            pe.wait_ge(S["z_dup"], t.up("z_dup"))
            full_clock(5)
            for g in range(2):
                gram(0, g)
            for g in range(2):
                token_major(0, g)
            turn_n(0)
            with t.loop(NCHUNK // 2, **per):
                chunk(0)
                chunk(1)
            full_clock(11)
            pe.wait_ge(S["state_in"], 32)
            chunk(0, more=False)

            def mean(i):
                sums(k("pair"), A[:, i, :])

            mean(0)
            for i in range(NPAIR):
                if i + 1 < NPAIR:
                    mean(i + 1)
                pe.wait_ge(S["dev_sq"], t.up("dev_sq"))
                sums(k("pair"), TM[:, 1, :])
            pe.wait_ge(S["gn_ready"], NPAIR)
            output_projection()
            channel_mixer()

        @block.scalar
        def _(act):
            t = Tally(act)

            def square(src, needs=None):
                j = t.n.get("sq_ready", 0) % 2
                if t.some("sq_ready", -1):
                    act.wait_ge(S["sq_used"], t.val("sq_ready", -1))
                nc.scalar.activation(TM[:, j, :], src, ACT.Square).then_inc(S["sq_ready"], 1)
                t.up("sq_ready")

            def root(scale=1.0 / D, e=0):
                s, mm, rd = t.unit()
                act.wait_ge(S["mm_done"], mm)
                nc.scalar.activation(c3(TM[:, 3, :]), pset(s), ACT.Sqrt, scale=scale,
                                     bias=eps[:, e:e + 1]).then_inc(S[f"read{s}"], 1)

            def copy_unit(dst, cols=P, func=ACT.Copy, **kw):
                s, mm, rd = t.unit()
                act.wait_ge(S["mm_done"], mm)
                nc.scalar.activation(c3(dst)[0:cols], pset(s)[0:cols], func, **kw).then_inc(S[f"read{s}"], 1)
                return s, rd

            def upper(src, dst):
                for j in range(KT):
                    act.wait_ge(S["normed"], t.up("normed"))
                    nc.scalar.activation(dst[j], src[j], ACT.Copy).then_inc(S["xh_ready"], 1)

            def upper_of_block():
                for j in range(KT):
                    nc.scalar.activation(Br[:, j, :], B[:, 8 + j, :], ACT.Copy).then_inc(S["xh_ready"], 1)

            act.wait_ge(S["setup"], 96 + 4)
            act.wait_ge(S["x_in"], 16 * KT)
            for j in range(KT):
                square(H[:, j, :])
            root()
            upper([A[:, j, :] for j in range(KT)], [Hr[:, j, :] for j in range(KT)])
            Vt = Bf[:, 16 * T:16 * T + 9 * 512].rearrange("p (b n) -> p b n", b=9)
            for tt in range(9):
                s, mm, rd = t.unit()
                act.wait_ge(S["mm_done"], mm)
                n = P if tt < 8 else DEC
                nc.scalar.activation(Vt[0:n, tt, :], ps[0:n, NCH * s, :], ACT.Copy).then_inc(S[f"read{s}"], 1)
            with t.loop(2, mm_done=4, read0=2, read1=2) as i:
                for j in range(4):
                    copy_unit(B[:, bass.ds(i * 4 + j, 1), :].rearrange("p a n -> p (a n)"))
            t.skip(1)
            for c in range(NA):
                if t.some("ax_ready"):
                    act.wait_ge(S["tm_free"], t.val("ax_ready"))
                s, mm, rd = t.unit()
                act.wait_ge(S["mm_done"], mm)
                nc.scalar.activation(c3(TM[:, 0, :]), pset(s), ACT.Copy).then_inc(S[f"read{s}"], 1)
                t.up("ax_ready")
                t.skip(2)

            z, e = B[0:HF, 15, :], Af[0:HF, 0:T]
            act.wait_ge(S["dve_p"], t.up("dve_p"))
            act.wait_ge(S["mm_done"], t.val("mm_done"))
            nc.scalar.activation(e, z, ACT.Abs).then_inc(S["act_step"], 1)
            act.wait_ge(S["act_step"], t.up("act_step"))
            nc.scalar.activation(e, e, ACT.Exp, scale=-1.0).then_inc(S["act_step"], 1)
            act.wait_ge(S["act_step"], t.up("act_step"))
            nc.scalar.activation(e, e, ACT.Ln, bias=1.0).then_inc(S["act_p"], 1)
            t.up("act_p")

            PTp = ps[:, 4:6, :].rearrange("p b n -> p (b n)")

            def exp(u, E, total):
                act.wait_ge(S["p_ready"], t.up("p_ready"))
                nc.scalar.activation(E, E, ACT.Exp, scale=0.125, bias=mx[:, 2 * u + 1:2 * u + 2],
                                     accum_out=mx[:, total:total + 1]).then_inc(S["e_ready"], 1)
                t.up("e_ready")

            def exp_of(u):
                exp(u % 2, EXP[u % 2][:, 0:P * (u // 2 + 1)], SUMS + u % 4)

            def turned(u):
                n = P * (u // 2 + 1)
                act.wait_ge(S["pt_done"], t.up("pt_done"))
                if u >= 2:
                    act.wait_ge(S["o_done"], t.val("o_done", -1))
                nc.scalar.activation(PT[u % 2][:, 0:n], PTp[:, 0:n], ACT.Copy).then_inc(S["pt_read"], 1)
                t.up("pt_read")

            def output_block(pair, qb):
                act.wait_ge(S["ot_done"], t.up("ot_done"))
                nc.scalar.activation(B[:, bass.ds(pair + 12, 1), P0 + P * qb:P0 + P * qb + P].rearrange("p a n -> p (a n)"),
                                     ps[:, 7, 0:P], ACT.Copy).then_inc(S["ot_read"], 1)
                t.up("ot_read")

            with t.loop(2, p_ready=32, e_ready=32, pt_done=32, pt_read=32, o_done=32, ot_done=16, ot_read=16) as i:
                for b in range(2):
                    pair = i * 2 + b
                    exp_of(0)
                    exp_of(1)
                    for u in range(16):
                        turned(u)
                        if u + 2 < 16:
                            exp_of(u + 2)
                        if u % 2 == 0 and u:
                            output_block(pair, u // 2 - 1)
                        t.up("o_done")
                    output_block(pair, 7)
            with t.loop(2, p_ready=2, e_ready=2, pt_done=6, pt_read=6, o_done=2, ot_done=2, ot_read=2) as i:
                for b in range(2):
                    exp(0, EXPS[b], SUMS)
                    for part in range(3):
                        act.wait_ge(S["pt_done"], t.up("pt_done"))
                        act.wait_ge(S["o_done"], t.val("o_done"))
                        if part < 2:
                            nc.scalar.activation(PTL[:, 1024 * part:1024 * part + 1024], PTp[:, :],
                                                 ACT.Copy).then_inc(S["pt_read"], 1)
                        else:
                            nc.scalar.activation(PTL[0:C, 2048:2048 + P], PTp[0:C, 0:P],
                                                 ACT.Copy).then_inc(S["pt_read"], 1)
                        t.up("pt_read")
                    t.up("o_done")
                    act.wait_ge(S["ot_done"], t.up("ot_done"))
                    for h in range(2):
                        ins = nc.scalar.activation(
                            B[C * h:C * h + C, bass.ds(i * 2 + (12 + b), 1), S0:T].rearrange("p a n -> p (a n)"),
                            ps[0:C, 7, C * h:C * h + C], ACT.Copy)
                    ins.then_inc(S["ot_read"], 1)
                    t.up("ot_read")

            def output_tiles(count):
                for j in range(count):
                    s, mm, rd = t.unit()
                    act.wait_ge(S["mm_done"], mm)
                    nc.scalar.activation(c3(A[:, j, :]), pset(s), ACT.Copy).then_inc(S[f"read{s}"], 1)
                    act.wait_ge(S[f"read{s}"], rd)
                    square(A[:, j, :])

            def post_and_pre():
                root()
                for j in range(KT):
                    act.wait_ge(S["h_ready"], t.up("h_ready"))
                    square(H[:, j, :])
                root()

            def channel_mixer(l):
                output_tiles(KT)
                post_and_pre()
                t.n["normed"] = NORMED[l]
                act.wait_ge(S["h_out"], KT * 16 * (l + 1))
                upper([A[:, j, :] for j in range(KT)], [Hr[:, j, :] for j in range(KT)])
                with t.loop(NF // 2, mm_done=4, read0=2, read1=2) as i:
                    for j in range(2):
                        s, mm, rd = t.unit()
                        act.wait_ge(S["mm_done"], mm)
                        act.wait_ge(S[f"read{1 - s}"], t.val(f"read{1 - s}", -1))
                        nc.scalar.activation(c3(TM[:, j, :]), pset(s), ACT.Silu).then_inc(S[f"read{s}"], 1)
                        t.skip(1)
                output_tiles(KT)
                post_and_pre()
                t.n["normed"] = NORMED[l] + 2 * KT
                upper([A[:, j, :] for j in range(KT)], [Br[:, NP_ + j, :] for j in range(KT)])
                with t.loop(KT // 2, mm_done=4, read0=2, read1=2, h_ready=2) as i:
                    for j in range(2):
                        s, mm, rd = t.unit()
                        act.wait_ge(S["mm_done"], mm)
                        act.wait_ge(S["h_ready"], t.val("h_ready", -1))
                        nc.scalar.activation(c3(TM[:, j, :]), pset(s), ACT.Sigmoid).then_inc(S[f"read{s}"], 1)
                        t.up("h_ready")
                        t.skip(1)

            act.wait_ge(S["ot_read"], t.val("ot_read"))
            upper_of_block()
            channel_mixer(0)
            if stop < 2:
                return

            act.wait_ge(S["h_ready"], t.val("h_ready"))
            for j in range(KT):
                square(H[:, j, :])
            root()
            act.wait_ge(S["dve_p"], t.up("dve_p"))

            def mix(n):
                for kt in range(KT):
                    j = t.n.get("xn_tmp", 0) % 2
                    if t.some("xn_tmp", -1):
                        act.wait_ge(S["xn_ready"], t.val("xn_tmp", -1))
                    nc.scalar.activation(TM[:, j, :], A[:, kt, :], ACT.Copy,
                                         scale=mub[:, n, kt:kt + 1]).then_inc(S["xn_tmp"], 1)
                    t.up("xn_tmp")

            def stage_first(func, bias):
                for n in range(KT):
                    j = n % 4
                    s, mm, rd = t.unit()
                    act.wait_ge(S["mm_done"], mm)
                    if n >= 4:
                        t.up(f"xs{j}", 16)
                        act.wait_ge(S[f"xs{j}"], t.val(f"xs{j}"))
                    nc.scalar.activation(c3(B[:, 18 + j, :]), pset(s), func,
                                         bias=v1(bias, n)).then_inc(S[f"read{s}"], 1)

            def stage(func=ACT.Copy, bias=None):
                with t.loop(2, mm_done=4, read0=2, read1=2, xs0=16, xs1=16, xs2=16, xs3=16) as i:
                    for j in range(4):
                        s, mm, rd = t.unit()
                        act.wait_ge(S["mm_done"], mm)
                        act.wait_ge(S[f"xs{j}"], t.val(f"xs{j}"))
                        t.up(f"xs{j}", 16)
                        kw = dict(bias=vec[:, V[bias], bass.ds(i * 4 + j, 1)]) if bias else {}
                        nc.scalar.activation(c3(B[:, 18 + j, :]), pset(s), func, **kw).then_inc(S[f"read{s}"], 1)

            def hidden(slot, rows, func):
                s, mm, rd = t.unit()
                act.wait_ge(S["mm_done"], mm)
                nc.scalar.activation(c3(B[:, slot, :])[0:rows], pset(s)[0:rows], func).then_inc(S[f"read{s}"], 1)

            mix(1)
            hidden(16, C, ACT.Tanh)
            mix(4)
            stage_first(ACT.Sigmoid, "w0")
            for j in range(4):
                t.up(f"xs{j}", 16)
            hidden(17, C, ACT.Copy)
            mix(5)
            stage(ACT.Sigmoid, bias="a0")
            hidden(16, P, ACT.Sigmoid)
            mix(0)
            stage()
            mix(2)
            stage()
            mix(3)
            stage()

            act.wait_ge(S["xn_ready"], t.val("xn_tmp"))
            with t.loop(2, l_in0=2 * 64, l_in1=2 * 64, act_p=16, dve_p=8, mm_done=12, read0=6, read1=6, key_scaled=4,
                        key_sq=4, rn_used=4, xs0=16, xs1=16, xs2=16, xs3=16) as i:
                for u in range(4):
                    pair, key, L = i * 4 + u, key2[u % 2], Lb[u % 2]
                    act.wait_ge(S[f"l_in{u % 2}"], t.up(f"l_in{u % 2}", 64))
                    nc.scalar.activation(key, L["k"], ACT.Copy,
                                         scale=vec[:, V["kk"], bass.ds(pair, 1)]).then_inc(S["key_scaled"], 1)
                    act.wait_ge(S["key_scaled"], t.up("key_scaled"))
                    nc.scalar.activation(TM[:, 1, :], key, ACT.Square).then_inc(S["key_sq"], 1)
                    t.up("key_sq")
                    nc.scalar.activation(L["w"], L["w"], ACT.Copy, scale=-DECAY).then_inc(S["act_p"], 1)
                    t.up("act_p")
                    s, mm, rd = t.unit()
                    act.wait_ge(S["mm_done"], mm)
                    act.wait_ge(S["rn_used"], t.up("rn_used"))
                    nc.scalar.activation(c3(TM[:, 3, :]), pset(s), ACT.Sqrt).then_inc(S[f"read{s}"], 1)
                    act.wait_ge(S["dve_p"], t.up("dve_p"))
                    nc.scalar.activation(expL, cumL, ACT.Exp).then_inc(S["act_p"], 1)
                    nc.scalar.activation(expnL, cumL, ACT.Exp, scale=-1.0).then_inc(S["act_p"], 1)
                    act.wait_ge(S["act_p"], t.up("act_p"))
                    t.up("act_p")
                    for c0, n, o in ((P0, NCHUNK, 0), (S0, 1, NCHUNK)):
                        nc.scalar.activation(eLC[:, bass.ds(pair, 1), o:o + n].rearrange("p a n -> p (a n)"),
                                             expL[:, c0 + C - 1:c0 + C * n:C], ACT.Copy)
                    act.wait_ge(S["dve_p"], t.up("dve_p"))
                    nc.scalar.activation(L["w"], L["w"], ACT.Exp).then_inc(S["act_p"], 1)
                    t.up("act_p")
                    s, mm, rd = t.unit()
                    act.wait_ge(S["mm_done"], mm)
                    act.wait_ge(S[f"xs{u}"], t.val(f"xs{u}"))
                    t.up(f"xs{u}", 16)
                    nc.scalar.activation(c3(B[:, 18 + u, :]), pset(s), ACT.Copy).then_inc(S[f"read{s}"], 1)
                    s, mm, rd = t.unit()
                    act.wait_ge(S["mm_done"], mm)
                    nc.scalar.activation(c3(TM[:, 2, :]), pset(s), ACT.Copy).then_inc(S[f"read{s}"], 1)

            def onto_diagonals(dst, src, g):
                for h in range(2):
                    r = slice(C * h, C * h + C)
                    ins = nc.scalar.activation(dst[r, 4 * g:4 * g + 4, r], src[r].rearrange("p (a n) -> p a n", a=4),
                                               ACT.Copy)
                return ins

            def off_diagonals(dst, bank, g):
                for h in range(2):
                    r = slice(C * h, C * h + C)
                    ins = nc.scalar.activation(dst[r, 4 * g:4 * g + 4, :],
                                               ps[r, bank, :].rearrange("p (a n) -> p a n", a=4)[:, :, r], ACT.Copy)
                return ins

            def token_major(u, g):
                act.wait_ge(S["tok_done"], t.up("tok_done"))
                for h in range(2):
                    nc.scalar.activation(BKUV[u][:, 4 * g:4 * g + 4, :, C * h:C * h + C],
                                         ps[:, 4 + 2 * g + h, :].rearrange("p (a j n) -> p a j n", a=4, j=2),
                                         ACT.Copy).then_inc(S["tok_read"], 1)

            def turn_n(u, groups=(0, 1)):
                for g in groups:
                    act.wait_ge(S["n_done"], t.up("n_done"))
                    off_diagonals(AB[u], 4 + 2 * g, g).then_inc(S["n_ready"], 1)

            def chunk(u, c0, more=True):
                for l in range(NL):
                    for g in range(2):
                        act.wait_ge(S["mt_done"], t.up("mt_done"))
                        off_diagonals(MT, 2 * g + 1, g).then_inc(S["mt_ready"], 1)
                    if l == 0:
                        for g in range(2):
                            act.wait_ge(S["a_done"], t.up("a_done"))
                            nc.scalar.activation(P1[:, 4 * g:4 * g + 4, :], four_of(2 * g + 1, 1),
                                                 ACT.Copy).then_inc(S["a_ready"], 1)
                    if l >= 3 and more:
                        token_major(1 - u, l - 3)
                for g in range(2):
                    act.wait_ge(S["u_done"], t.up("u_done"))
                    onto_diagonals(UV[u], ps[:, 2 * g + 1, 256:512], g).then_inc(S["u_ready"], 1)
                if more:
                    turn_n(1 - u, (0,))
                for g in range(2):
                    act.wait_ge(S["oo_done"], t.up("oo_done"))
                    dst = A[:, 4 * g:4 * g + 4, c0:c0 + C] if isinstance(c0, int) else A[:, 4 * g:4 * g + 4, bass.ds(c0, C)]
                    nc.scalar.activation(dst, four_of(2 * g, 0), ACT.Copy).then_inc(S["oo_read"], 1)
                if more:
                    turn_n(1 - u, (1,))

            act.wait_ge(S["st_ready"], 1)
            for g in range(2):
                token_major(0, g)
            turn_n(0)
            with t.loop(NCHUNK // 2, tok_done=4, n_done=4, mt_done=4 * NL, a_done=4, u_done=4, oo_done=4) as i:
                chunk(0, i * (2 * C) + P0)
                chunk(1, i * (2 * C) + (P0 + C))
            chunk(0, S0, more=False)

            def mean(i):
                t.unit()

            mean(0)
            for i in range(NPAIR):
                if i + 1 < NPAIR:
                    mean(i + 1)
                if i == 0:
                    act.wait_ge(S["state_out"], 1)
                act.wait_ge(S["mean_in"], i + 1)
                if i:
                    act.wait_ge(S["mm_done"], mm)
                nc.scalar.activation(TM[:, 1, :], B[:, 6 + i % 2, :], ACT.Square).then_inc(S["dev_sq"], 1)
                s, mm, rd = t.unit()
                act.wait_ge(S["mm_done"], mm)
                if i:
                    act.wait_ge(S["gn_used"], i)
                nc.scalar.activation(c3(TM[:, 2, :]), pset(s), ACT.Sqrt, scale=1.0 / C,
                                     bias=eps[:, 1:2]).then_inc(S[f"read{s}"], 1)
            act.wait_ge(S["gn_ready"], NPAIR)
            upper_of_block()
            channel_mixer(1)

        @block.vector
        def _(dve):
            t = Tally(dve)

            def step(ins):
                ins.then_inc(S["dve_step"], 1)
                dve.wait_ge(S["dve_step"], t.up("dve_step"))

            def stt(out, in0, scalar, in1, op0, op1):
                return nc.vector.scalar_tensor_tensor(out=out, in0=in0, scalar=scalar, in1=in1, op0=op0, op1=op1)

            def sum_squares(splitting=False):
                for j in range(KT):
                    dve.wait_ge(S["sq_ready"], t.up("sq_ready"))
                    if j == 0:
                        ins = nc.vector.tensor_copy(TM[:, 2, :], TM[:, 0, :])
                    else:
                        dve.wait_ge(S["sq_used"], t.val("sq_used"))
                        ins = nc.vector.tensor_tensor(TM[:, 2, :], TM[:, 2, :], TM[:, j % 2, :], ALU.add)
                    ins.then_inc(S["sq_used"], 1)
                    t.up("sq_used")
                    if splitting and j + 2 < KT:
                        split_chunk(j + 1 - KT)

            def rstd():
                s, mm, rd = t.unit()
                dve.wait_ge(S[f"read{s}"], rd)
                step(nc.vector.reciprocal(TM[:, 3, :], TM[:, 3, :]))

            def pre_norm(gain):
                t.up("sq_ready", KT)
                t.up("sq_used", KT)
                rstd()
                for j in range(KT):
                    stt(A[:, j, :], H[:, j, :], v1(gain, j), TM[:, 3, :], ALU.mult, ALU.mult).then_inc(S["normed"], 1)
                    t.up("normed")

            def split_chunk(off=0, n=KT * P):
                slot, landed = t.chunk()
                if t.some("mm_done", off):
                    dve.wait_ge(S["mm_done"], t.val("mm_done", off))
                dve.wait_ge(S[f"w{slot}"], landed)
                w, wh = W[:, slot, 0:n], wh_of(t)[:, 0:n]
                step(nc.vector.tensor_copy(wh, w))
                nc.vector.tensor_tensor(Wr[:, slot, 0:n], w, wh, ALU.subtract).then_inc(S["wl_ready"], 1)
                t.up("wl_ready")

            def pre_norm_split(gain, xh):
                t.up("sq_ready", KT)
                t.up("sq_used", KT)
                split_chunk()
                rstd()
                for j in range(KT + 1):
                    if j < KT:
                        stt(A[:, j, :], H[:, j, :], v1(gain, j), TM[:, 3, :], ALU.mult, ALU.mult).then_inc(S["normed"], 1)
                        t.up("normed")
                    if j:
                        dve.wait_ge(S["xh_ready"], t.up("xh_ready"))
                        nc.vector.tensor_tensor(Ar[:, j - 1, :], A[:, j - 1, :], xh[j - 1], ALU.subtract).then_inc(S["xl_ready"], 1)
                        t.up("xl_ready")

            def output_projection(l):
                enter(t, "out")
                t.n["chunk"] = t.n["w0"] = t.n["w1"] = t.n["w2"] = t.n["w3"] = 0
                t.skip_chunks(CHUNKS[l] - KT)
                split_chunk()
                for j in range(KT):
                    dve.wait_ge(S["xh_ready"], t.up("xh_ready"))
                    nc.vector.tensor_tensor(Br[:, 8 + j, :], B[:, 8 + j, :], Br[:, j, :], ALU.subtract).then_inc(S["xl_ready"], 1)
                    t.up("xl_ready")
                split_chunk()
                t.skip(KT)

            def post_norm(gain, splitting=False):
                sum_squares(splitting)
                rstd()
                dve.wait_ge(S["h_in"], t.val("h_in"))
                for j in range(KT):
                    stt(A[:, j, :], A[:, j, :], v1(gain, j), TM[:, 3, :], ALU.mult, ALU.mult).then_inc(S["normed"], 1)
                    dve.wait_ge(S["normed"], t.up("normed"))
                    nc.vector.tensor_tensor(H[:, j, :], H[:, j, :], A[:, j, :], ALU.add).then_inc(S["h_ready"], 1)
                    t.up("h_ready")

            dve.wait_ge(S["setup"], 96)
            nc.vector.memset(eps[:, 0:1], NORM_EPS)
            nc.vector.memset(eps[:, 1:2], GN_EPS).then_inc(S["setup"], 1)
            nc.vector.tensor_scalar(mub[:, :, :], vec[:, V["mu0"]:V["mu0"] + 6, :], -1.0, 1.0, ALU.mult,
                                    ALU.add).then_inc(S["setup"], 1)
            nc.vector.tensor_scalar(kab[:, :], vec[:, V["ka"], :], -1.0, 1.0, ALU.mult, ALU.add).then_inc(S["setup"], 1)
            nc.vector.tensor_copy(lvl[:, :, :].rearrange("p a n -> p (a n)"), TM[:, 3, 0:len(LEVELS) * C])
            nc.vector.tensor_copy(identb[:, :], k("ident"))
            nc.vector.tensor_copy(causb[:, :], cst[:, 3 * P:4 * P + C]).then_inc(S["setup"], 1)
            dve.wait_ge(S["x_in"], 16 * KT)
            dve.wait_ge(S["setup"], 100)
            dve.wait_ge(S["wv_in"], 16)
            step(nc.vector.tensor_copy(wvh, wv))
            nc.vector.tensor_tensor(wvl, wv, wvh, ALU.subtract).then_inc(S["wv_ready"], 1)
            enter(t, "first")
            pre_norm_split("pre0", [Hr[:, j, :] for j in range(KT)])
            split_chunk()
            t.skip(9)
            for c in range(2 * NA):
                t.unit()
                split_chunk(n=KT * HF if c + 2 == 2 * NA else KT * P)
            s, mm, rd = t.unit()
            dve.wait_ge(S["mm_done"], mm)
            nc.vector.tensor_scalar(c3(B[0:HF, 15, :]), pset(s)[0:HF], bf[:, 0:1], None,
                                    ALU.add).then_inc(S[f"read{s}"], 1)
            split_chunk()
            for c in range(NA):
                s, mm, rd = t.unit()
                dve.wait_ge(S[f"read{s}"], rd)
                split_chunk()
                s, mm, rd = t.unit()
                dve.wait_ge(S["mm_done"], mm)
                if c:
                    dve.wait_ge(S["conv_out"], 32 * c)
                nc.vector.tensor_tensor(c3(TM[:, 1, :]), pset(s), c3(TM[:, 0, :]), ALU.mult).then_inc(S[f"read{s}"], 1)
                dve.wait_ge(S[f"read{s}"], rd)
                nc.vector.memset(TM[:, 1, 0:PAD], 0.0).then_inc(S["dve_step"], 1)
                t.up("dve_step")
                nc.vector.tensor_copy(TM[:, 1, S0 - PAD:S0], convs[:, c, :]).then_inc(S["tm_free"], 1)
                dve.wait_ge(S["tm_free"], t.up("tm_free"))
                if c < NA - 1:
                    split_chunk()
                n = T - PAD
                step(nc.vector.tensor_scalar(TM[:, 2, PAD:T], TM[:, 1, 0:n], convw[:, 0, c:c + 1], None, ALU.mult))
                step(stt(TM[:, 2, PAD:T], TM[:, 1, 1:n + 1], convw[:, 1, c:c + 1], TM[:, 2, PAD:T], ALU.mult, ALU.add))
                step(stt(TM[:, 2, PAD:T], TM[:, 1, 2:T], convw[:, 2, c:c + 1], TM[:, 2, PAD:T], ALU.mult, ALU.add))
                step(nc.vector.memset(TM[:, 2, 0:PAD], 0.0))
                s, mm, rd = t.unit()
                dve.wait_ge(S["mm_done"], mm)
                nc.vector.tensor_tensor(c3(B[:, 8 + c, :]), pset(s), c3(TM[:, 2, :]), ALU.mult).then_inc(S[f"read{s}"], 1)
                dve.wait_ge(S[f"read{s}"], rd)
                if c < NA - 1:
                    split_chunk()
            z, e = B[0:HF, 15, :], Af[0:HF, 0:T]
            nc.vector.memset(B[:, 12:16, 0:PAD], 0.0)
            nc.vector.memset(B[:, 12:16, S0 - PAD:S0], 0.0).then_inc(S["dve_p"], 1)
            t.up("dve_p")
            dve.wait_ge(S["act_p"], t.up("act_p"))
            lf, zero = Af[0:HF, T:2 * T], Af[0:HF, 2 * T:2 * T + NALL]
            full, cum = Af[0:HF, 5000:5000 + NALL], Tf[0:HF, 0:NALL]
            cump = Tf[0:HF, NALL:NALL + SEQ]
            step(stt(lf, z, 0.0, e, ALU.min, ALU.subtract))
            step(nc.vector.memset(zero, 0.0))
            dve.wait_ge(S["cum_in"], t.up("cum_in", 16))
            step(nc.vector.tensor_copy(full[:, PAST:NALL], lf[:, S0:T]))
            nc.vector.tensor_tensor_scan(cump, lf[:, P0:P0 + SEQ], zero[:, 0:SEQ], 0.0, ALU.add, ALU.subtract)
            step(nc.vector.tensor_tensor_scan(cum, full, zero, 0.0, ALU.add, ALU.subtract))
            step(nc.vector.tensor_scalar(cump, cump, -8.0, None, ALU.mult))
            nc.vector.tensor_scalar(cum, cum, -8.0, None, ALU.mult).then_inc(S["cum_ready"], 1)

            def out_scaled(u, total, dst, src, turned):
                dve.wait_ge(S["e_ready"], t.up("e_ready"))
                step(nc.vector.reciprocal(mx[:, 6 + u % 2:7 + u % 2], mx[:, total:total + 1]))
                dve.wait_ge(S["o_done"], t.up("o_done"))
                if turned:
                    dve.wait_ge(S["ot_done"], t.val("ot_done"))
                nc.vector.tensor_scalar(dst, src, mx[:, 6 + u % 2:7 + u % 2], None, ALU.mult).then_inc(S["o_read"], 1)
                t.up("o_read")

            sc = ps[:, :, :].rearrange("p b n -> p (b n)")
            with t.loop(2, s_done=32, s_read=32, p_ready=32, e_ready=32, o_done=32, o_read=32, ot_done=16, ptd=32,
                        dve_step=32, bias_in0=32, bias_in1=32) as i:
                for b in range(2):
                    dve.wait_ge(S[f"bias_in{b}"], t.up(f"bias_in{b}", 32))
                    for u in range(18):
                        if u < 16:
                            qb, h = u // 2, u % 2
                            n = P * (qb + 1)
                            if u >= 2:
                                dve.wait_ge(S["pt_done"], t.val("ptd", -1))
                            t.up("ptd")
                            dve.wait_ge(S["s_done"], t.up("s_done"))
                            dve.sem_inc(S["held"], 1)
                            nc.vector.tensor_tensor_reduce(out=EXP[h][:, 0:n], in0=sc[:, 1024 * h:1024 * h + n],
                                                           in1=BIAS[b][:, h, 0:n],
                                                           scale=1.0, scalar=-3e38, op0=ALU.add, op1=ALU.max,
                                                           accum_out=mx[:, 2 * h:2 * h + 1]).then_inc(S["s_read"], 1)
                            dve.wait_ge(S["s_read"], t.up("s_read"))
                            nc.vector.tensor_scalar(mx[:, 2 * h + 1:2 * h + 2], mx[:, 2 * h:2 * h + 1], -0.125, None,
                                                    ALU.mult).then_inc(S["p_ready"], 1)
                            t.up("p_ready")
                        if u >= 2:
                            w = u - 2
                            out_scaled(w, SUMS + w % 4, OT[:, C * (w % 2):C * (w % 2) + C], ps[:, 6 + w % 2, 0:C], w // 2)
                            if w % 2:
                                t.up("ot_done")
            with t.loop(2, s_done=6, s_read=6, p_ready=2, e_ready=2, o_done=2, o_read=2, ot_done=2, dve_step=2,
                        kv_in0=64, kv_in1=64) as i:
                for b in range(2):
                    OTs = SM[b][:, 2 * P + C:3 * P]
                    dve.wait_ge(S[f"kv_in{b}"], t.up(f"kv_in{b}", 64))
                    for piece in range(3):
                        n = 1024 if piece < 2 else C
                        dve.wait_ge(S["s_done"], t.up("s_done"))
                        dve.sem_inc(S["held"], 1)
                        nc.vector.tensor_tensor_reduce(out=EXPS[b][:, 1024 * piece:1024 * piece + n],
                                                       in0=sc[:, 1024 * (piece % 2):1024 * (piece % 2) + n],
                                                       in1=BIASS[b][:, 1024 * piece:1024 * piece + n], scale=1.0,
                                                       scalar=-3e38 if piece == 0 else mx[:, 0:1],
                                                       op0=ALU.add, op1=ALU.max, accum_out=mx[:, 0:1]).then_inc(S["s_read"], 1)
                        dve.wait_ge(S["s_read"], t.up("s_read"))
                    nc.vector.tensor_scalar(mx[:, 1:2], mx[:, 0:1], -0.125, None, ALU.mult).then_inc(S["p_ready"], 1)
                    t.up("p_ready")
                    out_scaled(0, SUMS, OTs, ps[:, 6, 0:C], 0)
                    t.up("ot_done")
            t.up("h_in", 16)

            def channel_mixer(l):
                output_projection(l)
                post_norm(f"post{l}", splitting=True)
                enter(t, "mixer")
                t.n["chunk"] = t.n["w0"] = t.n["w1"] = t.n["w2"] = t.n["w3"] = 0
                t.skip_chunks(CHUNKS[l])
                pre_norm_split(f"fpre{l}", [Hr[:, j, :] for j in range(KT)])

                def mid_tiles(i, last):
                    for j in range(2):
                        split_chunk()
                        if not (last and j == 1):
                            split_chunk(1)
                        s, mm, rd = t.unit()
                        dve.wait_ge(S[f"read{s}"], rd)
                        s, mm, rd = t.unit()
                        dve.wait_ge(S["mm_done"], mm)
                        dst = B[:, NF - 2 + j, :] if last else B[:, bass.ds(i * 2 + j, 1), :].rearrange("p a n -> p (a n)")
                        nc.vector.tensor_tensor(c3(dst), pset(s), c3(TM[:, j, :]), ALU.mult).then_inc(S[f"read{s}"], 1)

                with t.loop(NF // 2 - 1, mm_done=4, read0=2, read1=2, chunk=4, w0=16, w1=16, w2=16, w3=16, wl_ready=4, wh=4,
                            dve_step=4) as i:
                    mid_tiles(i, False)
                mid_tiles(None, True)
                t.skip(KT)
                t.skip_chunks(2 * KT)
                t.up("h_in", 16)
                post_norm(f"fpost{l}")
                pre_norm_split(f"ple{l}", [Br[:, NP_ + j, :] for j in range(KT)])
                t.skip_chunks(1)

                def ple_tiles(i, last):
                    for j in range(2):
                        if not (last and j == 1):
                            split_chunk()
                            t.skip_chunks(1)
                        s, mm, rd = t.unit()
                        dve.wait_ge(S[f"read{s}"], rd)
                        s, mm, rd = t.unit()
                        dve.wait_ge(S["mm_done"], mm)
                        nc.vector.tensor_tensor(c3(TM[:, j, :]), pset(s), c3(TM[:, j, :]), ALU.mult).then_inc(S[f"read{s}"], 1)
                        dve.wait_ge(S[f"read{s}"], rd)
                        h = H[:, KT - 2 + j, :] if last else H[:, bass.ds(i * 2 + j, 1), :].rearrange("p a n -> p (a n)")
                        nc.vector.tensor_tensor(h, h, TM[:, j, :], ALU.add).then_inc(S["h_ready"], 1)
                        t.up("h_ready")

                with t.loop(KT // 2 - 1, mm_done=4, read0=2, read1=2, h_ready=2, chunk=4, w0=16, w1=16, w2=16, w3=16,
                            wl_ready=2, wh=2, dve_step=2) as i:
                    ple_tiles(i, False)
                ple_tiles(None, True)

            channel_mixer(0)
            if stop < 2:
                return

            pre_norm("pre1")
            dve.wait_ge(S["normed"], t.val("normed"))
            for g, c in enumerate((S0 - PAD - 1, T - 1)):
                ins = nc.vector.tensor_copy(last[:, g, :], A[:, :, c:c + 1].rearrange("p a n -> p (a n)"))
            ins.then_inc(S["shift_in"], 1)
            nc.vector.memset(A[:, :, P0 - 1:P0], 0.0)
            nc.vector.tensor_copy(A[:, :, S0 - 1:S0].rearrange("p a n -> p (a n)"), vec[:, V["shift"], :]).then_inc(S["dve_p"], 1)
            dve.wait_ge(S["dve_p"], t.up("dve_p"))
            mm0 = t.n["mm_done"]
            read_by = [mm0 + 1, mm0 + 10, mm0 + 19, mm0 + 35, mm0 + 43, mm0 + 51]
            nc.vector.memset(B[:, 0:16, 0:1], 0.0).then_inc(S["dve_step"], 1)
            dve.wait_ge(S["dve_step"], t.up("dve_step"))
            for order, n in enumerate((1, 4, 5, 0, 2, 3)):
                b = order % 2
                if order >= 2:
                    dve.wait_ge(S["mm_done"], read_by[order - 2])
                for kt in range(KT):
                    j = t.n.get("xn_tmp", 0) % 2
                    dve.wait_ge(S["xn_tmp"], t.up("xn_tmp"))
                    stt(B[:, 8 * b + kt, 1:T], A[:, kt, 0:T - 1], vec[:, V["mu0"] + n, kt:kt + 1], TM[:, j, 1:T],
                        ALU.mult, ALU.add).then_inc(S["xn_ready"], 1)
                    t.up("xn_ready")
            t.skip(43)

            dve.wait_ge(S["mm_done"], read_by[4])
            step(nc.vector.memset(reset, 1.0))
            nc.vector.memset(reset[:, P0:P0 + SEQ:C], 0.0)
            step(nc.vector.memset(reset[:, S0:S0 + 1], 0.0))

            def chunks(ap, n=P, o=0):
                v = ap.rearrange("p (c n) -> p c n", n=n)
                return v[:, 0:NCHUNK, o:o + C], v[:, NCHUNK, o:o + C]

            def tokens(ap):
                return ap[:, P0:P0 + SEQ].rearrange("p (c n) -> p c n", n=C), ap[:, S0:T]

            dve.sem_inc(S["rn_used"], 1)
            t.up("rn_used")
            with t.loop(2, l_in0=2 * 64, l_in1=2 * 64, act_p=16, dve_p=8, mm_done=12, read0=6, read1=6, dve_step=20,
                        key_scaled=4, rk_ready=4, rn_used=4, pair_stored=4, sum_stored=4, pair_done=4) as i:
                for u in range(4):
                    pair, key, L = i * 4 + u, key2[u % 2], Lb[u % 2]
                    dve.wait_ge(S[f"l_in{u % 2}"], t.up(f"l_in{u % 2}", 64))
                    step(nc.vector.tensor_scalar(tmpA, L["a"], vec[:, V["ka"], bass.ds(pair, 1)],
                                                 kab[:, bass.ds(pair, 1)], ALU.mult, ALU.add))
                    dve.wait_ge(S["key_scaled"], t.up("key_scaled"))
                    step(nc.vector.tensor_tensor(L["k"], tmpA, L["k"], ALU.mult))
                    dve.wait_ge(S["sum_stored"], t.up("sum_stored"))
                    stt(TM[:, 2, :], L["r"], vec[:, V["rk"], bass.ds(pair, 1)], L["k"], ALU.mult,
                        ALU.mult).then_inc(S["rk_ready"], 1)
                    t.up("rk_ready")
                    dve.wait_ge(S["act_p"], t.up("act_p"))
                    nc.vector.tensor_tensor_scan(cumL, reset, L["w"], 0.0, ALU.mult, ALU.add).then_inc(S["dve_p"], 1)
                    dve.wait_ge(S["dve_p"], t.up("dve_p"))
                    nc.vector.tensor_tensor(L["w"], cumL, L["w"], ALU.subtract).then_inc(S["dve_p"], 1)
                    t.up("dve_p")
                    s, mm, rd = t.unit()
                    dve.wait_ge(S[f"read{s}"], rd)
                    step(nc.vector.tensor_scalar(TM[:, 3, :], TM[:, 3, :], L2_EPS, None, ALU.max))
                    step(nc.vector.reciprocal(TM[:, 3, :], TM[:, 3, :]))
                    nc.vector.tensor_tensor(key, key, TM[:, 3, :], ALU.mult).then_inc(S["rn_used"], 1)
                    dve.wait_ge(S["rn_used"], t.up("rn_used"))
                    step(nc.vector.tensor_tensor(tmpA, key, L["a"], ALU.mult))
                    dve.wait_ge(S["pair_stored"], t.up("pair_stored"))
                    dve.wait_ge(S["act_p"], t.up("act_p"))
                    for dst, x, y in zip(chunks(ar_out, o=C), tokens(L["r"]), tokens(expL)):
                        nc.vector.tensor_tensor(dst, x, y, ALU.mult)
                    dve.wait_ge(S["act_p"], t.up("act_p"))
                    for dst, x, y in zip(chunks(bk_out), tokens(tmpA), tokens(expnL)):
                        nc.vector.tensor_tensor(dst, x, y, ALU.mult)
                    for dst, x, y in zip(chunks(bk_out, o=C), tokens(L["k"]), tokens(expnL)):
                        nc.vector.tensor_tensor(dst, x, y, ALU.mult)
                    dve.wait_ge(S["act_p"], t.up("act_p"))
                    for dst, x, y in zip(chunks(ar_out), tokens(key), tokens(L["w"])):
                        ins = stt(dst, x, -1.0, y, ALU.mult, ALU.mult)
                    ins.then_inc(S["pair_done"], 1)
                    dve.wait_ge(S["pair_done"], t.up("pair_done"))
                    t.skip(2)

            dve.wait_ge(S["pair_stored"], t.up("pair_stored"))
            dve.wait_ge(S["mm_done"], t.val("mm_done"))
            for u in range(2):
                nc.vector.memset(Z[u][2], 0.0)
            for c in (0, S0 - PAD):
                nc.vector.memset(A[:, :, c:c + PAD], 0.0)

            def four(ap, n=C):
                return ap.rearrange("p (a n) -> p a n", a=1).to_broadcast([ap.shape[0], 4, n])

            def init_m(u):
                for h in range(2):
                    r = slice(C * h, C * h + C)
                    ins = nc.vector.tensor_copy(Ms[u][r, :, r], k("ident2")[r].rearrange("p (a n) -> p a n", a=1)
                                                .to_broadcast([C, NPAIR, C]))
                ins.then_inc(S["m_init"], 1)

            for u in range(2):
                ins = nc.vector.memset(Ms[u], 0.0)
            step(ins)
            init_m(0)
            nc.vector.memset(ST, 0.0).then_inc(S["st_ready"], 1)
            dve.wait_ge(S["st_ready"], 1)
            for j in range(2):
                dve.sem_inc(S["c_in"], 1)

            def gram(u, g):
                dve.wait_ge(S["g_done"], t.up("g_done"))
                dve.sem_inc(S["held"], 1)
                for h in range(2):
                    r = slice(C * h, C * h + C)
                    bank = ps[:, 4 + 2 * g + h, :].rearrange("p (a n) -> p a n", a=4)
                    ins = nc.vector.copy_predicated(Ms[u][r, 4 * g:4 * g + 4, r], four(lvl[r, 0, :]), bank[r, :, C - C * h:P - C * h])
                ins.then_inc(S["m0_ready"], 1)
                for h, mask in enumerate(("gram_even", "gram_odd")):
                    bank = ps[:, 4 + 2 * g + h, :].rearrange("p (a n) -> p a n", a=4)
                    ins = nc.vector.tensor_tensor(Gs[u].rearrange("p a (h n) -> p a h n", h=2)[:, 4 * g:4 * g + 4, h, :],
                                                  bank, four(k(mask), P), ALU.mult)
                ins.then_inc(S["g_ready"], 1)

            def chunk(u, c, more=True):
                M = Ms[u]
                if more:
                    init_m(1 - u)
                for l in range(1, NL + 1):
                    for g in range(2):
                        dve.wait_ge(S["y_done"], t.up("y_done"))
                        nc.vector.tensor_copy(Y[:, 4 * g:4 * g + 4, :], four_of(2 * g, 0)).then_inc(S["y_ready"], 1)
                    for g in range(2):
                        dve.wait_ge(S["z_done"], t.up("z_done"))
                        dve.sem_inc(S["held"], 1)
                        for h in range(2):
                            r = slice(C * h, C * h + C)
                            ins = nc.vector.copy_predicated(M[r, 4 * g:4 * g + 4, r], four(lvl[r, l, :]),
                                                            four_of(2 * g, 1)[r])
                        ins.then_inc(S["m_ready"], 1)
                    if more and l in (3, 4):
                        if l == 3:
                            dve.wait_ge(S["m_init"], t.up("m_init"))
                        gram(1 - u, l - 3)
                for g in range(2):
                    dve.wait_ge(S["st_done"], t.up("st_done"))
                    for h in range(2):
                        r = slice(C * h, C * h + C)
                        st = ST[r, 4 * g:4 * g + 4, r]
                        ins = nc.vector.tensor_tensor(st, four_of(2 * g + 1, 0)[r], st, ALU.add)
                    ins.then_inc(S["st_read"], 1)
                    dve.wait_ge(S["st_read"], t.up("st_read"))
                    for h in range(2):
                        r = slice(C * h, C * h + C)
                        st = ST[r, 4 * g:4 * g + 4, r]
                        ins = nc.vector.tensor_tensor(st, st, eLC[r, 4 * g:4 * g + 4, c].to_broadcast([C, 4, C]), ALU.mult)
                    ins.then_inc(S["c_in"], 1)

            dve.wait_ge(S["m_init"], t.up("m_init"))
            for g in range(2):
                gram(0, g)
            per = dict(g_done=4, m_init=2, y_done=4 * NL, z_done=4 * NL, st_done=4, st_read=4)
            with t.loop(NCHUNK // 2, **per) as i:
                chunk(0, bass.ds(i * 2, 1))
                chunk(1, bass.ds(i * 2 + 1, 1))
            chunk(0, slice(NCHUNK, NCHUNK + 1), more=False)

            def mean(i):
                s, mm, rd = t.unit()
                dve.wait_ge(S["mm_done"], mm)
                if i >= 2:
                    dve.wait_ge(S["gn_ready"], i - 1)
                stt(c3(B[:, 6 + i % 2, :]), pset(s), -1.0 / C, c3(A[:, i, :]), ALU.mult, ALU.add).then_inc(S[f"read{s}"], 1)
                dve.wait_ge(S[f"read{s}"], rd)
                dve.sem_inc(S["mean_in"], 1)

            mean(0)
            for i in range(NPAIR):
                if i + 1 < NPAIR:
                    mean(i + 1)
                bonus, vv, gate = (B[:, 3 * (i % 2) + j, :] for j in range(3))
                dev, out = B[:, 6 + i % 2, :], B[:, 8 + i, :]
                dve.wait_ge(S[f"gn_in{i % 2}"], t.up(f"gn_in{i % 2}", 64))
                step(nc.vector.tensor_tensor(vv, bonus, vv, ALU.mult))
                s, mm, rd = t.unit()
                dve.wait_ge(S[f"read{s}"], rd)
                step(nc.vector.reciprocal(TM[:, 3, :], TM[:, 2, :]))
                stt(dev, dev, v1("lnw", i), TM[:, 3, :], ALU.mult, ALU.mult).then_inc(S["gn_used"], 1)
                dve.wait_ge(S["gn_used"], i + 1)
                step(stt(dev, dev, v1("lnb", i), vv, ALU.add, ALU.add))
                nc.vector.tensor_tensor(out, dev, gate, ALU.mult).then_inc(S["gn_ready"], 1)
            channel_mixer(1)

        @block.gpsimd
        def _(pool):
            t = Tally(pool)

            def store(dst, src):
                pool.dma_start(dst, src).then_inc(S["out_done"], 16)
                t.up("out_done", 16)

            t.skip(1)
            Vt = Bf[:, 16 * T:16 * T + 9 * 512].rearrange("p (b n) -> p b n", b=9)
            t.skip(9)
            pool.wait_ge(S["read0"], t.val("read0"))
            pool.wait_ge(S["read1"], t.val("read1"))
            store(O["v_p"], Vt[:, 0:8, :])
            store(O["v_s"], Vt[0:DEC, 8, :])
            n_v = t.n["out_done"]
            t.skip(8)
            pool.wait_ge(S["read0"], t.val("read0"))
            pool.wait_ge(S["read1"], t.val("read1"))
            store(O["k"], B[:, 4:8, :])
            t.skip(1)
            for c in range(NA):
                pool.wait_ge(S["tm_free"], t.up("tm_free"))
                pool.dma_start(O["conv"][:, c, 0:2], TM[:, 1, S0 - 2 * PAD:S0 - PAD]).then_inc(S["conv_out"], 16)
                pool.dma_start(O["conv"][:, c, 2:4], TM[:, 1, T - 2:T]).then_inc(S["conv_out"], 16)
                t.skip(3)
            pool.wait_ge(S["conv_out"], 32 * NA)
            pool.wait_ge(S["mm_done"], t.val("mm_done"))
            pool.dma_start(Af[0:HF, 5000:5000 + PAST], I["clogf"]).then_inc(S["cum_in"], 16)
            pool.wait_ge(S["cum_ready"], 1)
            store(O["logf"], Af[0:HF, T:2 * T])
            pool.dma_start(d_cum, Tf[0:HF, NALL:NALL + SEQ]).then_inc(S["cum_out"], 16)
            pool.dma_start(d_cums, Tf[0:HF, 0:NALL]).then_inc(S["cum_out"], 16)
            pool.wait_ge(S["cum_out"], 32)
            pool.wait_ge(S["out_done"], t.val("out_done"))

            d_c = d_cum.rearrange("(a h) n -> a h n", h=2)
            d_cs = d_cums.rearrange("(a h) n -> a h n", h=2)

            def stage_prompt(i):
                b = i % 2
                for h in range(2):
                    pool.dma_start(BIAS[b][:, h, :], d_c[i:i + 1, h, :].to_broadcast([P, SEQ])).then_inc(S[f"bias_in{b}"], 16)
                nc.gpsimd.tensor_copy(QK[b][0], B[:, i, :])
                nc.gpsimd.tensor_copy(QK[b][1], B[:, i + 4, :])
                nc.gpsimd.tensor_copy(VP[b], Vt[:, 0:8, i * P:i * P + P]).then_inc(S["staged"], 1)

            def sample_cache(i):
                b = i % 2
                pool.dma_start(CK[b], I["ck"][:, i, :]).then_inc(S[f"kv_in{b}"], 16)
                pool.dma_start(CV[b], I["cv"][:, :, i * P:i * P + P]).then_inc(S[f"kv_in{b}"], 16)

            def stage_sample(i):
                b = i % 2
                sm = SM[b]
                for h in range(2):
                    r = slice(C * h, C * h + C)
                    pool.dma_start(BIASS[b][r], d_cs[i:i + 1, h, :].to_broadcast([C, NALL])).then_inc(S[f"kv_in{b}"], 16)
                nc.gpsimd.tensor_copy(sm[0:C, 0:C], B[0:C, i, S0:T])
                nc.gpsimd.tensor_copy(sm[C:P, C:P], B[C:P, i, S0:T]).then_inc(S["pool_step"], 1)
                pool.wait_ge(S["pool_step"], t.up("pool_step"))
                nc.gpsimd.tensor_copy(sm[:, P:P + C], B[:, i + 4, S0:T]).then_inc(S["pool_step"], 1)
                pool.wait_ge(S["pool_step"], t.up("pool_step"))
                nc.gpsimd.tensor_copy(sm[0:DEC, P + C:2 * P + C], Vt[0:DEC, 8, i * P:i * P + P]).then_inc(S["staged"], 1)
                pool.wait_ge(S["staged"], NA + i + 1)

            stage_prompt(0)
            stage_prompt(1)
            for sm in SM:
                ins = nc.gpsimd.memset(sm[:, 0:P], 0.0)
            ins.then_inc(S["pool_step"], 1)
            pool.wait_ge(S["pool_step"], t.up("pool_step"))
            for i in range(NA):
                pool.wait_ge(S["ot_read"], t.up("ot_read", 8))
                if i + 2 < NA:
                    stage_prompt(i + 2)
                elif i + 2 == NA:
                    sample_cache(0)
            stage_sample(0)
            sample_cache(1)
            stage_sample(1)
            for i in range(NA):
                pool.wait_ge(S["ot_read"], t.up("ot_read"))
                if i + 2 < NA:
                    sample_cache(i + 2)
                    stage_sample(i + 2)
            pool.dma_start(H[:, :, :], I["x"]).then_inc(S["h_in"], 16)

            def lend_h(l):
                for j in range(KT):
                    pool.wait_ge(S["h_ready"], 24 * l + j + 1)
                    pool.dma_start(d_h[:, j, :], H[:, j, :]).then_inc(S["h_out"], 16)
                pool.wait_ge(S["mm_done"], t.val("mm_done") + KT + 2 + 2 * NF)
                pool.wait_ge(S["h_out"], 16 * KT * (l + 1))
                pool.dma_start(H[:, :, :], d_h).then_inc(S["h_in"], 16)
                t.skip(KT + 2 + 2 * NF + KT + 2 + 2 * KT)

            def finish_y():
                pool.wait_ge(S["h_ready"], 48)
                pool.sem_inc(S["held"], 1)
                store(O["y"], H[:, :, :])
                pool.wait_ge(S["out_done"], t.val("out_done"))

            lend_h(0)
            if stop < 2:
                pool.wait_ge(S["h_ready"], 24)
                pool.sem_inc(S["held"], 1)
                store(O["y"], H[:, :, :])
                pool.wait_ge(S["out_done"], t.val("out_done"))
                return

            pool.wait_ge(S["shift_in"], 1)
            store(O["shift"], last[:, :, :])

            UPTO = 1 + 9 + 8 + 1 + 3 * NA + KT + 2 + 2 * NF + KT + 2 + 2 * KT + 1
            t.n["mm_done"], t.n["read0"], t.n["read1"] = UPTO, (UPTO + 1) // 2, UPTO // 2

            def keep(name):
                with t.loop(2, mm_done=4, read0=2, read1=2, xs0=16, xs1=16, xs2=16, xs3=16) as i:
                    for j in range(4):
                        s, mm, rd = t.unit()
                        pool.wait_ge(S[f"read{s}"], rd)
                        pool.sem_inc(S["held"], 1)
                        pool.dma_start(d_x[name][bass.ds(i * 4 + j, 1)].rearrange("a p n -> (a p) n"),
                                       B[:, 18 + j, :]).then_inc(S[f"xs{j}"], 16)
                        t.up(f"xs{j}", 16)

            for name in "wag":
                t.skip(1)
                keep(name)
            for name in "rk":
                keep(name)
            for j in range(4):
                pool.wait_ge(S[f"xs{j}"], t.val(f"xs{j}"))
            pool.wait_ge(S["mm_done"], t.val("mm_done"))

            def load_pair(i):
                for n in "rkwa":
                    pool.dma_start(Lb[i % 2][n], d_x[n][i]).then_inc(S[f"l_in{i % 2}"], 16)

            load_pair(0)
            load_pair(1)
            pool.sem_inc(S["sum_stored"], 1)
            pool.sem_inc(S["pair_stored"], 1)
            for i in range(NPAIR):
                t.skip(1)
                s, mm, rd = t.unit()
                pool.wait_ge(S[f"read{s}"], rd)
                j = i % 4
                pool.dma_start(d_v[i, :, 0:SEQ], B[:, 18 + j, P0:P0 + SEQ]).then_inc(S[f"xv{j}"], 16)
                pool.dma_start(d_v[i, :, SEQ:SEQ + C], B[:, 18 + j, S0:T]).then_inc(S[f"xs{j}"], 16)
                t.up(f"xs{j}", 16)
                s, mm, rd = t.unit()
                pool.wait_ge(S[f"read{s}"], rd)
                pool.dma_start(d_x["sum"][i], TM[:, 2, :]).then_inc(S["sum_out"], 16)
                pool.wait_ge(S["sum_out"], 16 * i + 16)
                pool.sem_inc(S["sum_stored"], 1)
                pool.wait_ge(S["pair_done"], i + 1)
                pool.dma_start(d_bk[i], bk_out).then_inc(S["b_out"], 16)
                pool.dma_start(d_ar[i], ar_out).then_inc(S["b_out"], 16)
                if i + 2 < NPAIR:
                    load_pair(i + 2)
                pool.wait_ge(S["b_out"], 32 * i + 32)
                pool.sem_inc(S["pair_stored"], 1)
            for j in range(4):
                pool.wait_ge(S[f"xs{j}"], t.val(f"xs{j}"))
                pool.wait_ge(S[f"xv{j}"], 32)

            pool.wait_ge(S["st_ready"], 1)
            t.up("c_in", 2)

            def load_chunk(u, c):
                ZB, ZA, ZV = Z[u]
                for src, dst, n in ((d_bk, ZB[:, :, 0:P], P), (d_ar, ZA[:, :, C:C + P], P), (d_v, ZV[:, :, C:P], C)):
                    cols = slice(c * n, c * n + n) if isinstance(c, int) else bass.ds(c * n, n)
                    pool.dma_start(dst, src.rearrange("a p n -> p a n")[:, :, cols]).then_inc(S[f"zi{u}"], 16)
                pool.wait_ge(S[f"zi{u}"], t.up(f"zi{u}", 48))
                pool.sem_inc(S["held"], 1)
                nc.gpsimd.tensor_copy(ZB[:, :, P:P + C], ZB[:, :, 0:C])
                nc.gpsimd.tensor_copy(ZA[:, :, 0:C], ZA[:, :, P:P + C]).then_inc(S["z_dup"], 1)

            load_chunk(0, 0)
            with t.loop(NCHUNK // 2, c_in=4, zi0=48, zi1=48) as i:
                for u in range(2):
                    pool.wait_ge(S["c_in"], t.val("c_in"))
                    pool.sem_inc(S["held"], 1)
                    t.up("c_in", 2)
                    load_chunk(1 - u, i * 2 + (u + 1))
            pool.wait_ge(S["c_in"], t.val("c_in"))
            for h in range(2):
                r = slice(C * h, C * h + C)
                store(O["wkv"][r, 0], ST[r, :, C * h:C * h + C])
            pool.wait_ge(S["out_done"], t.val("out_done"))
            for h in range(2):
                r = slice(C * h, C * h + C)
                pool.dma_start(ST[r, :, C * h:C * h + C], I["wkv"][r]).then_inc(S["state_in"], 16)
            pool.wait_ge(S["c_in"], t.up("c_in", 2))
            for h in range(2):
                r = slice(C * h, C * h + C)
                store(O["wkv"][r, 1], ST[r, :, C * h:C * h + C])

            for i in range(NPAIR):
                if i == 2:
                    pool.wait_ge(S["out_done"], t.val("out_done"))
                    pool.sem_inc(S["state_out"], 1)
                if i >= 2:
                    pool.wait_ge(S["gn_ready"], i - 1)
                sm_, vv, gate = (B[:, 3 * (i % 2) + j, :] for j in range(3))
                done = S[f"gn_in{i % 2}"]
                pool.dma_start(sm_, d_x["sum"][i]).then_inc(done, 16)
                pool.dma_start(vv[:, P0:P0 + SEQ], d_v[i, :, 0:SEQ]).then_inc(done, 16)
                pool.dma_start(vv[:, S0:T], d_v[i, :, SEQ:SEQ + C]).then_inc(done, 16)
                pool.dma_start(gate, d_x["g"][i]).then_inc(done, 16)
            t.skip(2 * NPAIR)
            lend_h(1)
            finish_y()


def shape_constants():
    i = np.arange(P)
    eye = np.eye(P, dtype=np.float32)
    pair = (i[:, None] // C == i[None, :] // C).astype(np.float32)
    causal = np.where(i[None, :] > i[:, None], np.float32(NEG), np.float32(0))
    c = np.arange(C)
    causal2 = np.where(c[None, :] > (i % C)[:, None], np.float32(NEG), np.float32(0))
    strict = (c[:, None] < c[None, :]).astype(np.float32)
    incl = (c[:, None] <= c[None, :]).astype(np.float32)
    gram_even = np.block([[incl, strict], [incl, strict]])
    gram_odd = np.block([[strict, incl], [strict, incl]])

    def level(n):
        same = (i[:, None] % C) // (2 * n) == i[None, :] // (2 * n)
        return (same & (i[:, None] % (2 * n) < n) & (i[None, :] % (2 * n) >= n))[:, :C]

    cst = np.concatenate([eye, np.ones((P, P), np.float32), pair, causal, causal2, gram_even, gram_odd,
                          np.vstack([eye[:C, :C]] * 2)], 1)
    lvl = np.stack([level(n) for n in LEVELS], 1).astype(np.float32).reshape(P, -1)
    return np.ascontiguousarray(cst), np.ascontiguousarray(lvl)


def kernel(**inputs):
    import concourse.bacc as bacc
    from concourse.bass_utils import run_bass_kernel_spmd

    X = {n: np.asarray(a) for n, a in inputs.items()}

    def feature_major(prompt, sample):
        n = prompt.shape[1] // P
        out = np.zeros((P, n, T), np.float32)
        out[:, :, P0:P0 + SEQ] = prompt.T.reshape(n, P, SEQ).transpose(1, 0, 2)
        out[:, :, S0:] = sample.T.reshape(n, P, DEC).transpose(1, 0, 2)
        return out

    def tiles(w, cols=P):
        kk, m = w.shape
        return w.reshape(kk // P, P, m // cols, cols).transpose(2, 1, 0, 3).reshape(m // cols, P, -1)

    def columns(v):
        return v.reshape(-1, P).T

    def laced(*ws):
        return np.stack(ws, 1).reshape(-1, *ws[0].shape[1:])

    cst, lvl = shape_constants()
    w_in = X["e_w_in"][0]
    ax, ab, ac = (w_in[:, DA * j:DA * j + DA] for j in range(3))
    rows = {"mu%d" % n: X["r_mu"][0, n] for n in range(6)}
    for n in range(2):
        for short, name in (("pre", "mix_norm_pre"), ("post", "mix_norm_post"), ("fpre", "ffn_norm_pre"),
                            ("fpost", "ffn_norm_post"), ("ple", "ple_norm")):
            rows[f"{short}{n}"] = X[name][n]
    for short, name in (("w0", "r_w0"), ("a0", "r_a0"), ("kk", "r_k_k"), ("ka", "r_k_a"), ("lnw", "r_ln_w"),
                        ("lnb", "r_ln_b")):
        rows[short] = X[name][0]
    rows["rk"] = X["r_r_k"][0].reshape(-1)
    rows["shift"] = X["state_shift"][0, 0]
    down = [X["f_w_down"][l].reshape(2, HALF, P, KT, P).transpose(3, 0, 2, 1, 4).reshape(2 * KT, P, SLOT)
            for l in range(2)]
    arrays = {
        "cst": cst, "lvl": lvl, "vecs": np.stack([columns(rows[n]) for n in VEC], 1),
        "convw": np.stack([columns(X["e_conv_w"][0, j]) for j in range(3)], 1),
        "convs": np.stack([columns(X["state_conv"][0, 0, j]) for j in range(2)], 2),
        "bf": X["e_b_f"][0].reshape(HF, 1),
        "x": feature_major(X["x_prompt"][0], X["x_sample"][0]),
        "p": np.stack([feature_major(X["p_prompt"][l, 0], X["p_sample"][l, 0]) for l in range(2)]),
        "wv": tiles(w_in[:, 3 * DA + 1024:3 * DA + 1536], 512)[0],
        "wqk": tiles(w_in[:, 3 * DA:3 * DA + 1024]),
        "wf": tiles(w_in[:, 3 * DA + 1536:], HF)[0],
        "wconv": laced(tiles(ax), tiles(ac), tiles(ab)),
        "wout": tiles(X["e_w_out"][0]),
        "wgu": np.stack([laced(tiles(X["f_w_gate"][l]), tiles(X["f_w_up"][l])) for l in range(2)]),
        "wdown": np.stack(down),
        "wpg": np.stack([tiles(X["ple_gate"][l]) for l in range(2)]),
        "wpp": np.stack([tiles(X["ple_proj"][l]) for l in range(2)]),
        "clogf": X["cache_logf"][0, 0].T,
        "ck": X["cache_k"][0, 0].reshape(PAST, NA, P).transpose(2, 1, 0),
        "cv": X["cache_v"][0, 0].reshape(PAST // P, P, 512).transpose(1, 0, 2),
        "lw1": tiles(X["r_w1"][0], C)[0], "lw2": X["r_w2"][0], "la1": tiles(X["r_a1"][0], C)[0], "la2": X["r_a2"][0],
        "lg1": tiles(X["r_g1"][0])[0], "lg2": X["r_g2"][0],
        "wrkv": np.concatenate([tiles(X[n][0]) for n in ("r_w_r", "r_w_k", "r_w_v")]),
        "wo": tiles(X["r_w_o"][0]),
        "wkv": X["state_wkv"][0, 0].reshape(NPAIR, 2, C, C).transpose(1, 3, 0, 2).reshape(P, NPAIR, C),
    }
    shapes = {"y": (P, KT, T), "k": (P, NA, T), "v_p": (P, 8, 512), "v_s": (DEC, 512), "logf": (HF, T),
              "conv": (P, NA, 4), "shift": (P, 2, KT), "wkv": (P, 2, NPAIR, C)}

    nc = bacc.Bacc("TRN2", target_bir_lowering=False, num_devices=1)
    feed, ins = {}, {}
    for n, a in arrays.items():
        a = np.ascontiguousarray(a)
        feed["in_" + n] = a
        ins[n] = nc.dram_tensor("in_" + n, a.shape, mybir.dt.from_np(a.dtype), kind="ExternalInput").ap()
    outs = {n: nc.dram_tensor("out_" + n, s, F32, kind="ExternalOutput").ap() for n, s in shapes.items()}
    build_trunk(nc, ins, outs)
    res = run_bass_kernel_spmd(nc, [feed], core_ids=[0]).results[0]
    got = {n: res["out_" + n] for n in shapes}

    def tokens(a):
        flat = a.transpose(1, 0, 2).reshape(-1, T).T
        return flat[P0:P0 + SEQ], flat[S0:]

    y_p, y_s = tokens(got["y"])
    k_p, k_s = tokens(got["k"])
    v_p = got["v_p"].transpose(1, 0, 2).reshape(SEQ, 512)
    conv = got["conv"].transpose(1, 0, 2).reshape(DA, 4).T
    shift = got["shift"].transpose(1, 2, 0).reshape(2, D)
    wkv = got["wkv"].reshape(2, C, 2, NPAIR, C).transpose(2, 3, 0, 4, 1).reshape(2, HR, C, C)
    lf = got["logf"].T
    heads = lambda a, n: np.ascontiguousarray(a).reshape(1, 1, n, HF, C)
    groups = []
    for g, (n, y, kk, vv, c0) in enumerate(((SEQ, y_p, k_p, v_p, P0), (DEC, y_s, k_s, got["v_s"], S0))):
        groups.append((np.ascontiguousarray(y)[None], heads(kk, n), heads(vv, n),
                       np.ascontiguousarray(lf[c0:c0 + n]).reshape(1, 1, n, HF),
                       np.ascontiguousarray(conv[2 * g:2 * g + 2]).reshape(1, 1, 2, DA),
                       np.ascontiguousarray(shift[g]).reshape(1, 1, D),
                       np.ascontiguousarray(wkv[g]).reshape(1, 1, HR, C, C)))
    (yp, *prompt), (ys, *sample) = groups
    return (yp, ys, *prompt, *sample)
```
